# Optimizing a Trainium2 kernel written in Bass

```python
import math
import jax, jax.numpy as jnp
from jax import lax
import numpy as np
import jax
import jax.numpy as jnp

D_MODEL = 1024
BATCH = 1
SEQ = 256
DEPTH = 2

N_MIXERS = 3
BLOCK = 128
NORM_EPS = 1e-6

SB_HEADS = 16
SB_HEAD_DIM = 64
SB_WIDTH = SB_HEADS * SB_HEAD_DIM

MLA_HEADS = 8
MLA_NOPE_DIM = 128
MLA_ROPE_DIM = 64
MLA_QK_DIM = MLA_NOPE_DIM + MLA_ROPE_DIM
MLA_V_DIM = 128
MLA_Q_RANK = 256
MLA_KV_RANK = 128
MLA_WIDTH = MLA_HEADS * MLA_V_DIM
ROPE_THETA = 10000.0

SWA_HEADS = 16
SWA_KV_HEADS = 4
SWA_GROUP = SWA_HEADS // SWA_KV_HEADS
SWA_HEAD_DIM = 64
SWA_WINDOW = 128
SWA_WIDTH = SWA_HEADS * SWA_HEAD_DIM


def rms_norm(x, g):
    xf = x.astype(jnp.float32)
    y = xf * lax.rsqrt(jnp.mean(xf * xf, axis=-1, keepdims=True) + NORM_EPS)
    return (y * g.astype(jnp.float32)).astype(x.dtype)

def rope(x, pos):
    half = x.shape[-1] // 2
    inv_freq = ROPE_THETA ** (-jnp.arange(half, dtype=jnp.float32) / half)
    ang = pos.astype(jnp.float32)[:, None] * inv_freq[None, :]
    cos = jnp.cos(ang)[None, :, None, :]
    sin = jnp.sin(ang)[None, :, None, :]
    xf = x.astype(jnp.float32)
    x1, x2 = xf[..., :half], xf[..., half:]
    out = jnp.concatenate([x1 * cos - x2 * sin, x2 * cos + x1 * sin], axis=-1)
    return out.astype(x.dtype)

def alibi_slopes(n_heads):
    return 2.0 ** (-8.0 * jnp.arange(1, n_heads + 1, dtype=jnp.float32) / n_heads)

def stick_breaking_attention(q, k, v):
    B, S, H, d = q.shape
    scale = 1.0 / math.sqrt(d)
    outs = []
    for i in range(S // BLOCK):
        t0 = i * BLOCK
        kl = t0 + BLOCK
        z = jnp.einsum('bthd,bshd->bhts', q[:, t0:kl], k[:, :kl]).astype(jnp.float32) * scale
        t_idx = t0 + jnp.arange(BLOCK)[:, None]
        s_idx = jnp.arange(kl)[None, :]
        mask = s_idx < t_idx
        log_fail = jnp.where(mask, jax.nn.log_sigmoid(-z), 0.0)
        later = lax.cumsum(log_fail, axis=3, reverse=True) - log_fail
        a = jnp.where(mask, jnp.exp(jax.nn.log_sigmoid(z) + later), 0.0)
        outs.append(jnp.einsum('bhts,bshd->bthd', a.astype(v.dtype), v[:, :kl]))
    return jnp.concatenate(outs, axis=1)

def causal_softmax_attention(q, k, v, scale):
    B, S, H, _ = q.shape
    outs = []
    for i in range(S // BLOCK):
        t0 = i * BLOCK
        kl = t0 + BLOCK
        s = jnp.einsum('bthd,bshd->bhts', q[:, t0:kl], k[:, :kl]).astype(jnp.float32) * scale
        mask = jnp.arange(kl)[None, :] <= (t0 + jnp.arange(BLOCK)[:, None])
        p = jax.nn.softmax(jnp.where(mask, s, -jnp.inf), axis=-1)
        outs.append(jnp.einsum('bhts,bshd->bthd', p.astype(v.dtype), v[:, :kl]))
    return jnp.concatenate(outs, axis=1)

def sliding_window_sink_attention(q, k, v, sinks):
    B, S, H, d = q.shape
    nb = S // BLOCK
    qb = q.reshape(B, nb, BLOCK, SWA_KV_HEADS, SWA_GROUP, d)

    def band(t):
        prev = jnp.pad(t, ((0, 0), (BLOCK, 0), (0, 0), (0, 0)))[:, :S]
        return jnp.concatenate([prev.reshape(B, nb, BLOCK, SWA_KV_HEADS, d),
                                t.reshape(B, nb, BLOCK, SWA_KV_HEADS, d)], axis=2)

    kb, vb = band(k), band(v)
    s = jnp.einsum('bnqkgd,bnskd->bnkgqs', qb, kb).astype(jnp.float32) / math.sqrt(d)
    rel = jnp.arange(BLOCK)[:, None] + BLOCK - jnp.arange(2 * BLOCK)[None, :]
    abs_s = jnp.arange(nb)[:, None] * BLOCK - BLOCK + jnp.arange(2 * BLOCK)[None, :]
    valid = ((rel >= 0) & (rel < SWA_WINDOW))[None, :, :] & (abs_s >= 0)[:, None, :]
    slopes = alibi_slopes(SWA_HEADS).reshape(SWA_KV_HEADS, SWA_GROUP)
    s = s - slopes[:, :, None, None] * rel.astype(jnp.float32)
    s = jnp.where(valid[None, :, None, None, :, :], s, -jnp.inf)
    sink = sinks.astype(jnp.float32).reshape(SWA_KV_HEADS, SWA_GROUP)[None, None, :, :, None, None]
    m = jnp.maximum(jnp.max(s, axis=-1, keepdims=True), sink)
    e = jnp.exp(s - m)
    p = e / (jnp.sum(e, axis=-1, keepdims=True) + jnp.exp(sink - m))
    o = jnp.einsum('bnkgqs,bnskd->bnqkgd', p.astype(v.dtype), vb)
    return o.reshape(B, S, H, d)

def stick_breaking_layer(x, norm_g, w_in, w_out):
    B, S, _ = x.shape
    proj = rms_norm(x, norm_g) @ w_in
    q, k, v, gate = jnp.split(proj, 4, axis=-1)
    q = q.reshape(B, S, SB_HEADS, SB_HEAD_DIM)
    k = k.reshape(B, S, SB_HEADS, SB_HEAD_DIM)
    v = v.reshape(B, S, SB_HEADS, SB_HEAD_DIM)
    o = stick_breaking_attention(q, k, v).reshape(B, S, SB_WIDTH)
    return x + (o * jax.nn.silu(gate)) @ w_out

def mla_layer(x, norm_g, w_in, q_a_norm, w_uq, kv_a_norm, w_ukv, q_head_norm, k_head_norm, w_out):
    B, S, _ = x.shape
    proj = rms_norm(x, norm_g) @ w_in
    c1 = MLA_Q_RANK
    c2 = c1 + MLA_KV_RANK
    c3 = c2 + MLA_ROPE_DIM
    q_lat, kv_lat, k_pe, gate = proj[..., :c1], proj[..., c1:c2], proj[..., c2:c3], proj[..., c3:]
    q = (rms_norm(q_lat, q_a_norm) @ w_uq).reshape(B, S, MLA_HEADS, MLA_QK_DIM)
    kv = (rms_norm(kv_lat, kv_a_norm) @ w_ukv).reshape(B, S, MLA_HEADS, MLA_NOPE_DIM + MLA_V_DIM)
    k_nope, v = kv[..., :MLA_NOPE_DIM], kv[..., MLA_NOPE_DIM:]
    k_pe = jnp.broadcast_to(k_pe[:, :, None, :], (B, S, MLA_HEADS, MLA_ROPE_DIM))
    k = jnp.concatenate([k_nope, k_pe], axis=-1)
    q = rms_norm(q, q_head_norm)
    k = rms_norm(k, k_head_norm)
    pos = jnp.arange(S)
    q = jnp.concatenate([q[..., :MLA_NOPE_DIM], rope(q[..., MLA_NOPE_DIM:], pos)], axis=-1)
    k = jnp.concatenate([k[..., :MLA_NOPE_DIM], rope(k[..., MLA_NOPE_DIM:], pos)], axis=-1)
    o = causal_softmax_attention(q, k, v, 1.0 / math.sqrt(MLA_QK_DIM)).reshape(B, S, MLA_WIDTH)
    return x + (o * jax.nn.silu(gate)) @ w_out

def swa_layer(x, norm_g, w_in, q_head_norm, k_head_norm, sinks, w_out):
    B, S, _ = x.shape
    proj = rms_norm(x, norm_g) @ w_in
    kv_w = SWA_KV_HEADS * SWA_HEAD_DIM
    c1 = SWA_WIDTH
    c2 = c1 + kv_w
    c3 = c2 + kv_w
    q = proj[..., :c1].reshape(B, S, SWA_HEADS, SWA_HEAD_DIM)
    k = proj[..., c1:c2].reshape(B, S, SWA_KV_HEADS, SWA_HEAD_DIM)
    v = proj[..., c2:c3].reshape(B, S, SWA_KV_HEADS, SWA_HEAD_DIM)
    gate = proj[..., c3:]
    q = rms_norm(q, q_head_norm)
    k = rms_norm(k, k_head_norm)
    o = sliding_window_sink_attention(q, k, v, sinks).reshape(B, S, SWA_WIDTH)
    return x + (o * jax.nn.silu(gate)) @ w_out

def _dense(key, fan_in, fan_out):
    return jax.random.normal(key, (fan_in, fan_out), jnp.float32) * fan_in ** -0.5

def _gain(key, n):
    return 1.0 + 0.02 * jax.random.normal(key, (n,), jnp.float32)

def first_inputs(seed: int = 0) -> dict:
    key = jax.random.key(seed)
    ks = jax.random.split(key, 24)
    sb_in = 4 * SB_WIDTH
    mla_in = MLA_Q_RANK + MLA_KV_RANK + MLA_ROPE_DIM + MLA_WIDTH
    swa_in = SWA_WIDTH + 2 * SWA_KV_HEADS * SWA_HEAD_DIM + SWA_WIDTH
    return {
        'x': jax.random.normal(ks[0], (BATCH, SEQ, D_MODEL), jnp.float32),
        'l0_norm': _gain(ks[1], D_MODEL),
        'l0_w_in': _dense(ks[2], D_MODEL, sb_in),
        'l0_w_out': _dense(ks[3], SB_WIDTH, D_MODEL),
        'l1_norm': _gain(ks[4], D_MODEL),
        'l1_w_in': _dense(ks[5], D_MODEL, mla_in),
        'l1_q_a_norm': _gain(ks[6], MLA_Q_RANK),
        'l1_w_uq': _dense(ks[7], MLA_Q_RANK, MLA_HEADS * MLA_QK_DIM),
        'l1_kv_a_norm': _gain(ks[8], MLA_KV_RANK),
        'l1_w_ukv': _dense(ks[9], MLA_KV_RANK, MLA_HEADS * (MLA_NOPE_DIM + MLA_V_DIM)),
        'l1_q_head_norm': _gain(ks[10], MLA_QK_DIM),
        'l1_k_head_norm': _gain(ks[11], MLA_QK_DIM),
        'l1_w_out': _dense(ks[12], MLA_WIDTH, D_MODEL),
        'l2_norm': _gain(ks[13], D_MODEL),
        'l2_w_in': _dense(ks[14], D_MODEL, swa_in),
        'l2_q_head_norm': _gain(ks[15], SWA_HEAD_DIM),
        'l2_k_head_norm': _gain(ks[16], SWA_HEAD_DIM),
        'l2_sinks': 0.5 * jax.random.normal(ks[17], (SWA_HEADS,), jnp.float32),
        'l2_w_out': _dense(ks[18], SWA_WIDTH, D_MODEL),
        'l3_norm': _gain(ks[19], D_MODEL),
        'l3_w_in': _dense(ks[20], D_MODEL, sb_in),
        'l3_w_out': _dense(ks[21], SB_WIDTH, D_MODEL),
    }

def first_block(x, l0_norm, l0_w_in, l0_w_out,
              l1_norm, l1_w_in, l1_q_a_norm, l1_w_uq, l1_kv_a_norm, l1_w_ukv,
              l1_q_head_norm, l1_k_head_norm, l1_w_out,
              l2_norm, l2_w_in, l2_q_head_norm, l2_k_head_norm, l2_sinks, l2_w_out,
              l3_norm, l3_w_in, l3_w_out):
    layer_params = [
        (l0_norm, l0_w_in, l0_w_out),
        (l1_norm, l1_w_in, l1_q_a_norm, l1_w_uq, l1_kv_a_norm, l1_w_ukv,
         l1_q_head_norm, l1_k_head_norm, l1_w_out),
        (l2_norm, l2_w_in, l2_q_head_norm, l2_k_head_norm, l2_sinks, l2_w_out),
        (l3_norm, l3_w_in, l3_w_out),
    ]
    mixers = (stick_breaking_layer, mla_layer, swa_layer)
    for i in range(DEPTH):
        x = mixers[i % N_MIXERS](x, *layer_params[i])
    return x


DEPTH_2 = 1

GRID_W = 64
CTX_LEN = 256
N_MOD = 6
EPS = 1e-6
NEG_INF = -1e30

D_MIX = D_MODEL
NA_HEAD_DIM = 64
D_NA = D_MIX // 2
NA_HEADS = D_NA // NA_HEAD_DIM
NA_WIN_H = 8
NA_WIN_W = 16
RPB_H = 2 * NA_WIN_H - 1
RPB_W = 2 * NA_WIN_W - 1
D_HY = D_MIX // 4
HY_ORDER = 2
HY_SHORT = 3
HY_EMB = 33
HY_FILT = 64
HY_FAST_DECAY = 0.3
HY_SLOW_DECAY = 1.5
HY_TARGET = 1e-2
D_CF = D_MIX - D_NA - D_HY
CF_KERNEL = 31
D_IN = 3 * D_NA + (HY_ORDER + 1) * D_HY + 2 * D_CF
N_EXPERTS = 16
EC_CAPACITY = 2
EXPERT_FF = 2 * D_MODEL


def rmsnorm(x, g):
    x32 = x.astype(jnp.float32)
    y = x32 * lax.rsqrt(jnp.mean(x32 * x32, axis=-1, keepdims=True) + EPS)
    return (y * g.astype(jnp.float32)).astype(x.dtype)

def modulate(h, shift, scale):
    return h * (1 + scale) + shift

def adaln(cvec, w_mod, b_mod):
    m = jax.nn.silu(cvec) @ w_mod + b_mod
    return jnp.split(m, N_MOD, axis=-1)

def heads(t):
    return t.reshape(t.shape[0], t.shape[1], NA_HEADS, NA_HEAD_DIM)

def depthwise_conv(x, w, b):
    k = w.shape[0]
    pad = (k - 1) // 2
    y = lax.conv_general_dilated(
        x, w.astype(x.dtype)[:, None, :], window_strides=(1,), padding=[(pad, k - 1 - pad)],
        dimension_numbers=('NWC', 'WIO', 'NWC'), feature_group_count=x.shape[-1])
    return y + b.astype(x.dtype)

def neighbourhood_attention(q, k, v, k_ctx, v_ctx, rpb):
    B, S, H, Dh = q.shape
    rows = S // GRID_W
    wh = min(NA_WIN_H, rows)
    nk = wh * GRID_W
    scale = Dh ** -0.5
    qg = q.reshape(B, rows, GRID_W, H, Dh)
    kg = k.reshape(B, rows, GRID_W, H, Dh)
    vg = v.reshape(B, rows, GRID_W, H, Dh)
    col = jnp.arange(GRID_W)
    c0 = jnp.clip(col - NA_WIN_W // 2, 0, GRID_W - NA_WIN_W)
    col_ok = (col[None, :] >= c0[:, None]) & (col[None, :] < c0[:, None] + NA_WIN_W)
    mask = jnp.broadcast_to(col_ok[:, None, :], (GRID_W, wh, GRID_W)).reshape(GRID_W, nk)
    dc = jnp.clip(col[None, :] - col[:, None], 1 - NA_WIN_W, NA_WIN_W - 1) + NA_WIN_W - 1
    rpb32 = rpb.astype(jnp.float32)

    def row_block(r):
        r0 = jnp.clip(r - wh // 2, 0, rows - wh)
        qb = lax.dynamic_index_in_dim(qg, r, axis=1, keepdims=False)
        kb = lax.dynamic_slice_in_dim(kg, r0, wh, axis=1).reshape(B, nk, H, Dh)
        vb = lax.dynamic_slice_in_dim(vg, r0, wh, axis=1).reshape(B, nk, H, Dh)
        dr = r0 + jnp.arange(wh) - r + NA_WIN_H - 1
        bias = rpb32[:, dr[None, :, None], dc[:, None, :]].reshape(H, GRID_W, nk)
        s_nb = jnp.einsum('bqhd,bkhd->bhqk', qb, kb).astype(jnp.float32) * scale + bias
        s_nb = jnp.where(mask, s_nb, NEG_INF)
        s_cx = jnp.einsum('bqhd,bkhd->bhqk', qb, k_ctx).astype(jnp.float32) * scale
        p = jax.nn.softmax(jnp.concatenate([s_nb, s_cx], axis=-1), axis=-1).astype(v.dtype)
        return (jnp.einsum('bhqk,bkhd->bqhd', p[..., :nk], vb)
                + jnp.einsum('bhqk,bkhd->bqhd', p[..., nk:], v_ctx))

    out = lax.map(row_block, jnp.arange(rows))
    return out.transpose(1, 0, 2, 3, 4).reshape(B, S, H * Dh)

def context_attention(q, k, v):
    s = jnp.einsum('bqhd,bkhd->bhqk', q, k).astype(jnp.float32) * (q.shape[-1] ** -0.5)
    p = jax.nn.softmax(s, axis=-1).astype(v.dtype)
    o = jnp.einsum('bhqk,bkhd->bqhd', p, v)
    return o.reshape(o.shape[0], o.shape[1], -1)

def hyena_filter_spectrum(L, w1, b1, freq, w2, b2, w3):
    f32 = jnp.float32
    pos = jnp.arange(L, dtype=f32)[:, None]
    t = pos / max(L - 1, 1)
    bands = (HY_EMB - 1) // 2
    fb = jnp.linspace(1e-4, bands - 1, bands, dtype=f32)[None, :]
    ang = fb * (2.0 * math.pi) * pos / L
    z = jnp.concatenate([t, jnp.cos(ang), -jnp.sin(ang)], axis=-1)
    fr = freq.astype(f32)
    h = jnp.sin(fr * (z @ w1.astype(f32) + b1.astype(f32)))
    h = jnp.sin(fr * (h @ w2.astype(f32) + b2.astype(f32)))
    h = (h @ w3.astype(f32)).reshape(L, 2, HY_ORDER, D_HY)
    min_decay = math.log(HY_TARGET) / HY_SLOW_DECAY
    max_decay = math.log(HY_TARGET) / HY_FAST_DECAY
    rate = jnp.abs(jnp.linspace(min_decay, max_decay, D_HY, dtype=f32))
    h = h * jnp.exp(-t * rate)[:, None, None, :]
    fwd, bwd = h[:, 0], h[:, 1]
    k_circ = jnp.concatenate([fwd, jnp.zeros_like(fwd[:1]), bwd[1:][::-1]], axis=0)
    return jnp.fft.rfft(k_circ, axis=0)

def hyena_mixer(u, short_w, short_b, bias_d, w1, b1, freq, w2, b2, w3):
    dt = u.dtype
    L = u.shape[1]
    u = depthwise_conv(u, short_w, short_b).astype(jnp.float32)
    x1, x2, v = jnp.split(u, 3, axis=-1)
    k_spec = hyena_filter_spectrum(L, w1, b1, freq, w2, b2, w3)
    d = bias_d.astype(jnp.float32)
    z = v
    for n, gate in enumerate((x1, x2)):
        z_f = jnp.fft.rfft(z, n=2 * L, axis=1)
        conv = jnp.fft.irfft(z_f * k_spec[None, :, n], n=2 * L, axis=1)[:, :L]
        z = gate * (conv + d[n] * z)
    return z.astype(dt)

def conformer_conv(u, dw_w, dw_b, ln_g, ln_b):
    a, g = jnp.split(u, 2, axis=-1)
    y = depthwise_conv(a * jax.nn.sigmoid(g), dw_w, dw_b).astype(jnp.float32)
    mu = jnp.mean(y, axis=-1, keepdims=True)
    var = jnp.mean(jnp.square(y - mu), axis=-1, keepdims=True)
    y = (y - mu) * lax.rsqrt(var + EPS) * ln_g.astype(jnp.float32) + ln_b.astype(jnp.float32)
    return jax.nn.silu(y).astype(u.dtype)

def expert_choice_ffn(h, w_router, w1, w3, w2):
    B, L, _ = h.shape
    cap = EC_CAPACITY * L // N_EXPERTS
    aff = jax.nn.softmax((h @ w_router).astype(jnp.float32), axis=-1)
    gate, idx = lax.top_k(jnp.swapaxes(aff, 1, 2), cap)
    b_idx = jnp.arange(B)[:, None, None]
    xe = h[b_idx, idx]
    a = jnp.einsum('becd,edf->becf', xe, w1)
    u = jnp.einsum('becd,edf->becf', xe, w3)
    y = jnp.einsum('becf,efd->becd', jax.nn.silu(a) * u, w2)
    y = y * gate[..., None].astype(y.dtype)
    return jnp.zeros_like(h).at[b_idx, idx].add(y)

def second_inputs(seed: int = 0) -> dict:
    key = jax.random.key(seed)
    ks = jax.random.split(key, 32)
    f32 = jnp.float32

    def nrm(k, shape, scale):
        return scale * jax.random.normal(k, shape, f32)

    L = DEPTH_2
    return {
        'x': nrm(ks[0], (BATCH, SEQ, D_MODEL), 1.0),
        'c': nrm(ks[1], (BATCH, D_MODEL), 1.0),
        'ctx': nrm(ks[2], (BATCH, CTX_LEN, D_MODEL), 1.0),
        'c_ctx': nrm(ks[3], (D_MODEL,), 1.0),
        'w_mod': nrm(ks[4], (L, D_MODEL, N_MOD * D_MODEL), 0.5 * D_MODEL ** -0.5),
        'b_mod': nrm(ks[5], (L, N_MOD * D_MODEL), 0.02),
        'norm1_g': 1.0 + nrm(ks[6], (L, D_MODEL), 0.02),
        'norm2_g': 1.0 + nrm(ks[7], (L, D_MODEL), 0.02),
        'w_in': nrm(ks[8], (L, D_MODEL, D_IN), D_MODEL ** -0.5),
        'na_rpb': nrm(ks[9], (L, NA_HEADS, RPB_H, RPB_W), 0.1),
        'hy_short_w': nrm(ks[10], (L, HY_SHORT, (HY_ORDER + 1) * D_HY), HY_SHORT ** -0.5),
        'hy_short_b': nrm(ks[11], (L, (HY_ORDER + 1) * D_HY), 0.02),
        'hy_filt_w1': nrm(ks[12], (L, HY_EMB, HY_FILT), HY_EMB ** -0.5),
        'hy_filt_b1': nrm(ks[13], (L, HY_FILT), 0.02),
        'hy_filt_freq': 1.0 + nrm(ks[14], (L, HY_FILT), 0.02),
        'hy_filt_w2': nrm(ks[15], (L, HY_FILT, HY_FILT), HY_FILT ** -0.5),
        'hy_filt_b2': nrm(ks[16], (L, HY_FILT), 0.02),
        'hy_filt_w3': nrm(ks[17], (L, HY_FILT, 2 * HY_ORDER * D_HY), 0.05 * HY_FILT ** -0.5),
        'hy_bias_d': nrm(ks[18], (L, HY_ORDER, D_HY), 0.5),
        'cf_dw_w': nrm(ks[19], (L, CF_KERNEL, D_CF), CF_KERNEL ** -0.5),
        'cf_dw_b': nrm(ks[20], (L, D_CF), 0.02),
        'cf_ln_g': 1.0 + nrm(ks[21], (L, D_CF), 0.02),
        'cf_ln_b': nrm(ks[22], (L, D_CF), 0.02),
        'w_out': nrm(ks[23], (L, D_MIX, D_MODEL), D_MIX ** -0.5),
        'router_w': nrm(ks[24], (L, D_MODEL, N_EXPERTS), D_MODEL ** -0.5),
        'expert_w1': nrm(ks[25], (L, N_EXPERTS, D_MODEL, EXPERT_FF), D_MODEL ** -0.5),
        'expert_w3': nrm(ks[26], (L, N_EXPERTS, D_MODEL, EXPERT_FF), D_MODEL ** -0.5),
        'expert_w2': nrm(ks[27], (L, N_EXPERTS, EXPERT_FF, D_MODEL), EXPERT_FF ** -0.5),
        'final_norm_g': 1.0 + nrm(ks[28], (D_MODEL,), 0.02),
    }

def second_block(x, c, ctx, c_ctx, w_mod, b_mod, norm1_g, norm2_g, w_in, na_rpb,
              hy_short_w, hy_short_b, hy_filt_w1, hy_filt_b1, hy_filt_freq, hy_filt_w2,
              hy_filt_b2, hy_filt_w3, hy_bias_d, cf_dw_w, cf_dw_b, cf_ln_g, cf_ln_b,
              w_out, router_w, expert_w1, expert_w3, expert_w2, final_norm_g):
    splits = [D_NA, 2 * D_NA, 3 * D_NA, 3 * D_NA + (HY_ORDER + 1) * D_HY]
    xc = ctx
    for l in range(DEPTH_2):
        last = l == DEPTH_2 - 1
        sh1, sc1, g1, sh2, sc2, g2 = [m[:, None, :] for m in adaln(c, w_mod[l], b_mod[l])]
        csh1, csc1, cg1, csh2, csc2, cg2 = adaln(c_ctx, w_mod[l], b_mod[l])

        def head_groups(attn, hy_in, cf_in):
            hy = hyena_mixer(hy_in, hy_short_w[l], hy_short_b[l], hy_bias_d[l], hy_filt_w1[l], hy_filt_b1[l],
                             hy_filt_freq[l], hy_filt_w2[l], hy_filt_b2[l], hy_filt_w3[l])
            cf = conformer_conv(cf_in, cf_dw_w[l], cf_dw_b[l], cf_ln_g[l], cf_ln_b[l])
            return jnp.concatenate([attn, hy, cf], axis=-1) @ w_out[l]

        h = modulate(rmsnorm(x, norm1_g[l]), sh1, sc1)
        q, k, v, hy_in, cf_in = jnp.split(h @ w_in[l], splits, axis=-1)
        hc = modulate(rmsnorm(xc, norm1_g[l]), csh1, csc1)
        if last:
            kc, vc = jnp.split(hc @ w_in[l][:, D_NA:3 * D_NA], 2, axis=-1)
        else:
            qc, kc, vc, hyc_in, cfc_in = jnp.split(hc @ w_in[l], splits, axis=-1)
        attn = neighbourhood_attention(heads(q), heads(k), heads(v), heads(kc), heads(vc), na_rpb[l])
        x = x + g1 * head_groups(attn, hy_in, cf_in)
        h2 = modulate(rmsnorm(x, norm2_g[l]), sh2, sc2)
        x = x + g2 * expert_choice_ffn(h2, router_w[l], expert_w1[l], expert_w3[l], expert_w2[l])

        if not last:
            attn_c = context_attention(heads(qc), heads(kc), heads(vc))
            xc = xc + cg1 * head_groups(attn_c, hyc_in, cfc_in)
            hc2 = modulate(rmsnorm(xc, norm2_g[l]), csh2, csc2)
            xc = xc + cg2 * expert_choice_ffn(hc2, router_w[l], expert_w1[l], expert_w3[l], expert_w2[l])
    return rmsnorm(x, final_norm_g)


def setup_inputs(seed=0):
    out = dict(first_inputs(seed))
    for name, value in second_inputs(seed + 1).items():
        if name != "x":
            out[name + "_2"] = value
    return out


def reference(
    x, l0_norm, l0_w_in, l0_w_out, l1_norm, l1_w_in, l1_q_a_norm, l1_w_uq, l1_kv_a_norm,
    l1_w_ukv, l1_q_head_norm, l1_k_head_norm, l1_w_out, l2_norm, l2_w_in, l2_q_head_norm,
    l2_k_head_norm, l2_sinks, l2_w_out, l3_norm, l3_w_in, l3_w_out, c_2, ctx_2, c_ctx_2,
    w_mod_2, b_mod_2, norm1_g_2, norm2_g_2, w_in_2, na_rpb_2, hy_short_w_2, hy_short_b_2,
    hy_filt_w1_2, hy_filt_b1_2, hy_filt_freq_2, hy_filt_w2_2, hy_filt_b2_2, hy_filt_w3_2,
    hy_bias_d_2, cf_dw_w_2, cf_dw_b_2, cf_ln_g_2, cf_ln_b_2, w_out_2, router_w_2, expert_w1_2,
    expert_w3_2, expert_w2_2, final_norm_g_2,
):
    x = first_block(
        x, l0_norm, l0_w_in, l0_w_out, l1_norm, l1_w_in, l1_q_a_norm, l1_w_uq, l1_kv_a_norm,
        l1_w_ukv, l1_q_head_norm, l1_k_head_norm, l1_w_out, l2_norm, l2_w_in, l2_q_head_norm,
        l2_k_head_norm, l2_sinks, l2_w_out, l3_norm, l3_w_in, l3_w_out,
    )
    return second_block(
        x, c_2, ctx_2, c_ctx_2, w_mod_2, b_mod_2, norm1_g_2, norm2_g_2, w_in_2, na_rpb_2,
        hy_short_w_2, hy_short_b_2, hy_filt_w1_2, hy_filt_b1_2, hy_filt_freq_2, hy_filt_w2_2,
        hy_filt_b2_2, hy_filt_w3_2, hy_bias_d_2, cf_dw_w_2, cf_dw_b_2, cf_ln_g_2, cf_ln_b_2,
        w_out_2, router_w_2, expert_w1_2, expert_w3_2, expert_w2_2, final_norm_g_2,
    )


_drawn_inputs = setup_inputs


def setup_inputs(seed=0):
    import zlib

    import numpy as np

    out = dict(_drawn_inputs(seed))
    spreads = {}
    factors = {'l0_norm': 4.179,
     'l1_norm': 8.0,
     'l1_q_a_norm': 8.0,
     'l1_kv_a_norm': 8.0,
     'l1_q_head_norm': 8.0,
     'l1_k_head_norm': 8.0,
     'ctx_2': 2.844,
     'b_mod_2': 4.706,
     'norm1_g_2': 8.0,
     'norm2_g_2': 28.059,
     'na_rpb_2': 64.0,
     'hy_short_b_2': 21.529,
     'hy_filt_b1_2': 8.0,
     'hy_filt_freq_2': 8.0,
     'hy_filt_b2_2': 8.0,
     'cf_dw_b_2': 64.0,
     'cf_ln_g_2': 200.0,
     'cf_ln_b_2': 200.0,
     'final_norm_g_2': 25.26,
     'cf_dw_w_2': 3.109}
    for name, (base, spread) in spreads.items():
        noise = np.random.default_rng([zlib.crc32(name.encode()), seed]).standard_normal(out[name].shape)
        drawn = base * np.exp(spread * noise) if base else spread * noise
        out[name] = jnp.asarray(drawn.astype(out[name].dtype))
    for name, factor in factors.items():
        out[name] = (out[name] * factor).astype(out[name].dtype)
    return out
```

```python
import math
from contextlib import ExitStack

import numpy as np
import concourse.bass as bass
from concourse import mybir

F32 = mybir.dt.float32
ALU = mybir.AluOpType
ACT = mybir.ActivationFunctionType
AX = mybir.AxisListType

T = 256
D = 1024
NEG = -1e30
NSLOT = 6
SLOT = 4096
TWO_PI = 2.0 * math.pi
MAGIC = 1.5 * 2.0 ** 23

COLS = {}


def _cols_layout():
    at = 0
    for name, n in [("l0_norm", 8), ("l1_norm", 8), ("q_a", 2), ("kv_a", 1), ("gq", 1), ("gk", 1),
                    ("b_mod", 48), ("norm1", 8), ("norm2", 8), ("final", 8), ("c", 16),
                    ("sw", 18), ("sb", 6), ("bd", 4), ("cw", 62), ("cb", 2), ("lng", 2), ("lnb", 2)]:
        COLS[name] = (at, n)
        at += n
    return at


NCOL = _cols_layout()

CONST = {}


def _const_layout():
    at = 0
    for name, n in [("ident", 128), ("ones", 128), ("ntri", 128), ("nones", 128), ("m01", 128),
                    ("cap", 384), ("caus", 128), ("iota", 32), ("cosd", 128), ("sind", 128),
                    ("fwd", 1024), ("nyq", 256), ("inv", 1024), ("half", 1), ("flip", 128)]:
        CONST[name] = (at, n)
        at += n
    return at


NCONST = _const_layout()


class Recorder:

    def matmul(self, *a, **k):
        return lambda e: e.matmul(*a, **k)

    def transpose(self, *a, **k):
        return lambda e: e.transpose(*a, **k)

    def activation(self, *a, **k):
        return lambda e: e.activation(*a, **k)

    def tensor_scalar(self, *a, **k):
        return lambda e: e.tensor_scalar(*a, **k)

    def tensor_tensor(self, *a, **k):
        return lambda e: e.tensor_tensor(*a, **k)

    def scalar_tensor_tensor(self, *a, **k):
        return lambda e: e.scalar_tensor_tensor(*a, **k)

    def tensor_copy(self, *a, **k):
        return lambda e: e.tensor_copy(*a, **k)

    def tensor_reduce(self, *a, **k):
        return lambda e: e.tensor_reduce(*a, **k)

    def reciprocal(self, *a, **k):
        return lambda e: e.reciprocal(*a, **k)

    def memset(self, *a, **k):
        return lambda e: e.memset(*a, **k)

    def dma_start(self, *a, **k):
        return lambda e: e.dma_start(*a, **k)

    def max(self, *a, **k):
        return lambda e: e.max(*a, **k)

    def match_replace(self, *a, **k):
        return lambda e: e.match_replace(*a, **k)

    def tensor_tensor_scan(self, *a, **k):
        return lambda e: e.tensor_tensor_scan(*a, **k)

    def bn_stats(self, *a, **k):
        return lambda e: e.bn_stats(*a, **k)

    def bn_aggr(self, *a, **k):
        return lambda e: e.bn_aggr(*a, **k)


REC = Recorder()


class Queue:

    def __init__(self, name, sem):
        self.name, self.sem, self.n, self.items, self.seen = name, sem, 0, [], {}

    def waits(self, after):
        need = {}
        for tok in after:
            if tok is None:
                continue
            s, v = tok
            if self.seen.get(id(s), 0) < v:
                need[id(s)] = (s, max(v, need.get(id(s), (s, 0))[1]))
        for k, (s, v) in need.items():
            self.seen[k] = v
            self.items.append(("w", s, v))

    def __call__(self, fn, *after):
        self.waits(after)
        self.n += 1
        self.items.append(("i", fn(REC), self.sem, 1))
        return (self.sem, self.n)

    def dma(self, fn, sem, *after):
        self.waits(after)
        self.items.append(("i", fn(REC), sem, 16))

    def more(self, fn):
        self.items.append(("m", fn(REC)))


class Buf:

    def __init__(self, ap):
        self.ap, self.free = ap, ()


def build_program(nc, ins, outs, level=99):
    with ExitStack() as ctx:
        _program(nc, ins, outs, ctx, level)


def _program(nc, I, O, ctx, level):
    def sb(name, n, p=128):
        return ctx.enter_context(nc.sbuf_tensor(name, [p, n], F32))

    def sem(name):
        return ctx.enter_context(nc.semaphore(name))

    pe = Queue("pe", sem("s_pe"))
    act = Queue("act", sem("s_act"))
    dve = Queue("dve", sem("s_dve"))
    pool = Queue("pool", sem("s_pool"))
    sp = Queue("sp", None)
    out_sems = []

    ring = [sb(f"ring{i}", SLOT) for i in range(NSLOT)]
    xT = sb("xT", 8 * T)
    hT = sb("hT", 8 * T)
    A = sb("A", 16 * T)
    V = sb("V", 8 * T)
    G = sb("G", 8 * T)
    U = sb("U", 8 * T)
    S = sb("S", 8 * T)
    CC = sb("CC", NCONST)
    PC = sb("PC", NCOL)
    SPEC = sb("SPEC", 10 * T)
    BB = sb("BB", 8 * T)
    R = sb("R", 11 * T)
    mod = sb("mod", 96)
    sm = sb("sm", 256)
    rowg = sb("rowg", 128)
    rw = sb("rw", 128)
    fp = sb("fp", 3, 64)

    banks = [Buf(ctx.enter_context(nc.psum_tensor(f"ps{i}", [128, 512], F32))) for i in range(8)]
    turn = [0]

    def bank():
        b = banks[turn[0] % 6]
        turn[0] += 1
        return b

    def c_(name, a=None, b=None):
        at, n = CONST[name]
        return CC[:, at + (a or 0):at + (n if b is None else b)]

    def p_(name, i=0, n=1):
        at, _ = COLS[name]
        return PC[:, at + i:at + i + n]

    def v3(t, c, w=T, at=0):
        return t[:, at:at + c * w].rearrange("p (c t) -> p c t", c=c)

    s_ld = {}

    def load(q, name, dst, src, *after):
        s = sem("s_ld_" + name)
        q.dma(lambda e: e.dma_start(dst, src), s, *after)
        s_ld[name] = (s, 16)
        return s_ld[name]

    k_x = load(act, "x", v3(xT, 8), I["xT"].rearrange("(c p) t -> p c t", p=128))
    k_pc = load(sp, "pc", PC[:, :], I["cols"])
    k_cc = load(sp, "cc", CC[:, :], I["consts"])

    slot_sem = [sem(f"s_ring{i}") for i in range(NSLOT)]
    slot_uses = [0] * NSLOT
    slot_free = [()] * NSLOT
    next_slot = [0]

    def piece(src, c, n):
        i = next_slot[0] % NSLOT
        next_slot[0] += 1
        dst = ring[i][:, 0:c * n].rearrange("p (c n) -> p c n", c=c)
        sp.dma(lambda e: e.dma_start(dst, src), slot_sem[i], *slot_free[i])
        slot_uses[i] += 1
        return dst, (slot_sem[i], 16 * slot_uses[i]), i

    def done_with(i, *toks):
        slot_free[i] = toks

    def wview(w, a, n):
        return w.rearrange("(c p) n -> p c n", p=128)[:, :, a:a + n]

    mm = lambda e, o, l, r, st, sp_=True, sk=False: e.matmul(o, l, r, start=st, stop=sp_, skip_group_check=sk)

    def rsq(ap, *k):
        k = act(lambda e: e.activation(ap, ap, ACT.Sqrt), *k)
        return dve(lambda e: e.reciprocal(ap, ap), k)

    def rms_T(src, nch, dim, k_src, scale_of, out, bias_of=None, eps=1e-6, scr=None, k_scr=()):
        scr = scr if scr is not None else v3(S, 8)
        b = bank()
        ks = []
        for c in range(nch):
            ks.append(act(lambda e, c=c: e.activation(scr[:, c, :], src(c), ACT.Square),
                          *(k_src if c == 0 else ()), *(k_scr if c == 0 else ())))
        for c in range(nch):
            k = pe(lambda e, c=c: mm(e, b.ap[:, 0:T], c_("ones"), scr[:, c, :], c == 0, c == nch - 1),
                   ks[c], *(b.free if c == 0 else ()), k_cc)
        k1 = dve(lambda e: e.tensor_scalar(sm_r, b.ap[:, 0:T], 1.0 / dim, eps, ALU.mult, ALU.add), k, *smr_free[0])
        b.free = (k1,)
        k2 = rsq(sm_r, k1)
        ko = []
        for c in range(nch):
            k3 = dve(lambda e, c=c: e.scalar_tensor_tensor(out(c), src(c), scale_of(c), sm_r, ALU.mult, ALU.mult),
                     k2, k_pc)
            if bias_of is not None:
                k3 = act(lambda e, c=c: e.activation(out(c), out(c), ACT.Identity, bias=bias_of(c)), k3)
            ko.append(k3)
        smr_free[0] = (k3,) if bias_of is None else (ko[-1], (dve.sem, dve.n))
        return tuple(ko), k

    sm_r = R[:, 10 * T:11 * T]
    smr_free = [()]

    def proj_T(W, kW, hsrc, kh, cols, nch, consume):
        for j0 in range(0, len(cols), 2):
            b = bank()
            js = cols[j0:j0 + 2]
            for n, j in enumerate(js):
                for c in range(nch):
                    first = n == 0 and c == 0
                    if c < nch - 1:
                        pe.waits([kW, kh[c]] + (list(b.free) if first else []))
                        pe.more(lambda e, n=n, j=j, c=c: mm(
                            e, b.ap[:, n * T:(n + 1) * T], W[:, c, j:j + 128], hsrc(c), c == 0, False))
                    else:
                        k = pe(lambda e, n=n, j=j, c=c: mm(
                            e, b.ap[:, n * T:(n + 1) * T], W[:, c, j:j + 128], hsrc(c), c == 0, True), kW, kh[c],
                            *(b.free if first else ()))
            b.free = consume(j0, b, k)
        return k

    def proj_tok(W, kW, hsrc, kh, t, a, n, nch, consume, order=None):
        b = bank()
        for c in range(nch):
            f = lambda e, c=c: mm(e, b.ap[:, 0:n], hsrc(c)[:, t * 128:(t + 1) * 128], W[:, c, a:a + n], c == 0, c == nch - 1)
            if c < nch - 1:
                pe.waits([kW, kh[c]] + (list(b.free) if c == 0 else []))
                pe.more(f)
            else:
                k = pe(f, kW, kh[c], *(b.free if c == 0 else ()))
        b.free = consume(b, k)
        return k

    fillers = []

    def fill(n=1):
        for _ in range(n):
            if fillers:
                fillers.pop(0)()

    def gate_T(W, kW, h_, kh, cols, nch, dst, ch0, k_free=()):
        ks = []

        def consume(j0, b, k):
            o = v3(dst, 8)[:, ch0 + j0:ch0 + j0 + 2, :]
            bb = b.ap[:, :].rearrange("p (c t) -> p c t", c=2)
            k1 = act(lambda e: e.activation(o, bb, ACT.Tanh, scale=0.5), k, *k_free)
            k2 = dve(lambda e: e.scalar_tensor_tensor(o, o, 1.0, bb, ALU.add, ALU.mult), k1)
            ks.append(k2)
            return (k2,)
        k = proj_T(W, kW, h_, kh, cols, nch, consume)
        return k, ks

    def out_proj(w, u, ku, scale_of, k_extra=(), hook=None):
        for half in range(2):
            W, kW, i = piece(wview(w, half * 512, 512), 8, 512)

            def consume(j0, b, k, half=half):
                kk = None
                for n in range(2):
                    c = half * 4 + j0 + n
                    xc = xT[:, c * T:(c + 1) * T]
                    if scale_of is None:
                        kk = dve(lambda e, n=n, xc=xc: e.tensor_tensor(xc, b.ap[:, n * T:(n + 1) * T], xc, ALU.add), k, *k_extra)
                    else:
                        kk = dve(lambda e, n=n, xc=xc, c=c: e.scalar_tensor_tensor(
                            xc, b.ap[:, n * T:(n + 1) * T], scale_of(c), xc, ALU.mult, ALU.add), k, *k_extra)
                    kx[c] = kk
                return (kk,)
            k = proj_T(W, kW, u, ku, [0, 128, 256, 384], 8, consume)
            done_with(i, k)
            if half == 0 and hook is not None:
                hook()

    def xc(c):
        return xT[:, c * T:(c + 1) * T]

    def hc(c):
        return hT[:, c * T:(c + 1) * T]

    kx = [k_x] * 8

    s_silu = v3(sm, 8, 2)
    cview = PC[:, COLS["c"][0]:COLS["c"][0] + 16].rearrange("p (c t) -> p c t", c=8)
    k_c = act(lambda e: e.activation(s_silu, cview, ACT.Tanh, scale=0.5), k_pc)
    k_c = dve(lambda e: e.scalar_tensor_tensor(s_silu, s_silu, 1.0, cview, ALU.add, ALU.mult), k_c)
    k_c = dve(lambda e: e.tensor_scalar(s_silu, s_silu, 0.5, None, ALU.mult), k_c)
    k_mod = {}

    def mod_piece(i):
        def run():
            W, kW, slot = piece(wview(I["w_mod_2"][0], i * 512, 512), 8, 512)
            b = bank()
            pe.waits([k_c, kW, *b.free])
            for j in range(4):
                for c in range(8):
                    f = lambda e, j=j, c=c: mm(e, b.ap[:, 2 * j:2 * j + 2], W[:, c, j * 128:(j + 1) * 128],
                                               s_silu[:, c, :], c == 0, c == 7)
                    if j == 3 and c == 7:
                        k = pe(f)
                    else:
                        pe.more(f)
            done_with(slot, k)
            bm = PC[:, COLS["b_mod"][0] + 4 * i:COLS["b_mod"][0] + 4 * i + 4].unsqueeze(2).broadcast_to([128, 4, 2])
            k2 = dve(lambda e: e.tensor_tensor(mod[:, 8 * i:8 * i + 8].rearrange("p (c t) -> p c t", t=2),
                                               b.ap[:, 0:8].rearrange("p (c t) -> p c t", t=2), bm, ALU.add), k, k_pc)
            b.free = (k2,)
            k_mod[i] = k2
        return run

    for i in range(12):
        fillers.append(mod_piece(i))

    def m_(group, c, ctx_=0):
        j = (group * 8 + c) * 2 + ctx_
        return mod[:, j:j + 1]

    def hyena_filters():
        w3 = U[0:64, 0:1024]
        w2 = U[0:64, 1024:1088]
        w1 = U[0:33, 1088:1152]
        zf = U[0:33, 1152:1408]
        kw3 = load(sp, "w3", w3, I["hy_filt_w3_2"][0])
        kw2 = load(sp, "w2", w2, I["hy_filt_w2_2"][0])
        kw1 = load(sp, "w1", w1, I["hy_filt_w1_2"][0])
        kz = load(sp, "zf", zf, I["zfeat"])
        kd = load(sp, "dec", BB[:, 0:1024], I["decay"])
        kfp = load(sp, "fp", fp[:, :], I["filtp"])
        u = BB[0:64, 1024:1280]
        kk = BB[0:64, 1280:1536]
        h = BB[0:64, 1536:1792]

        def sine(b, k, bias):
            k = dve(lambda e: e.tensor_scalar(u, b.ap[0:64, 0:T], fp[:, bias:bias + 1], fp[:, 1:2], ALU.add, ALU.mult), k, kfp)
            b.free = (k,)
            k = dve(lambda e: e.tensor_scalar(kk, u, 1.0 / TWO_PI, MAGIC, ALU.mult, ALU.add), k)
            k = dve(lambda e: e.tensor_scalar(kk, kk, MAGIC, None, ALU.subtract), k)
            c1 = 6.28125
            c2 = float(np.float32(np.round((TWO_PI - c1) * 2 ** 20) / 2 ** 20))
            c3 = TWO_PI - c1 - c2
            for cst in (c1, c2, c3):
                k = dve(lambda e, cst=cst: e.scalar_tensor_tensor(u, kk, -cst, u, ALU.mult, ALU.add), k)
            lim = 3.1415925
            k = dve(lambda e: e.tensor_scalar(u, u, lim, -lim, ALU.min, ALU.max), k)
            return act(lambda e: e.activation(h, u, ACT.Sin), k)
        b = bank()
        k = pe(lambda e: mm(e, b.ap[0:64, 0:T], w1, zf, True), kw1, kz, *b.free)
        yield
        k = sine(b, k, 0)
        yield
        b = bank()
        k = pe(lambda e: mm(e, b.ap[0:64, 0:T], w2, h, True), kw2, k, *b.free)
        yield
        k = sine(b, k, 2)
        yield
        summ = v3(S, 2, 512)
        diff = v3(S, 2, 512, at=1024)
        ks = []
        for t in range(2):
            bf, bb = bank(), bank()
            k1 = pe(lambda e: mm(e, bf.ap[:, :], h[:, t * 128:(t + 1) * 128], w3[:, 0:512], True), k, kw3, *bf.free)
            k2 = pe(lambda e: mm(e, bb.ap[:, :], h[:, t * 128:(t + 1) * 128], w3[:, 512:1024], True), *bb.free)
            dcf = BB[:, t * 512:t * 512 + 256].unsqueeze(1).broadcast_to([128, 2, 256])
            dcb = BB[:, t * 512 + 256:t * 512 + 512].unsqueeze(1).broadcast_to([128, 2, 256])
            o2 = lambda a: a.rearrange("p (o c) -> p o c", o=2)
            tmp = U[:, 1408:1920]
            k3 = dve(lambda e: e.tensor_tensor(o2(summ[:, t, :]), o2(bf.ap[:, :]), dcf, ALU.mult), k1, kd)
            k4 = dve(lambda e: e.tensor_tensor(o2(tmp), o2(bb.ap[:, :]), dcb, ALU.mult), k2, *(ks[-1:]))
            bf.free, bb.free = (k3,), (k4,)
            k5 = dve(lambda e: e.tensor_tensor(diff[:, t, :], summ[:, t, :], tmp, ALU.subtract), k3, k4)
            k6 = dve(lambda e: e.tensor_tensor(summ[:, t, :], summ[:, t, :], tmp, ALU.add), k5)
            ks.append(k6)
            yield
        fw = v3(CC, 2, 512, at=CONST["fwd"][0])
        ny = v3(CC, 2, 128, at=CONST["nyq"][0])
        KA, KB, KC = v3(SPEC, 2, 512), v3(SPEC, 2, 512, at=1024), v3(SPEC, 1, 512, at=2048)
        last = []
        for dst, rhs, lhs in [(KA[:, 0, :], summ, lambda t: fw[:, t, 0:128]), (KA[:, 1, :], summ, lambda t: fw[:, t, 128:256]),
                              (KB[:, 0, :], diff, lambda t: kb0(t)), (KB[:, 1, :], diff, lambda t: fw[:, t, 384:512]),
                              (KC[:, 0, :], summ, lambda t: ny[:, t, :])]:
            b = bank()
            for t in range(2):
                k = pe(lambda e, t=t, rhs=rhs, lhs=lhs, b=b: mm(e, b.ap[:, :], lhs(t), rhs[:, t, :], t == 0, t == 1), ks[t], k_cc,
                       *(b.free if t == 0 else ()))
            k = act(lambda e, dst=dst, b=b: e.activation(dst, b.ap[:, :], ACT.Copy), k)
            b.free = (k,)
            last.append(k)
            yield
        kz0 = pool(lambda e: e.memset(KB[0:1, 0, :], 0.0), last[2])
        k_spec.extend([kz0, *last])

    def kb0(t):
        return v3(CC, 2, 512, at=CONST["fwd"][0])[:, t, 256:384]

    k_spec = []
    kh, _ = rms_T(xc, 8, D, kx, lambda c: p_("l0_norm", c), hc, scr=v3(A, 8))
    hy_steps = hyena_filters()
    next(hy_steps)

    w = I["l0_w_in"]
    kq = {}
    qk = v3(A, 16)
    for grp, (a, sc) in enumerate(((0, 0.125), (1024, 1.0))):
        for half in range(2):
            W, kW, i = piece(wview(w, a + half * 512, 512), 8, 512)

            def consume(j0, b, k, grp=grp, half=half, sc=sc):
                ch = grp * 8 + half * 4 + j0
                o = A[:, ch * T:(ch + 2) * T]
                k2 = act(lambda e: e.activation(o, b.ap[:, :], ACT.Copy, scale=sc), k)
                kq[ch] = kq[ch + 1] = k2
                return (k2,)
            k = proj_T(W, kW, hc, kh, [0, 128, 256, 384], 8, consume)
            done_with(i, k)
            next(hy_steps, None)
            next(hy_steps, None)
    kv = {}
    for half in range(2):
        W, kW, i = piece(wview(w, 2048 + half * 512, 512), 8, 512)
        for t in range(2):
            def consume(b, k, t=t, half=half):
                k2 = dve(lambda e: e.tensor_copy(V[:, t * 1024 + half * 512:t * 1024 + half * 512 + 512], b.ap[:, :]), k)
                kv[(t, half)] = k2
                return (k2,)
            k = proj_tok(W, kW, hc, kh, t, 0, 512, 8, consume)
        done_with(i, k)
    kg = []
    for half in range(2):
        W, kW, i = piece(wview(w, 3072 + half * 512, 512), 8, 512)
        k, ks = gate_T(W, kW, hc, kh, [0, 128, 256, 384], 8, G, half * 4)
        kg += ks
        done_with(i, k)

    for _ in hy_steps:
        pass
    act.items.append(("t", "natural_log_exp_and_others"))

    def sb_attention():
        e1 = [Buf(R[:, i * 384:(i + 1) * 384]) for i in range(3)]
        Lb = [Buf(R[:, 1152 + i * 384:1152 + (i + 1) * 384]) for i in range(3)]
        abuf = [Buf(S[:, i * 384:(i + 1) * 384]) for i in range(3)]
        st = {}

        def stage_z(h):
            b = bank()
            p0 = 64 * (h % 2)
            q = A[p0:p0 + 64, (h // 2) * T:(h // 2 + 1) * T]
            k_ = A[p0:p0 + 64, (8 + h // 2) * T:(9 + h // 2) * T]
            pe.waits([kq[h // 2], kq[8 + h // 2], *b.free])
            pe.more(lambda e: mm(e, b.ap[:, 0:256], k_[:, 0:128], q, True, True, True))
            k = pe(lambda e: mm(e, b.ap[:, 256:384], k_[:, 128:256], q[:, 128:256], False, True, True))
            e_, L = e1[h % 3], Lb[h % 3]
            k0 = dve(lambda e: e.tensor_scalar(L.ap, b.ap[:, 0:384], 0.0, None, ALU.max), k, *L.free)
            k1 = dve(lambda e: e.scalar_tensor_tensor(e_.ap, b.ap[:, 0:384], 0.0, L.ap, ALU.min, ALU.subtract), k0, *e_.free)
            k2 = act(lambda e: e.activation(e_.ap, e_.ap, ACT.Exp), k1)
            k3 = act(lambda e: e.activation(e_.ap, e_.ap, ACT.Ln, bias=1.0), k2)
            k4 = pool(lambda e: e.tensor_tensor(L.ap, L.ap, e_.ap, ALU.add), k3)
            e_.free = (k4,)
            k6 = None
            for a in (0, 256):
                k6 = pool(lambda e, a=a: e.tensor_tensor(L.ap[:, a:a + 128], L.ap[:, a:a + 128], c_("m01"), ALU.mult), k4, k_cc)
            st[h] = (b, L, k6, k4)

        def stage_c(h):
            b, L, k6, k4 = st[h]
            pe.waits([k6, k4])
            pe.more(lambda e: mm(e, b.ap[:, 0:256], c_("ntri"), L.ap[:, 0:256], False, True, True))
            pe.more(lambda e: mm(e, b.ap[:, 128:256], c_("nones"), L.ap[:, 256:384], False, True, True))
            k = pe(lambda e: mm(e, b.ap[:, 256:384], c_("ntri"), L.ap[:, 256:384], False, True, True))
            L.free = (k,)
            a = abuf[h % 3]
            a.free = a.free or tuple(k_spec)
            k1 = dve(lambda e: e.tensor_tensor(a.ap, b.ap[:, 0:384], c_("cap"), ALU.min), k, *a.free)
            b.free = (k1,)
            k2 = act(lambda e: e.activation(a.ap, a.ap, ACT.Exp), k1)
            st[h] = (a, k2)

        ku = []

        def stage_o(h):
            a, k2 = st.pop(h)
            b = banks[6 + (h // 2) % 2]
            p0 = 64 * (h % 2)
            o = b.ap[p0:p0 + 64, 0:256]
            pe.waits([k2, *b.free, kv[(0, h // 8)], kv[(1, h // 8)]])
            pe.more(lambda e: mm(e, o, V[:, h * 64:h * 64 + 64], a.ap[:, 0:256], True, True, True))
            k = pe(lambda e: mm(e, o[:, 128:256], V[:, 1024 + h * 64:1088 + h * 64], a.ap[:, 256:384], False, True, True))
            a.free = (k,)
            if h % 2:
                c = h // 2
                k3 = dve(lambda e: e.scalar_tensor_tensor(U[:, c * T:(c + 1) * T], b.ap[:, 0:256], 0.5,
                                                          G[:, c * T:(c + 1) * T], ALU.mult, ALU.mult), k, kg[c // 2], *k_spec)
                b.free = (k3,)
                ku.append(k3)
        for i in range(16 + 3):
            if i < 16:
                stage_z(i)
            if i % 3 == 2:
                fill()
            if 0 <= i - 1 < 16:
                stage_c(i - 1)
            if 0 <= i - 3 < 16:
                stage_o(i - 3)
        return ku

    ku = sb_attention()
    out_proj(I["l0_w_out"], lambda c: U[:, c * T:(c + 1) * T], ku, None)
    if level == 1:
        return finish(nc, locals())

    kh, _ = rms_T(xc, 8, D, kx, lambda c: p_("l1_norm", c), hc)
    k_rowg = load(sp, "rowg", rowg[:, :], I["rowg"].broadcast_to([128, 128]))
    w = I["l1_w_in"]
    W, kW, i = piece(wview(w, 0, 448), 8, 448)
    lat = [S[:, 0:448], S[:, 448:896]]
    klat = []
    for t in range(2):
        def consume(b, k, t=t):
            k2 = act(lambda e: e.activation(lat[t], b.ap[:, 0:448], ACT.Copy), k, kh[-1])
            klat.append(k2)
            return (k2,)
        k = proj_tok(W, kW, hc, kh, t, 0, 448, 8, consume)
    done_with(i, k)
    kg = []
    for half in range(2):
        W, kW, i = piece(wview(w, 448 + half * 512, 512), 8, 512)
        k, ks = gate_T(W, kW, hc, kh, [0, 128, 256, 384], 8, G, half * 4)
        kg += ks
        done_with(i, k)
    sq = S[:, 1024:1472]
    st_ = sm[:, 32:64]
    latT = v3(S, 3, T, at=1472 - 192)
    latT = v3(R, 3, T)
    klt = []
    k_prev = None
    stat_k = []
    for t in range(2):
        k = act(lambda e, t=t: e.activation(sq[:, 0:256], lat[t][:, 0:256], ACT.Square, accum_out=sm[:, 32 + 4 * t:33 + 4 * t]), klat[t])
        k = act(lambda e, t=t: e.activation(sq[:, 256:384], lat[t][:, 256:384], ACT.Square, accum_out=sm[:, 33 + 4 * t:34 + 4 * t]), k)
        k = act(lambda e, t=t: e.activation(sq[:, 384:448], lat[t][:, 384:448], ACT.Square, accum_out=sm[:, 34 + 4 * t:35 + 4 * t]), k)
        ka = dve(lambda e, t=t: e.tensor_scalar(sm[:, 40 + 4 * t:41 + 4 * t], sm[:, 32 + 4 * t:33 + 4 * t], 1.0 / 256, 1e-6, ALU.mult, ALU.add), k)
        kb = dve(lambda e, t=t: e.tensor_scalar(sm[:, 41 + 4 * t:42 + 4 * t], sm[:, 33 + 4 * t:34 + 4 * t], 1.0 / 128, 1e-6, ALU.mult, ALU.add), k)
        k2 = rsq(sm[:, 40 + 4 * t:42 + 4 * t], ka, kb)
        ka = dve(lambda e, t=t: e.tensor_scalar(lat[t][:, 0:256], lat[t][:, 0:256], sm[:, 40 + 4 * t:41 + 4 * t], None, ALU.mult), k2)
        kb = dve(lambda e, t=t: e.tensor_scalar(lat[t][:, 256:384], lat[t][:, 256:384], sm[:, 41 + 4 * t:42 + 4 * t], None, ALU.mult), k2)
        stat_k.append((ka, kb))
    bq, bk = bank(), bank()
    for t in range(2):
        for j in range(3):
            b, o = (bq, j * T) if j < 2 else (bk, 0)
            k = pe(lambda e, t=t, j=j, b=b, o=o: e.transpose(b.ap[:, o + t * 128:o + t * 128 + 128], lat[t][:, j * 128:(j + 1) * 128], c_("ident")),
                   *stat_k[t], *(b.free if t == 0 else ()))
    klq = []
    for j in range(3):
        b, o = (bq, j * T) if j < 2 else (bk, 0)
        g = p_("q_a", j) if j < 2 else p_("kv_a")
        klq.append(dve(lambda e, j=j, b=b, o=o, g=g: e.tensor_scalar(latT[:, j, :], b.ap[:, o:o + T], g, None, ALU.mult), k))
    bq.free = bk.free = (klq[-1],)
    fill()

    Wq, kWq, iq = piece(I["l1_w_uq"].rearrange("(c p) n -> p c n", p=128), 2, 1536)
    Wk, kWk, ik = piece(I["l1_w_ukv"].unsqueeze(1), 1, 2048)
    qnT, knT = v3(A, 8), v3(A, 8, T, at=8 * T)
    qrT = v3(hT, 4)
    krT = v3(hT, 4, T, at=4 * T)
    qt = [S[:, 0:1536], U[:, 0:1536]]
    kt = [SCK[0], SCK[1]] if False else None
    ssq = sm[:, 64:96]
    kss = {}
    pe_rope = R[:, 3 * T:3 * T + 128]
    t1 = R[:, 4 * T:4 * T + 64]
    cosd = lambda t: c_("cosd", 64 * t, 64 * t + 64)
    sind = lambda t: c_("sind", 64 * t, 64 * t + 64)
    kpe = []
    for t in range(2):
        x_ = lat[t][:, 384:448]
        o = pe_rope[:, 64 * t:64 * t + 64]
        k = dve(lambda e, x_=x_: e.tensor_tensor(x_, x_, rowg[:, 64:128], ALU.mult), klat[t], k_rowg, stat_k[t][0])
        ka = dve(lambda e, t=t, x_=x_, o=o: e.tensor_tensor(o, x_, cosd(t), ALU.mult), k)
        kb = dve(lambda e, t=t, x_=x_: e.tensor_tensor(t1[:, 0:32], x_[:, 32:64], sind(t)[:, 0:32], ALU.mult), k, *kpe[-1:])
        kc = dve(lambda e, t=t, x_=x_: e.tensor_tensor(t1[:, 32:64], x_[:, 0:32], sind(t)[:, 32:64], ALU.mult), k)
        kpe.append(dve(lambda e, o=o: e.tensor_tensor(o, o, t1, ALU.add), ka, kb, kc))

    qn = {}
    sqb = [Buf(R[:, 5 * T:5 * T + 512]), Buf(R[:, 7 * T:7 * T + 512])]
    nsq = [0]
    hq = lambda c: latT[:, c, :]
    k_qt = {}
    for t in range(2):
        for g in range(4):
            def consume(b, k, t=t, g=g):
                o = qt[t][:, g * 384:(g + 1) * 384]
                s = sqb[nsq[0] % 2]
                nsq[0] += 1
                k1 = act(lambda e: e.activation(o, b.ap[:, 0:384], ACT.Copy), k, kpe[0], kpe[1], klq[2])
                k2 = act(lambda e: e.activation(s.ap[:, 0:384], b.ap[:, 0:384], ACT.Square), k, *s.free)
                k3 = dve(lambda e: e.tensor_reduce(ssq[:, t * 8 + 2 * g:t * 8 + 2 * g + 2],
                                                   s.ap[:, 0:384].rearrange("p (h d) -> p h d", h=2), AX.X, ALU.add), k2)
                s.free = (k3,)
                k_qt[(t, g)] = (k1, k3)
                return (k1, k2)
            k = proj_tok(Wq, kWq, hq, klq, t, g * 384, 384, 2, consume)
    done_with(iq, k)
    kqr = []
    tq = R[:, 3 * T + 128:3 * T + 128]
    for t in range(2):
        qv = qt[t].rearrange("p (h d) -> p h d", h=8)[:, :, 128:192]
        tmp = R[:, 5 * T:5 * T + 512].rearrange("p (h d) -> p h d", h=8)
        tm2 = R[:, 7 * T:7 * T + 512].rearrange("p (h d) -> p h d", h=8)
        rg = rowg[:, 0:64].unsqueeze(1).broadcast_to([128, 8, 64])
        cb_ = cosd(t).unsqueeze(1).broadcast_to([128, 8, 64])
        sb_ = lambda a, b, t=t: sind(t)[:, a:b].unsqueeze(1).broadcast_to([128, 8, 32])
        dep = [x for g in range(4) for x in k_qt[(t, g)]] + [x for s in sqb for x in s.free]
        k = dve(lambda e, qv=qv, tmp=tmp, rg=rg: e.tensor_tensor(tmp, qv, rg, ALU.mult), *dep, *kqr[-1:])
        ka = dve(lambda e, tm2=tm2, tmp=tmp, sb_=sb_: e.tensor_tensor(tm2[:, :, 0:32], tmp[:, :, 32:64], sb_(0, 32), ALU.mult), k, *kqr[-1:])
        kb = dve(lambda e, tm2=tm2, tmp=tmp, sb_=sb_: e.tensor_tensor(tm2[:, :, 32:64], tmp[:, :, 0:32], sb_(32, 64), ALU.mult), k)
        kc = dve(lambda e, tmp=tmp, cb_=cb_: e.tensor_tensor(tmp, tmp, cb_, ALU.mult), ka, kb)
        kqr.append(dve(lambda e, qv=qv, tmp=tmp, tm2=tm2: e.tensor_tensor(qv, tmp, tm2, ALU.add), kc, ka, kb))
    for s in sqb:
        s.free = (kqr[-1],)
    scq = sm[:, 96:112]
    k = dve(lambda e: e.tensor_scalar(scq, ssq[:, 0:16], 1.0 / 192, 1e-6, ALU.mult, ALU.add), k_qt[(1, 3)][1], k_qt[(0, 3)][1])
    k = rsq(scq, k)
    k_scq = dve(lambda e: e.tensor_scalar(scq, scq, 192.0 ** -0.5, None, ALU.mult), k)
    fill()

    k_kh = kh
    k_qnT, k_qrT = {}, {}
    for hp in range(4):
        b = bank()
        for n in range(4):
            h, t = 2 * hp + n // 2, n % 2
            k = pe(lambda e, n=n, h=h, t=t, b=b: e.transpose(b.ap[:, n * 128:(n + 1) * 128], qt[t][:, h * 192:h * 192 + 128], c_("ident")),
                   k_qt[(t, h // 2)][0], *(b.free if n == 0 else ()))
        k = act(lambda e, hp=hp, b=b: e.activation(A[:, 2 * hp * T:(2 * hp + 2) * T], b.ap[:, :], ACT.Copy, scale=p_("gq")), k)
        b.free = (k,)
        k_qnT[hp] = k
    qr2 = R[:, 5 * T:5 * T + 512]
    for t in range(2):
        qv = qt[t].rearrange("p (h d) -> p h d", h=8)[:, :, 128:192]
        kcp = pool(lambda e, qv=qv: e.tensor_copy(qr2.rearrange("p (h d) -> p h d", h=8), qv), kqr[t], *( [k_qrT[(0, 1)]] if t else [kqr[1]]))
        b = bank()
        for n in range(4):
            k = pe(lambda e, n=n, b=b: e.transpose(b.ap[:, n * 128:(n + 1) * 128], qr2[:, n * 128:(n + 1) * 128], c_("ident")), kcp, *(b.free if n == 0 else ()))
        kk = dve(lambda e, b=b, t=t: e.tensor_copy(qrT[:, :, t * 128:(t + 1) * 128], b.ap[:, :].rearrange("p (c t) -> p c t", c=4)), k, (pe.sem, pe.n))
        b.free = (kk,)
        k_qrT[(t, 0)] = kk
        k_qrT[(0, 1)] = k
    k_r2 = k
    ktk = [S[:, 0:1024], U[:, 0:1024]]
    ssk = sm[:, 80:96]
    k_kt = {}
    kvv = {}
    trans_done = (pe.sem, pe.n)
    for t in range(2):
        for g in range(4):
            def consume(b, k, t=t, g=g):
                bb = b.ap[:, :].rearrange("p (h d) -> p h d", h=2)
                o = ktk[t][:, g * 256:(g + 1) * 256].rearrange("p (h d) -> p h d", h=2)
                vv = V[:, t * 1024 + g * 256:t * 1024 + (g + 1) * 256].rearrange("p (h d) -> p h d", h=2)
                s = sqb[nsq[0] % 2]
                nsq[0] += 1
                k1 = act(lambda e: e.activation(o, bb[:, :, 0:128], ACT.Copy), k, trans_done, *kqr)
                k2 = act(lambda e: e.activation(s.ap[:, 0:256].rearrange("p (h d) -> p h d", h=2), bb[:, :, 0:128], ACT.Square), k, *s.free, k_r2)
                k3 = dve(lambda e: e.tensor_reduce(ssk[:, t * 8 + 2 * g:t * 8 + 2 * g + 2],
                                                   s.ap[:, 0:256].rearrange("p (h d) -> p h d", h=2), AX.X, ALU.add), k2)
                k4 = dve(lambda e: e.tensor_copy(vv, bb[:, :, 128:256]), k)
                s.free = (k3,)
                k_kt[(t, g)] = (k1, k3)
                kvv[(t, g)] = k4
                return (k1, k2, k4)
            k = proj_tok(Wk, kWk, lambda c: latT[:, 2, :], [klq[2]], t, g * 512, 512, 1, consume)
    done_with(ik, k)
    rk = sm[:, 112:128]
    k_knT = {}
    krb = R[:, 5 * T:5 * T + 512]
    kk_prev = None
    knorm = []
    krd = {}
    for t in range(2):
        k = dve(lambda e, t=t: e.tensor_scalar(rk[:, 8 * t:8 * t + 8], ssk[:, 8 * t:8 * t + 8], sm[:, 34 + 4 * t:35 + 4 * t], 1.0 / 192, ALU.add, ALU.mult), k_kt[(t, 3)][1])
        k = dve(lambda e, t=t: e.tensor_scalar(rk[:, 8 * t:8 * t + 8], rk[:, 8 * t:8 * t + 8], 1e-6, None, ALU.add), k)
        k = rsq(rk[:, 8 * t:8 * t + 8], k)
        rb = rk[:, 8 * t:8 * t + 8].unsqueeze(2)
        kt3 = ktk[t].rearrange("p (h d) -> p h d", h=8)
        ka = dve(lambda e, kt3=kt3, rb=rb: e.tensor_tensor(kt3, kt3, rb.broadcast_to([128, 8, 128]), ALU.mult), k, *[k_kt[(t, g)][0] for g in range(4)])
        kr3 = krb.rearrange("p (h d) -> p h d", h=8)
        pr = pe_rope[:, 64 * t:64 * t + 64].unsqueeze(1).broadcast_to([128, 8, 64])
        kb = dve(lambda e, kr3=kr3, rb=rb, pr=pr: e.tensor_tensor(kr3, pr, rb.broadcast_to([128, 8, 64]), ALU.mult), k, k_r2, kpe[t],
                 *([krd[0]] if t else []), *[x for s in sqb for x in s.free])
        knorm.append(ka)
        b = bank()
        for n in range(4):
            k = pe(lambda e, n=n, b=b: e.transpose(b.ap[:, n * 128:(n + 1) * 128], krb[:, n * 128:(n + 1) * 128], c_("ident")), kb, *(b.free if n == 0 else ()))
        krd[t] = k
        kk = dve(lambda e, b=b, t=t: e.tensor_copy(krT[:, :, t * 128:(t + 1) * 128], b.ap[:, :].rearrange("p (c t) -> p c t", c=4)), k)
        b.free = (kk,)
        k_knT[("r", t)] = kk
    for hp in range(4):
        b = bank()
        for n in range(4):
            h, t = 2 * hp + n // 2, n % 2
            k = pe(lambda e, n=n, h=h, t=t, b=b: e.transpose(b.ap[:, n * 128:(n + 1) * 128], ktk[t][:, h * 128:h * 128 + 128], c_("ident")),
                   knorm[t], *(b.free if n == 0 else ()))
        k = act(lambda e, hp=hp, b=b: e.activation(A[:, (8 + 2 * hp) * T:(8 + 2 * hp + 2) * T], b.ap[:, :], ACT.Copy, scale=p_("gk")), k)
        b.free = (k,)
        k_knT[hp] = k
    k_alltr = (pe.sem, pe.n)

    def mla_attention():
        pb = [Buf(S[:, i * 384:(i + 1) * 384]) for i in range(3)]
        pt = [Buf(R[:, 5 * T + i * 384:5 * T + (i + 1) * 384]) for i in range(3)]
        for x_ in pb + pt:
            x_.free = (k_alltr,)
        st = {}
        ku = []
        s8 = lambda h, j: sm[:, 128 + (h % 4) * 8 + j:129 + (h % 4) * 8 + j]
        r0 = [klq[2], k_qrT[(0, 0)], k_qrT[(1, 0)], k_knT[("r", 0)], k_knT[("r", 1)]]

        def stage_s(h):
            b = bank()
            p0 = 64 * (h % 2)
            q, k_ = qnT[:, h, :], knT[:, h, :]
            qr = hT[p0:p0 + 64, (h // 2) * T:(h // 2 + 1) * T]
            kr = hT[p0:p0 + 64, (4 + h // 2) * T:(5 + h // 2) * T]
            pe.waits([k_qnT[h // 2], k_knT[h // 2], *r0, *b.free])
            add = lambda f: pe.more(f)
            add(lambda e: mm(e, b.ap[:, 0:128], q[:, 0:128], k_[:, 0:128], True, True, True))
            add(lambda e: mm(e, b.ap[:, 128:384], q[:, 128:256], k_[:, 0:256], False, True, True))
            add(lambda e: mm(e, b.ap[:, 0:128], c_("ident"), c_("caus"), False, True, True))
            add(lambda e: mm(e, b.ap[:, 256:384], c_("ident"), c_("caus"), False, True, True))
            add(lambda e: mm(e, b.ap[:, 0:128], qr[:, 0:128], kr[:, 0:128], False, True, True))
            k = pe(lambda e: mm(e, b.ap[:, 128:384], qr[:, 128:256], kr[:, 0:256], False, True, True))
            p = pb[h % 3]
            rng = [(0, 128), (128, 384)]
            ke = []
            for t in range(2):
                a, z = rng[t]
                k1 = dve(lambda e, a=a, z=z, t=t: e.tensor_reduce(s8(h, t), b.ap[:, a:z], AX.X, ALU.max), k, *st.get(("s", h - 4), ()))
                k2 = dve(lambda e, t=t: e.tensor_scalar(s8(h, 2 + t), s8(h, t), scq[:, 8 * t + h:8 * t + h + 1], -1.0, ALU.mult, ALU.mult), k1, k_scq)
                k3 = act(lambda e, a=a, z=z, t=t: e.activation(p.ap[:, a:z], b.ap[:, a:z], ACT.Exp, bias=s8(h, 2 + t),
                                                               scale=scq[:, 8 * t + h:8 * t + h + 1], accum_out=s8(h, 4 + t)), k2, *p.free)
                k4 = dve(lambda e, t=t: e.reciprocal(s8(h, 6 + t), s8(h, 4 + t)), k3)
                k5 = dve(lambda e, a=a, z=z, t=t: e.tensor_scalar(p.ap[:, a:z], p.ap[:, a:z], s8(h, 6 + t), None, ALU.mult), k4)
                ke.append(k5)
            b.free = (k3,)
            st[("s", h)] = (k5,)
            st[h] = (p, ke)

        def stage_t(h):
            p, ke = st[h]
            b = bank()
            pe.waits([*ke, *b.free])
            pe.more(lambda e: e.transpose(b.ap[:, 0:128], p.ap[:, 0:128], c_("ident")))
            pe.more(lambda e: e.transpose(b.ap[:, 128:256], p.ap[:, 128:256], c_("ident")))
            k = pe(lambda e: e.transpose(b.ap[:, 256:384], p.ap[:, 256:384], c_("ident")))
            p.free = (k,)
            q = pt[h % 3]
            k2 = act(lambda e: e.activation(q.ap, b.ap[:, 0:384], ACT.Copy), k, *q.free)
            b.free = (k2,)
            st[h] = (q, k2)

        def stage_o(h):
            q, k2 = st.pop(h)
            b = bank()
            pe.waits([k2, *b.free, kvv[(0, h // 2)], kvv[(1, h // 2)]])
            pe.more(lambda e: mm(e, b.ap[:, 0:256], V[:, h * 128:(h + 1) * 128], q.ap[:, 0:256], True, True, True))
            k = pe(lambda e: mm(e, b.ap[:, 128:256], V[:, 1024 + h * 128:1024 + (h + 1) * 128], q.ap[:, 256:384], False, True, True))
            q.free = (k,)
            k3 = dve(lambda e: e.scalar_tensor_tensor(U[:, h * T:(h + 1) * T], b.ap[:, 0:256], 0.5, G[:, h * T:(h + 1) * T], ALU.mult, ALU.mult),
                     k, kg[h // 2], k_alltr)
            b.free = (k3,)
            ku.append(k3)
        for i in range(8 + 3):
            if i < 8:
                stage_s(i)
            fill()
            if 0 <= i - 2 < 8:
                stage_t(i - 2)
            if 0 <= i - 3 < 8:
                stage_o(i - 3)
        return ku

    ku = mla_attention()
    k_s = (act.sem, act.n), (dve.sem, dve.n), (pe.sem, pe.n)
    k_ctx = load(sp, "ctx", v3(S, 8), I["ctxT"].rearrange("(c p) t -> p c t", p=128), *k_s)
    k_wm = load(sp, "wm", A[:, 15 * T:16 * T], I["wmask"], *k_s)
    k_rw = load(sp, "rw", rw[:, :].rearrange("p (c e) -> p c e", c=8), I["router_w_2"][0].rearrange("(c p) e -> p c e", p=128))
    wmask = A[:, 15 * T:16 * T]
    gs = sm[:, 192:216]
    modv = mod[:, :].rearrange("p (g c t) -> p g c t", g=6, t=2)

    def gain(j, group, col, name):
        return dve(lambda e: e.scalar_tensor_tensor(gs[:, 8 * j:8 * j + 8], modv[:, group, :, col], 1.0, p_(name, 0, 8),
                                                    ALU.add, ALU.mult), k_pc, *[k_mod[i] for i in (2 * group, 2 * group + 1)])

    def sc_(c):
        return S[:, c * T:(c + 1) * T]

    state = {}

    def ctx_norm():
        fill(12)
        kg_ = [gain(0, 1, 0, "norm1"), gain(1, 1, 1, "norm1"), gain(2, 4, 0, "norm2")]
        state["gain"] = kg_
        state["khc"], _ = rms_T(sc_, 8, D, [k_ctx] * 8, lambda c: gs[:, 8 + c:9 + c], sc_, lambda c: m_(0, c, 1),
                                scr=v3(A, 8), k_scr=k_s)

    out_proj(I["l1_w_out"], lambda c: U[:, c * T:(c + 1) * T], ku, None, hook=ctx_norm)
    if level == 2:
        return finish(nc, locals())
    khc = state["khc"]
    k_old = (pe.sem, pe.n)
    kh, _ = rms_T(xc, 8, D, kx, lambda c: gs[:, c:c + 1], hc, lambda c: m_(0, c), scr=v3(A, 8), k_scr=(k_old, *khc))
    w = I["w_in_2"][0]

    HU = G[:, 0:6 * 258].rearrange("p (c t) -> p c t", c=6)
    CF = A[:, 12 * T:12 * T + 572].rearrange("p (c t) -> p c t", c=2)
    CT = v3(R, 6)
    cy = v3(R, 2, T, at=6 * T)
    kz1 = pool(lambda e: e.memset(HU[:, :, 0:1], 0.0), k_old)
    kz1 = pool(lambda e: e.memset(HU[:, :, 257:258], 0.0), k_old)
    kz2 = pool(lambda e: e.memset(CF[:, :, 0:15], 0.0), k_old)
    kz2 = pool(lambda e: e.memset(CF[:, :, 271:286], 0.0), k_old)
    k_hu, k_cf = {}, []
    aglu = {}

    def consume_mix(ch, b, k):
        bb = b.ap[:, :].rearrange("p (c t) -> p c t", c=2)
        if ch < 6:
            k2 = act(lambda e: e.activation(HU[:, ch:ch + 2, 1:257], bb, ACT.Copy), k, k_old)
            k_hu[ch] = k_hu[ch + 1] = k2
            return (k2,)
        if ch == 6:
            o = CF[:, :, 15:271]
            k2 = act(lambda e: e.activation(o, bb, ACT.Copy), k, k_old)
            aglu[0] = k2
            return (k2,)
        tg = v3(A, 2, T, at=8 * T)
        k2 = act(lambda e: e.activation(tg, bb, ACT.Tanh, scale=0.5), k, k_old)
        for c in range(2):
            k_cf.append(dve(lambda e, c=c: e.scalar_tensor_tensor(CF[:, c, 15:271], tg[:, c, :], 1.0, CF[:, c, 15:271], ALU.add, ALU.mult), k2, aglu[0]))
        return (k2,)

    ch = 0
    for a, n in ((1536, 512), (2048, 512), (2560, 256)):
        W, kW, i = piece(wview(w, a, n), 8, n)
        k = proj_T(W, kW, hc, kh, list(range(0, n, 128)), 8, lambda j0, b, k, ch=ch: consume_mix(ch + j0, b, k))
        done_with(i, k)
        ch += n // 128

    k_ct = []
    for c in range(6):
        kk = dve(lambda e, c=c: e.tensor_scalar(CT[:, c, :], HU[:, c, 0:256], p_("sw", 3 * c), p_("sb", c), ALU.mult, ALU.add), k_hu[c], kz1, k_old)
        for j in (1, 2):
            kk = dve(lambda e, c=c, j=j: e.scalar_tensor_tensor(CT[:, c, :], HU[:, c, j:j + 256], p_("sw", 3 * c + j), CT[:, c, :], ALU.mult, ALU.add), kk)
        k_ct.append(kk)
    kcy = [None, None]
    for j in range(31):
        for c in range(2):
            if j == 0:
                kcy[c] = dve(lambda e, c=c: e.tensor_scalar(cy[:, c, :], CF[:, c, 0:256], p_("cw", c), None, ALU.mult), *k_cf, kz2, k_old)
            else:
                kcy[c] = dve(lambda e, c=c, j=j: e.scalar_tensor_tensor(cy[:, c, :], CF[:, c, j:j + 256], p_("cw", 2 * j + c), cy[:, c, :], ALU.mult, ALU.add), kcy[c])

    qkT = v3(A, 12)
    k_q = {}
    for src, off, a, sc in ((0, 0, 0, 0.125), (0, 4, 512, 1.0), (1, 8, 512, 1.0)):
        if src == 0:
            W, kW, i = piece(wview(w, a, 512), 8, 512)

        def consume(j0, b, k, off=off, sc=sc):
            k2 = act(lambda e: e.activation(qkT[:, off + j0:off + j0 + 2, :], b.ap[:, :].rearrange("p (c t) -> p c t", c=2), ACT.Copy, scale=sc),
                     k, *k_cf)
            k_q[off + j0] = k_q[off + j0 + 1] = k2
            return (k2,)
        hs, kk = (sc_, khc) if src else (hc, kh)
        k = proj_T(W, kW, hs, kk, [0, 128, 256, 384], 8, consume)
        done_with(i, k)
    W, kW, i = piece(wview(w, 1024, 512), 8, 512)
    k_v = []
    for t in range(4):
        def consume(b, k, t=t):
            k2 = act(lambda e: e.activation(V[:, t * 512:(t + 1) * 512], b.ap[:, :], ACT.Copy), k, k_old)
            k_v.append(k2)
            return (k2,)
        k = proj_tok(W, kW, sc_ if t >= 2 else hc, khc if t >= 2 else kh, t % 2, 0, 512, 8, consume)
    done_with(i, k)
    k_proj = k

    bias = [Buf(BB[:, i * 512:(i + 1) * 512]) for i in range(4)]
    for b_ in bias:
        b_.free = (k_old,)
    bsem = [sem(f"s_bias{i}") for i in range(4)]
    buse = [0] * 4
    k_bias = {}
    rpb = I["rpb"]

    def load_bias(h):
        b = bias[h % 4]
        for r in range(4):
            src = bass.AP(rpb.tensor, h * 465 + (7 - r) * 31 + 15 - 63, [[1, 64], [31, 4], [1, 64]])
            dst = b.ap[64 * (r % 2):64 * (r % 2) + 64, (r // 2) * 256:(r // 2) * 256 + 256].rearrange("p (a c) -> p a c", a=4)
            sp.dma(lambda e: e.dma_start(dst, src), bsem[h % 4], *b.free)
        buse[h % 4] += 64
        b3 = b.ap.rearrange("p (t k) -> p t k", t=2)
        k_bias[h] = pool(lambda e: e.tensor_tensor(b3, b3, wmask.unsqueeze(1).broadcast_to([128, 2, 256]), ALU.add),
                         (bsem[h % 4], buse[h % 4]), k_wm)

    for h in range(4):
        load_bias(h)

    fwd = v3(CC, 2, 512, at=CONST["fwd"][0])
    inv = v3(CC, 4, 256, at=CONST["inv"][0])
    KA, KB, KC = v3(SPEC, 2, 512), v3(SPEC, 2, 512, at=1024), SPEC[:, 2048:2560]
    kmix = [None] * 8

    def hyena_run():
        Zt = v3(G, 2)
        Y = v3(G, 4, T, at=2 * T)
        tmp = v3(G, 2, T, at=6 * T)
        zT = CT[:, 4:6, :]
        kzt = [k_ct[4], k_ct[5]]
        for n in range(2):
            b = bank()
            for c in range(2):
                for t in range(2):
                    o = b.ap[:, t * 256 + c * 128:t * 256 + c * 128 + 128]
                    k = pe(lambda e: e.transpose(o, zT[:, c, t * 128:(t + 1) * 128], c_("ident")), kzt[c], *b.free)
            k = act(lambda e: e.activation(Zt, b.ap[:, :].rearrange("p (c t) -> p c t", c=2), ACT.Copy), k, *k_ct)
            b.free = (k,)
            yield
            zb = []
            for part in range(2):
                b = bank()
                for f in range(2):
                    for t in range(2):
                        kk = pe(lambda e: mm(e, b.ap[:, f * 256:(f + 1) * 256], fwd[:, t, part * 256 + f * 128:part * 256 + f * 128 + 128],
                                             Zt[:, t, :], t == 0, t == 1), k, *b.free)
                zb.append((b, kk))
            (br, kr), (bi, ki) = zb
            sl = slice(n * 256, n * 256 + 256)
            c2 = lambda a: a.rearrange("p (c t) -> p c t", c=2)
            k1 = dve(lambda e: e.tensor_tensor(Y[:, 0:2, :], c2(br.ap[:, :]), KA[:, :, sl], ALU.mult), kr, *k_ct)
            k2 = dve(lambda e: e.tensor_tensor(tmp, c2(bi.ap[:, :]), KB[:, :, sl], ALU.mult), ki)
            k3 = pool(lambda e: e.tensor_tensor(Y[:, 0:2, :], Y[:, 0:2, :], tmp, ALU.subtract), k1, k2)
            k4 = dve(lambda e: e.tensor_tensor(Y[:, 2:4, :], c2(br.ap[:, :]), KB[:, :, sl], ALU.mult), kr)
            k5 = dve(lambda e: e.tensor_tensor(tmp[:, 0, :], bi.ap[:, 0:256], KC[:, sl], ALU.mult), k3)
            k6 = dve(lambda e: e.tensor_tensor(tmp[:, 1, :], bi.ap[:, 256:512], KA[:, 1, sl], ALU.mult), k3)
            br.free, bi.free = (k4,), (k6,)
            k7 = pool(lambda e: e.tensor_tensor(Y[:, 2:4, :], Y[:, 2:4, :], tmp, ALU.add), k4, k5, k6)
            yield
            yield
            b = bank()
            for c in range(2):
                for f in range(4):
                    k = pe(lambda e: mm(e, b.ap[:, c * 256:(c + 1) * 256], Y[:, f, c * 128:(c + 1) * 128], inv[:, f, :], f == 0, f == 3), k3, k7, *b.free)
            kn = []
            for c in range(2):
                o = zT[:, c, :] if n == 0 else U[:, (4 + c) * T:(5 + c) * T]
                k8 = dve(lambda e: e.scalar_tensor_tensor(zT[:, c, :], zT[:, c, :], p_("bd", 2 * n + c), b.ap[:, c * 256:(c + 1) * 256], ALU.mult, ALU.add), k)
                k9 = dve(lambda e: e.tensor_tensor(o, zT[:, c, :], CT[:, 2 * n + c, :], ALU.mult), k8, k_ct[2 * n + c], k_old)
                kn.append(k9)
            b.free = (k8,)
            kzt = kn
            yield
        kmix[4], kmix[5] = kn

    def cf_run():
        t8 = v3(R, 2, T, at=8 * T)
        t9 = v3(A, 2, T, at=12 * T)
        ky = []
        for c in range(2):
            ky.append(dve(lambda e: e.tensor_scalar(cy[:, c, :], cy[:, c, :], 0.5, p_("cb", c), ALU.mult, ALU.add), kcy[c]))
        b = bank()
        for c in range(2):
            k = pe(lambda e: mm(e, b.ap[:, 0:T], c_("ones"), cy[:, c, :], c == 0, c == 1), ky[c], *b.free)
        for c in range(2):
            ky[c] = dve(lambda e: e.scalar_tensor_tensor(cy[:, c, :], b.ap[:, 0:T], -1.0 / 256, cy[:, c, :], ALU.mult, ALU.add), k)
        b.free = (ky[1],)
        k = act(lambda e: e.activation(t8, cy, ACT.Square), *ky)
        yield
        b = bank()
        for c in range(2):
            kk = pe(lambda e: mm(e, b.ap[:, 0:T], c_("ones"), t8[:, c, :], c == 0, c == 1), k, *b.free)
        k = dve(lambda e: e.tensor_scalar(sm_r, b.ap[:, 0:T], 1.0 / 256, 1e-6, ALU.mult, ALU.add), kk, *smr_free[0])
        b.free = (k,)
        k = rsq(sm_r, k)
        for c in range(2):
            k1 = dve(lambda e: e.tensor_tensor(cy[:, c, :], cy[:, c, :], sm_r, ALU.mult), k)
            ky[c] = dve(lambda e: e.tensor_scalar(cy[:, c, :], cy[:, c, :], p_("lng", c), p_("lnb", c), ALU.mult, ALU.add), k1)
        smr_free[0] = (k1,)
        k = act(lambda e: e.activation(t9, cy, ACT.Tanh, scale=0.5), *ky)
        yield
        for c in range(2):
            k1 = dve(lambda e: e.scalar_tensor_tensor(cy[:, c, :], t9[:, c, :], 1.0, cy[:, c, :], ALU.add, ALU.mult), k)
            kmix[6 + c] = dve(lambda e: e.tensor_scalar(U[:, (6 + c) * T:(7 + c) * T], cy[:, c, :], 0.5, None, ALU.mult), k1, k_old)

    def na_attention(steps):
        pb = [Buf(hT[:, i * 512:(i + 1) * 512]) for i in range(3)]
        pt = [Buf(S[:, i * 512:(i + 1) * 512]) for i in range(3)]
        for x_ in pb + pt:
            x_.free = (k_proj,)
        st = {}
        s4 = lambda u, j: sm[:, 128 + (u % 4) * 4 + j:129 + (u % 4) * 4 + j]

        def stage_s(u):
            h, t = u // 2, u % 2
            b = bank()
            p0 = 64 * (h % 2)
            q = qkT[p0:p0 + 64, h // 2, t * 128:(t + 1) * 128]
            pe.waits([k_q[h // 2], k_q[4 + h // 2], k_q[8 + h // 2], k_bias[h], *b.free])
            pe.more(lambda e: mm(e, b.ap[:, 0:256], q, qkT[p0:p0 + 64, 4 + h // 2, :], True, True, True))
            pe.more(lambda e: mm(e, b.ap[:, 256:512], q, qkT[p0:p0 + 64, 8 + h // 2, :], False, True, True))
            k = pe(lambda e: mm(e, b.ap[:, 0:256], c_("flip"), bias[h % 4].ap[:, t * 256:(t + 1) * 256], False, True, True))
            if t == 1:
                bias[h % 4].free = (k,)
                if h + 4 < 8:
                    load_bias(h + 4)
            p = pb[u % 3]
            k1 = dve(lambda e: e.tensor_reduce(s4(u, 0), b.ap[:, :], AX.X, ALU.max), k, *st.get(("s", u - 4), ()))
            k2 = dve(lambda e: e.tensor_scalar(s4(u, 1), s4(u, 0), -1.0, None, ALU.mult), k1)
            k3 = act(lambda e: e.activation(p.ap, b.ap[:, :], ACT.Exp, bias=s4(u, 1), accum_out=s4(u, 2)), k2, *p.free)
            b.free = (k3,)
            k4 = dve(lambda e: e.reciprocal(s4(u, 3), s4(u, 2)), k3)
            k5 = dve(lambda e: e.tensor_scalar(p.ap, p.ap, s4(u, 3), None, ALU.mult), k4)
            st[("s", u)] = (k5,)
            st[u] = (p, k5)

        def stage_t(u):
            p, kp = st[u]
            b = bank()
            for j in range(4):
                k = pe(lambda e: e.transpose(b.ap[:, j * 128:(j + 1) * 128], p.ap[:, j * 128:(j + 1) * 128], c_("ident")), kp, *b.free)
            p.free = (k,)
            q = pt[u % 3]
            k2 = act(lambda e: e.activation(q.ap, b.ap[:, :], ACT.Copy), k, *q.free)
            b.free = (k2,)
            st[u] = (q, k2)


        def stage_o(u):
            h, t = u // 2, u % 2
            q, k2 = st.pop(u)
            b = banks[6 + (h // 2) % 2]
            p0 = 64 * (h % 2)
            for j in range(4):
                k = pe(lambda e: mm(e, b.ap[p0:p0 + 64, t * 128:(t + 1) * 128], V[:, j * 512 + h * 64:j * 512 + h * 64 + 64],
                                    q.ap[:, j * 128:(j + 1) * 128], j == 0, j == 3), k2, *k_v, *b.free)
            q.free = (k,)
            if u % 4 == 3:
                c = h // 2
                k3 = dve(lambda e: e.tensor_copy(U[:, c * T:(c + 1) * T], b.ap[:, 0:256]), k, k_old)
                b.free = (k3,)
                kmix[c] = k3
        for i in range(16 + 3):
            if i < 16:
                stage_s(i)
            if steps:
                try:
                    next(steps[0])
                except StopIteration:
                    steps.pop(0)
            if 0 <= i - 2 < 16:
                stage_t(i - 2)
            if 0 <= i - 3 < 16:
                stage_o(i - 3)

    steps = [hyena_run(), cf_run()]
    na_attention(steps)
    for s_ in steps:
        for _ in s_:
            pass
    if level == 25:
        s5 = sem("s_dbg")
        sp.dma(lambda e: e.dma_start(O["dbg"], U[:, :]), s5, *kmix)
        sp.items.append(("w", s5, 16))
        return finish(nc, locals())
    out_proj(I["w_out_2"][0], lambda c: U[:, c * T:(c + 1) * T], kmix, lambda c: m_(2, c))
    if level == 3:
        return finish(nc, locals())

    k_old = (pe.sem, pe.n)
    kh, _ = rms_T(xc, 8, D, kx, lambda c: gs[:, 16 + c:17 + c], hc, lambda c: m_(3, c))
    b = bank()
    for t in range(2):
        for c in range(8):
            k = pe(lambda e: mm(e, b.ap[:, t * 16:(t + 1) * 16], hc(c)[:, t * 128:(t + 1) * 128], rw[:, c * 16:(c + 1) * 16], c == 0, c == 7),
                   kh[c], k_rw, *b.free)
    aff = sm[:, 128:160]
    a3 = aff.rearrange("p (t e) -> p t e", t=2)
    mx = sm[:, 160:164]
    b3 = b.ap[:, 0:32].rearrange("p (t e) -> p t e", t=2)
    k = dve(lambda e: e.tensor_reduce(mx[:, 0:2], b3, AX.X, ALU.max), k)
    k = dve(lambda e: e.tensor_tensor(a3, b3, mx[:, 0:2].unsqueeze(2).broadcast_to([128, 2, 16]), ALU.subtract), k)
    b.free = (k,)
    k = act(lambda e: e.activation(aff, aff, ACT.Exp), k)
    k = dve(lambda e: e.tensor_reduce(mx[:, 2:4], a3, AX.X, ALU.add), k)
    k = dve(lambda e: e.reciprocal(mx[:, 2:4], mx[:, 2:4]), k)
    k_aff = dve(lambda e: e.tensor_tensor(a3, a3, mx[:, 2:4].unsqueeze(2).broadcast_to([128, 2, 16]), ALU.mult), k)
    b = bank()
    for t in range(2):
        k = pe(lambda e: e.transpose(b.ap[0:16, t * 128:(t + 1) * 128], a3[:, t, :], c_("ident")), k_aff, *b.free)
    w0 = BB[0:16, 0:256]
    sel = BB[0:16, 256:512]
    slot = BB[0:16, 512:768]
    m8 = BB[0:16, 768:800]
    k = dve(lambda e: e.tensor_copy(w0, b.ap[0:16, 0:256]), k)
    b.free = (k,)
    k_ht = []
    for t in range(2):
        for c0 in (0, 4):
            b = bank()
            for c in range(c0, c0 + 4):
                kk = pe(lambda e: e.transpose(b.ap[:, (c - c0) * 128:(c - c0 + 1) * 128], hc(c)[:, t * 128:(t + 1) * 128], c_("ident")), kh[c], *b.free)
            kk = act(lambda e: e.activation(V[:, t * 1024 + c0 * 128:t * 1024 + c0 * 128 + 512], b.ap[:, :], ACT.Copy), kk, k_old)
            b.free = (kk,)
            k_ht.append(kk)
    for r in range(4):
        k = dve(lambda e: e.max(m8[:, 8 * r:8 * r + 8], w0), k)
        k = dve(lambda e: e.match_replace(w0, m8[:, 8 * r:8 * r + 8], w0, -1.0), k)
    k = dve(lambda e: e.tensor_scalar(sel, w0, -1.0, None, ALU.is_equal), k)
    k = dve(lambda e: e.tensor_tensor_scan(slot, sel, sel, 0.0, ALU.add, ALU.bypass), k)
    k = dve(lambda e: e.tensor_tensor(slot, slot, sel, ALU.mult), k)
    b = bank()
    for t in range(2):
        k1 = pe(lambda e: e.transpose(b.ap[:, t * 16:(t + 1) * 16], slot[:, t * 128:(t + 1) * 128], c_("ident")[0:16, 0:16]), k, *b.free)
    GM = v3(S, 2, 512)
    GA = v3(S, 2, 512, at=1024)
    k_gm = []
    k_ga = []
    io = c_("iota").unsqueeze(1).broadcast_to([128, 16, 32])
    ko_ = (act.sem, act.n)
    for t in range(2):
        g3 = GM[:, t, :].rearrange("p (e j) -> p e j", e=16)
        k2 = dve(lambda e: e.tensor_tensor(g3, b.ap[:, t * 16:(t + 1) * 16].unsqueeze(2).broadcast_to([128, 16, 32]), io, ALU.is_equal), k1, k_old, kh[0])
        k_gm.append(k2)
        ga3 = GA[:, t, :].rearrange("p (e j) -> p e j", e=16)
        k_ga.append(pool(lambda e: e.tensor_tensor(ga3, g3, a3[:, t, :].unsqueeze(2).broadcast_to([128, 16, 32]), ALU.mult), k2, k_aff))
    b.free = (k2,)
    xe = v3(A, 8, 512)
    k_xe = []
    for c in range(8):
        b = bank()
        for t in range(2):
            k = pe(lambda e: mm(e, b.ap[:, :], V[:, t * 1024 + c * 128:t * 1024 + (c + 1) * 128], GM[:, t, :], t == 0, t == 1),
                   k_gm[t], *k_ht, *b.free)
        if c % 2:
            k = act(lambda e: e.activation(xe[:, c, :], b.ap[:, :], ACT.Copy), k, k_old)
        else:
            k = dve(lambda e: e.tensor_copy(xe[:, c, :], b.ap[:, :]), k, k_old)
        b.free = (k,)
        k_xe.append(k)
    Sg = v3(R, 4)
    k_sg = []
    for g in range(4):
        b = bank()
        for t in range(2):
            k = pe(lambda e: e.transpose(b.ap[:, t * 128:(t + 1) * 128], GA[:, t, g * 128:(g + 1) * 128], c_("ident")), k_ga[t], *b.free)
        k = act(lambda e: e.activation(Sg[:, g, :], b.ap[:, 0:256], ACT.Copy), k)
        b.free = (k,)
        k_sg.append(k)

    hb = [Buf(G[:, i * 512:(i + 1) * 512]) for i in range(2)]
    tb = [Buf(G[:, (2 + i) * 512:(3 + i) * 512]) for i in range(2)]
    ysb = Buf(U[:, 0:1024])
    ytk = Buf(U[:, 1024:2048])
    for x_ in hb + tb + [ysb, ytk]:
        x_.free = (k_old,)
    yb, gb = banks[4:6], banks[6:8]
    W1, W3, W2 = I["expert_w1_2"][0], I["expert_w3_2"][0], I["expert_w2_2"][0]
    k_y = []
    for ex in range(16):
        y_ = yb[ex % 2]
        hx, tx = hb[ex % 2], tb[ex % 2]
        xs = slice(ex * 32, ex * 32 + 32)
        kh2 = []
        for f in range(4):
            kk = []
            au = banks[f]
            for w_, o_ in ((W1, 0), (W3, 128)):
                W, kW, i = piece(wview(w_[ex], f * 512, 512), 8, 512)
                pe.waits([kW, *k_xe, *au.free])
                for j in range(4):
                    for c in range(8):
                        fn = lambda e: mm(e, au.ap[:, o_ + j * 32:o_ + (j + 1) * 32], W[:, c, j * 128:(j + 1) * 128], xe[:, c, xs], c == 0, c == 7)
                        if j == 3 and c == 7:
                            kk.append(pe(fn))
                        else:
                            pe.more(fn)
                done_with(i, kk[-1])
            q = slice(128 * f, 128 * f + 128)
            k1 = act(lambda e: e.activation(tx.ap[:, q], au.ap[:, 0:128], ACT.Tanh, scale=0.5), *kk, *tx.free)
            k2 = dve(lambda e: e.scalar_tensor_tensor(tx.ap[:, q], tx.ap[:, q], 1.0, au.ap[:, 0:128], ALU.add, ALU.mult), k1)
            k3 = dve(lambda e: e.scalar_tensor_tensor(hx.ap[:, q], tx.ap[:, q], 0.5, au.ap[:, 128:256], ALU.mult, ALU.mult), k2, kk[1], *hx.free)
            kh2.append(k3)
            au.free = (k3,)
        tx.free = (k3,)
        for f in range(4):
            W, kW, i = piece(W2[ex].rearrange("(c p) n -> p c n", p=128)[:, 4 * f:4 * f + 4, :], 4, 1024)
            pe.waits([kW, kh2[f], *(y_.free if f == 0 else ())])
            for j in range(4):
                for c in range(8):
                    fn = lambda e: mm(e, y_.ap[:, c * 32:(c + 1) * 32], W[:, j, c * 128:(c + 1) * 128],
                                      hx.ap[:, (4 * f + j) * 32:(4 * f + j + 1) * 32], f == 0 and j == 0 and c == 0, f == 3 and j == 3 and c == 7, True)
                    if j == 3 and c == 7:
                        k = pe(fn)
                    else:
                        pe.more(fn)
            done_with(i, k)
        hx.free = (k,)
        g, m = ex // 4, ex % 4
        ys = ysb.ap.rearrange("p (c m t) -> p c m t", c=8, m=4)
        k = act(lambda e: e.activation(ys[:, :, m, :], y_.ap[:, 0:256].rearrange("p (c t) -> p c t", c=8), ACT.Copy), k, *ysb.free)
        y_.free = (k,)
        k_y.append(k)
        if m == 3:
            kt_ = []
            for n in range(2):
                b = gb[n]
                for c in range(4):
                    k = pe(lambda e: e.transpose(b.ap[:, c * 128:(c + 1) * 128], ysb.ap[:, (4 * n + c) * 128:(4 * n + c + 1) * 128], c_("ident")), *k_y[-4:], *b.free)
                k1 = act(lambda e: e.activation(ytk.ap[:, n * 512:(n + 1) * 512], b.ap[:, :], ACT.Copy), k, *ytk.free)
                b.free = (k1,)
                kt_.append(k1)
            ysb.free = (k,)
            for c0 in range(0, 8, 2):
                b = gb[(c0 // 2) % 2]
                for c in (c0, c0 + 1):
                    o = b.ap[:, (c % 2) * T:(c % 2 + 1) * T]
                    k = pe(lambda e: mm(e, o, ytk.ap[:, c * 128:(c + 1) * 128], Sg[:, g, :], True), kt_[c // 4], k_sg[g], *b.free)
                for c in (c0, c0 + 1):
                    o = b.ap[:, (c % 2) * T:(c % 2 + 1) * T]
                    kx[c] = dve(lambda e: e.scalar_tensor_tensor(xc(c), o, m_(5, c), xc(c), ALU.mult, ALU.add), k, kx[c])
                b.free = (kx[c],)
            ytk.free = (k,)
    if level == 4:
        return finish(nc, locals())
    oT = lambda c: hT[:, c * T:(c + 1) * T]
    ko, _ = rms_T(xc, 8, D, kx, lambda c: p_("final", c), oT)
    xout = []
    for half in range(2):
        s = sem(f"s_out{half}")
        sp.dma(lambda e: e.dma_start(O["out"].rearrange("(c p) t -> p c t", p=128)[:, 4 * half:4 * half + 4, :], v3(hT, 4, T, at=4 * half * T)), s,
               *ko[4 * half:4 * half + 4])
        xout.append(s)
    for s in xout:
        sp.items.append(("w", s, 16))
    finish(nc, locals())


def finish(nc, L):
    I, O = L["I"], L["O"]
    sp, sem = L["sp"], L["sem"]
    if "xout" not in L:
        s = sem("s_out")
        xT = L["xT"]
        sp.dma(lambda e: e.dma_start(O["out"].rearrange("(c p) t -> p c t", p=128), xT[:, :].rearrange("p (c t) -> p c t", c=8)), s, *L["kx"])
        sp.items.append(("w", s, 16))
        if L["level"] == 0:
            s2 = sem("s_out2")
            sp.dma(lambda e: e.dma_start(O["dbg"], L["SPEC"][:, :]), s2, *L["k_spec"])
            sp.items.append(("w", s2, 16))
    block = L["ctx"].enter_context(nc.Block())

    def emit(q, eng):
        for it in q.items:
            if it[0] == "w":
                eng.wait_ge(it[1], it[2])
            elif it[0] == "m":
                it[1](eng)
            elif it[0] == "t":
                eng.preload_act_table_set(it[1])
            else:
                it[1](eng).then_inc(it[2], it[3])

    @block.sync
    def _(eng):
        emit(L["sp"], eng)

    @block.gpsimd
    def _(eng):
        emit(L["pool"], eng)

    @block.scalar
    def _(eng):
        emit(L["act"], eng)

    @block.vector
    def _(eng):
        emit(L["dve"], eng)

    @block.tensor
    def _(eng):
        emit(L["pe"], eng)


def _constants():
    f = np.float64
    p = np.arange(128)
    c = {}
    c["ident"] = np.eye(128)
    c["ones"] = np.ones((128, 128))
    c["ntri"] = -(p[:, None] >= p[None, :]).astype(f)
    c["nones"] = -np.ones((128, 128))
    c["m01"] = (p[:, None] < p[None, :]).astype(f)
    cap = np.where(p[:, None] < p[None, :], 0.0, NEG)
    c["cap"] = np.concatenate([cap, np.zeros((128, 128)), cap], 1)
    c["caus"] = np.where(p[None, :] <= p[:, None], 0.0, NEG)
    c["iota"] = np.tile(np.arange(1, 33), (128, 1))
    half = 32
    inv = (np.float32(10000.0) ** (-np.arange(half, dtype=np.float32) / np.float32(half))).astype(np.float32)
    ang = (np.arange(T, dtype=np.float32)[:, None] * inv[None, :]).astype(np.float32).astype(f)
    cos = np.concatenate([np.cos(ang), np.cos(ang)], 1)
    sin = np.concatenate([-np.sin(ang), np.sin(ang)], 1)
    c["cosd"] = np.concatenate([cos[:128], cos[128:]], 1)
    c["sind"] = np.concatenate([sin[:128], sin[128:]], 1)
    s = np.arange(T)
    k = np.arange(T)
    th = 2 * math.pi * ((s[:, None] * k[None, :]) % 512) / 512
    Fre, Fim = np.cos(th), -np.sin(th)
    alt = np.where(s % 2 == 0, 1.0, -1.0)
    Fimn = Fim.copy()
    Fimn[:, 0] = alt
    fw = np.concatenate([Fre, Fimn], 1)
    c["fwd"] = np.concatenate([fw[:128], fw[128:]], 1)
    ny = Fre[:, :128].copy()
    ny[:, 0] = alt
    c["nyq"] = np.concatenate([ny[:128], ny[128:]], 1)
    wt = np.where(k == 0, 1.0, 2.0)[:, None] / 512
    Gre = wt * np.cos(th.T)
    Gim = -(2.0 / 512) * np.sin(th.T)
    Gim[0] = alt / 512
    g = np.concatenate([Gre, Gim], 0)
    c["inv"] = np.concatenate([g[i * 128:(i + 1) * 128] for i in range(4)], 1)
    c["flip"] = (p[:, None] // 64 * 64 + 63 - p[:, None] % 64 == p[None, :]).astype(f)
    c["half"] = np.full((128, 1), -0.5)
    out = np.zeros((128, NCONST), np.float32)
    for name, (at, n) in CONST.items():
        out[:, at:at + n] = c[name].astype(np.float32)
    t = np.arange(T, dtype=np.float32)[:, None] / np.float32(T - 1)
    fb = np.linspace(1e-4, 15, 16, dtype=np.float32)[None, :]
    angf = (fb * np.float32(TWO_PI) * np.arange(T, dtype=np.float32)[:, None] / np.float32(T)).astype(f)
    z = np.concatenate([t.astype(f), np.cos(angf), -np.sin(angf)], 1).T.astype(np.float32)
    rate = np.abs(np.linspace(math.log(1e-2) / 1.5, math.log(1e-2) / 0.3, 256, dtype=np.float32)).astype(f)
    dec = np.exp(-t.astype(f) * rate[None, :])
    decb = dec.copy()
    decb[0] = 0
    d = np.concatenate([dec[:128], decb[:128], dec[128:], decb[128:]], 1).astype(np.float32)
    col = np.arange(T) % 64
    c0 = np.clip(col - 8, 0, 48)
    ok = (col[None, :] >= c0[:, None]) & (col[None, :] < c0[:, None] + 16)
    wm = np.where(ok, 0.0, NEG).astype(np.float32)[:128]
    wm = np.ascontiguousarray(wm.reshape(2, 64, T)[:, ::-1].reshape(128, T))
    return out, np.ascontiguousarray(z), d, wm


def _cols(inp):
    out = np.zeros((128, NCOL), np.float32)

    def put(name, a):
        at, n = COLS[name]
        out[:, at:at + n] = a

    ch = lambda v: np.asarray(v).reshape(-1, 128).T
    put("l0_norm", ch(inp["l0_norm"]))
    put("l1_norm", ch(inp["l1_norm"]))
    put("q_a", ch(inp["l1_q_a_norm"]))
    put("kv_a", ch(inp["l1_kv_a_norm"]))
    put("gq", np.asarray(inp["l1_q_head_norm"])[:128, None])
    put("gk", np.asarray(inp["l1_k_head_norm"])[:128, None])
    put("b_mod", ch(inp["b_mod_2"][0]))
    put("norm1", ch(inp["norm1_g_2"][0]))
    put("norm2", ch(inp["norm2_g_2"][0]))
    put("final", ch(inp["final_norm_g_2"]))
    put("c", np.stack([ch(inp["c_2"][0]), ch(inp["c_ctx_2"])], 2).reshape(128, 16))
    put("sw", np.asarray(inp["hy_short_w_2"][0]).reshape(3, 6, 128).transpose(2, 1, 0).reshape(128, 18))
    put("sb", ch(inp["hy_short_b_2"][0]))
    put("bd", np.asarray(inp["hy_bias_d_2"][0]).reshape(2, 2, 128).transpose(2, 0, 1).reshape(128, 4))
    put("cw", np.asarray(inp["cf_dw_w_2"][0]).reshape(31, 2, 128).transpose(2, 0, 1).reshape(128, 62))
    put("cb", ch(inp["cf_dw_b_2"][0]))
    put("lng", ch(inp["cf_ln_g_2"][0]))
    put("lnb", ch(inp["cf_ln_b_2"][0]))
    return out


def kernel(**inputs):
    import concourse.bacc as _bacc
    from concourse.bass_utils import run_bass_kernel_spmd as _run

    inp = {k: np.asarray(v) for k, v in inputs.items()}
    consts, zfeat, decay, wmask = _constants()
    arr = {
        "xT": np.ascontiguousarray(inp["x"][0].T),
        "ctxT": np.ascontiguousarray(inp["ctx_2"][0].T),
        "cols": _cols(inp),
        "consts": consts, "zfeat": zfeat, "decay": decay, "wmask": wmask,
        "rowg": np.concatenate([inp["l1_q_head_norm"][128:], inp["l1_k_head_norm"][128:]])[None, :],
        "filtp": np.stack([inp["hy_filt_b1_2"][0], inp["hy_filt_freq_2"][0], inp["hy_filt_b2_2"][0]], 1),
        "rpb": np.ascontiguousarray(inp["na_rpb_2"][0].reshape(8, 15 * 31)),
    }
    for n in ["l0_w_in", "l0_w_out", "l1_w_in", "l1_w_uq", "l1_w_ukv", "l1_w_out", "w_mod_2", "w_in_2",
              "hy_filt_w1_2", "hy_filt_w2_2", "hy_filt_w3_2", "w_out_2", "router_w_2",
              "expert_w1_2", "expert_w3_2", "expert_w2_2"]:
        arr[n] = np.ascontiguousarray(inp[n])
    nc = _bacc.Bacc("TRN2", target_bir_lowering=False, num_devices=1)
    ins = {n: nc.dram_tensor(f"in_{n}", a.shape, F32, kind="ExternalInput").ap() for n, a in arr.items()}
    outs = {"out": nc.dram_tensor("out_0", (D, T), F32, kind="ExternalOutput").ap()}
    if LEVEL == 25:
        outs["dbg"] = nc.dram_tensor("dbg_0", (128, 8 * T), F32, kind="ExternalOutput").ap()
    build_program(nc, ins, outs, LEVEL)
    r = _run(nc, [{f"in_{n}": a for n, a in arr.items()}], core_ids=[0])
    got = np.asarray(r.results[0]["out_0"])
    return np.ascontiguousarray(got.T)[None]


LEVEL = 99
```

```python
import math
from collections import deque
from contextlib import ExitStack

import numpy as np
import concourse.bass as bass
from concourse import mybir

F32 = mybir.dt.float32
ALU = mybir.AluOpType
ACT = mybir.ActivationFunctionType
AX = mybir.AxisListType

T = 256
D = 1024
NEG = -1e30
NSLOT = 6
SLOT = 4096
TWO_PI = 2.0 * math.pi
MAGIC = 1.5 * 2.0 ** 23

COLS = {}


def _cols_layout():
    at = 0
    for name, n in [("l0_norm", 8), ("l1_norm", 8), ("q_a", 2), ("kv_a", 1), ("gq", 1), ("gk", 1),
                    ("b_mod", 48), ("norm1", 8), ("norm2", 8), ("final", 8), ("c", 16),
                    ("sw", 18), ("sb", 6), ("bd", 4), ("cw", 62), ("cb", 2), ("lng", 2), ("lnb", 2)]:
        COLS[name] = (at, n)
        at += n
    return at


NCOL = _cols_layout()

CONST = {}


def _const_layout():
    at = 0
    for name, n in [("nones", 128), ("ident", 128), ("ntri", 128), ("m01", 128),
                    ("cap", 384), ("caus", 128), ("iota", 32), ("cosd", 128), ("sind", 128),
                    ("flip", 128), ("fwd", 1024), ("nyq", 256), ("inv", 1024)]:
        CONST[name] = (at, n)
        at += n
    return at


NCONST = _const_layout()


class Recorder:

    def matmul(self, *a, **k):
        CNT[1] += 1
        return lambda e: e.matmul(*a, **k)

    def transpose(self, *a, **k):
        CNT[0] += 1
        return lambda e: e.transpose(*a, **k)

    def activation(self, *a, **k):
        return lambda e: e.activation(*a, **k)

    def tensor_scalar(self, *a, **k):
        return lambda e: e.tensor_scalar(*a, **k)

    def tensor_tensor(self, *a, **k):
        return lambda e: e.tensor_tensor(*a, **k)

    def scalar_tensor_tensor(self, *a, **k):
        return lambda e: e.scalar_tensor_tensor(*a, **k)

    def tensor_copy(self, *a, **k):
        return lambda e: e.tensor_copy(*a, **k)

    def tensor_reduce(self, *a, **k):
        return lambda e: e.tensor_reduce(*a, **k)

    def reciprocal(self, *a, **k):
        return lambda e: e.reciprocal(*a, **k)

    def memset(self, *a, **k):
        return lambda e: e.memset(*a, **k)

    def dma_start(self, *a, **k):
        return lambda e: e.dma_start(*a, **k)

    def max(self, *a, **k):
        return lambda e: e.max(*a, **k)

    def match_replace(self, *a, **k):
        return lambda e: e.match_replace(*a, **k)

    def tensor_tensor_scan(self, *a, **k):
        return lambda e: e.tensor_tensor_scan(*a, **k)

    def bn_stats(self, *a, **k):
        return lambda e: e.bn_stats(*a, **k)

    def bn_aggr(self, *a, **k):
        return lambda e: e.bn_aggr(*a, **k)


REC = Recorder()


class Queue:

    def __init__(self, name, sem):
        self.name, self.sem, self.n, self.items, self.seen = name, sem, 0, [], {}

    def waits(self, after):
        need = {}
        for tok in after:
            if tok is None:
                continue
            s, v = tok
            if self.seen.get(id(s), 0) < v:
                need[id(s)] = (s, max(v, need.get(id(s), (s, 0))[1]))
        for k, (s, v) in need.items():
            self.seen[k] = v
            self.items.append(("w", s, v))

    def __call__(self, fn, *after):
        self.waits(after)
        self.n += 1
        self.items.append(("i", fn(REC), self.sem, 1))
        return (self.sem, self.n)

    def dma(self, fn, sem, *after):
        self.waits(after)
        self.items.append(("i", fn(REC), sem, 16))

    def more(self, fn):
        self.items.append(("m", fn(REC)))


class Buf:

    def __init__(self, ap):
        self.ap, self.free = ap, ()


def build_program(nc, ins, outs, level=99):
    with ExitStack() as ctx:
        _program(nc, ins, outs, ctx, level)


def _program(nc, I, O, ctx, level):
    def sb(name, n, p=128):
        return ctx.enter_context(nc.sbuf_tensor(name, [p, n], F32))

    def sem(name):
        return ctx.enter_context(nc.semaphore(name))

    pe = Queue("pe", sem("s_pe"))
    act = Queue("act", sem("s_act"))
    dve = Queue("dve", sem("s_dve"))
    pool = Queue("pool", sem("s_pool"))
    sp = Queue("sp", None)
    out_sems = []

    ring = [sb(f"ring{i}", SLOT) for i in range(NSLOT)]
    late = [sb(f"late{i}", n) for i, n in enumerate((16 * T, 18 * T, NCONST + 11 * T))]
    xT = sb("xT", 8 * T)
    hT = sb("hT", 8 * T)
    A = late[0]
    V = sb("V", 8 * T)
    G = sb("G", 8 * T)
    U = sb("U", 8 * T)
    S = sb("S", 8 * T)
    CC = late[2][:, 0:NCONST]
    PC = sb("PC", NCOL)
    SPEC = late[1][:, 0:10 * T]
    BB = late[1][:, 10 * T:18 * T]
    R = late[2][:, NCONST:NCONST + 11 * T]
    at = CONST["fwd"][0]
    ring += [late[1][:, 0:SLOT], late[2][:, at:at + SLOT], late[0][:, 0:SLOT]]
    b16 = ctx.enter_context(nc.sbuf_tensor("b16", [128, 256], mybir.dt.bfloat16))
    identb, causb = b16[:, 0:128], b16[:, 128:256]
    mod = sb("mod", 96)
    sm = sb("sm", 256)
    rowg = sb("rowg", 128)
    rw = sb("rw", 128)
    fp = sb("fp", 3, 64)

    banks = [Buf(ctx.enter_context(nc.psum_tensor(f"ps{i}", [128, 512], F32))) for i in range(8)]
    turn = [0]

    rota = [5]

    def bank():
        b = banks[turn[0] % rota[0]]
        turn[0] += 1
        return b

    def c_(name, a=None, b=None):
        at, n = CONST[name]
        return CC[:, at + (a or 0):at + (n if b is None else b)]

    def p_(name, i=0, n=1):
        at, _ = COLS[name]
        return PC[:, at + i:at + i + n]

    def v3(t, c, w=T, at=0):
        return t[:, at:at + c * w].rearrange("p (c t) -> p c t", c=c)

    s_ld = {}

    def load(q, name, dst, src, *after):
        s = sem("s_ld_" + name)
        q.dma(lambda e: e.dma_start(dst, src), s, *after)
        s_ld[name] = (s, 16)
        return s_ld[name]

    xv = I["xT"].rearrange("(c p) t -> p c t", p=128)
    k_xh = [load(act, f"x{i}", v3(xT, 4, at=1024 * i), xv[:, 4 * i:4 * i + 4, :]) for i in range(2)]
    k_on = load(sp, "ones", CC[:, 0:128], I["consts"][:, 0:128])
    k_pc = load(sp, "pc", PC[:, :], I["cols"])

    def mark(name):
        MARKS.append((name, CNT[0], CNT[1]))

    slot_sem = [sem(f"s_ring{i}") for i in range(NSLOT + 3)]
    slot_uses = [0] * (NSLOT + 3)
    slot_free = [()] * (NSLOT + 3)
    order = deque(range(NSLOT))

    def piece(src, c, n):
        i = order.popleft()
        order.append(i)
        dst = ring[i][:, 0:c * n].rearrange("p (c n) -> p c n", c=c)
        sp.dma(lambda e: e.dma_start(dst, src), slot_sem[i], *slot_free[i])
        slot_uses[i] += 1
        return dst, (slot_sem[i], 16 * slot_uses[i]), i

    def done_with(i, *toks):
        slot_free[i] = toks

    def wview(w, a, n):
        return w.rearrange("(c p) n -> p c n", p=128)[:, :, a:a + n]

    mm = lambda e, o, l, r, st, sp_=True, sk=False: e.matmul(o, l, r, start=st, stop=sp_, skip_group_check=sk)

    def rsq(ap, *k):
        act.items.append(("t", "sqrt_and_others"))
        k = act(lambda e: e.activation(ap, ap, ACT.Sqrt), *k)
        act.items.append(("t", "exp_and_others"))
        return dve(lambda e: e.reciprocal(ap, ap), k)

    def rms_T(src, nch, dim, k_src, scale_of, out, bias_of=None, eps=1e-6, scr=None, k_scr=(), nfill=0):
        scr = scr if scr is not None else v3(S, 8)
        b = bank()
        ks = []
        for c in range(nch):
            ks.append(act(lambda e, c=c: e.activation(scr[:, c, :], src(c), ACT.Square),
                          k_src[c], *(k_scr if c == 0 else ())))
        for c in range(nch):
            k = pe(lambda e, c=c: mm(e, b.ap[:, 0:T], c_("nones"), scr[:, c, :], c == 0, c == nch - 1),
                   ks[c], *(b.free if c == 0 else ()), k_on)
        k1 = dve(lambda e: e.tensor_scalar(sm_r, b.ap[:, 0:T], -1.0 / dim, eps, ALU.mult, ALU.add), k, *smr_free[0])
        b.free = (k1,)
        k2 = rsq(sm_r, k1)
        ko = []
        for c in range(nch):
            k3 = dve(lambda e, c=c: e.scalar_tensor_tensor(out(c), src(c), scale_of(c), sm_r, ALU.mult, ALU.mult),
                     k2, k_pc)
            if bias_of is not None:
                k3 = act(lambda e, c=c: e.activation(out(c), out(c), ACT.Identity, bias=bias_of(c)), k3)
            ko.append(k3)
        smr_free[0] = (k3,) if bias_of is None else (ko[-1], (dve.sem, dve.n))
        fill(nfill)
        return tuple(ko), k

    sm_r = R[:, 10 * T:11 * T]
    smr_free = [()]

    def proj_T(W, kW, hsrc, kh, cols, nch, consume):
        for j0 in range(0, len(cols), 2):
            b = bank()
            js = cols[j0:j0 + 2]
            for n, j in enumerate(js):
                for c in range(nch):
                    first = n == 0 and c == 0
                    if c < nch - 1:
                        pe.waits([kW, kh[c]] + (list(b.free) if first else []))
                        pe.more(lambda e, n=n, j=j, c=c: mm(
                            e, b.ap[:, n * T:(n + 1) * T], W[:, c, j:j + 128], hsrc(c), c == 0, False))
                    else:
                        k = pe(lambda e, n=n, j=j, c=c: mm(
                            e, b.ap[:, n * T:(n + 1) * T], W[:, c, j:j + 128], hsrc(c), c == 0, True), kW, kh[c],
                            *(b.free if first else ()))
            b.free = consume(j0, b, k)
        return k

    def proj_tok(W, kW, hsrc, kh, t, a, n, nch, consume, order=None):
        b = bank()
        for c in range(nch):
            f = lambda e, c=c: mm(e, b.ap[:, 0:n], hsrc(c)[:, t * 128:(t + 1) * 128], W[:, c, a:a + n], c == 0, c == nch - 1)
            if c < nch - 1:
                pe.waits([kW, kh[c]] + (list(b.free) if c == 0 else []))
                pe.more(f)
            else:
                k = pe(f, kW, kh[c], *(b.free if c == 0 else ()))
        b.free = consume(b, k)
        return k

    fillers = []

    def fill(n=1):
        for _ in range(n):
            if fillers:
                fillers.pop(0)()

    def gate_T(W, kW, h_, kh, cols, nch, dst, ch0, k_free=()):
        ks = []

        def consume(j0, b, k):
            o = v3(dst, 8)[:, ch0 + j0:ch0 + j0 + 2, :]
            bb = b.ap[:, :].rearrange("p (c t) -> p c t", c=2)
            k1 = act(lambda e: e.activation(o, bb, ACT.Tanh, scale=0.5), k, *k_free)
            k2 = dve(lambda e: e.scalar_tensor_tensor(o, o, 1.0, bb, ALU.add, ALU.mult), k1)
            ks.append(k2)
            return (k2,)
        k = proj_T(W, kW, h_, kh, cols, nch, consume)
        return k, ks

    def out_proj(ws, u, ku, scale_of, k_extra=(), hook=None):
        for half in range(2):
            W, kW, i = ws[half]

            def consume(j0, b, k, half=half):
                kk = None
                for n in range(2):
                    c = half * 4 + j0 + n
                    xc = xT[:, c * T:(c + 1) * T]
                    if scale_of is None:
                        kk = dve(lambda e, n=n, xc=xc: e.tensor_tensor(xc, b.ap[:, n * T:(n + 1) * T], xc, ALU.add), k, *k_extra)
                    else:
                        kk = dve(lambda e, n=n, xc=xc, c=c: e.scalar_tensor_tensor(
                            xc, b.ap[:, n * T:(n + 1) * T], scale_of(c), xc, ALU.mult, ALU.add), k, *k_extra)
                    kx[c] = kk
                return (kk,)
            k = proj_T(W, kW, u, ku, [0, 128, 256, 384], 8, consume)
            done_with(i, k)
            if half == 0 and hook is not None:
                hook()

    def halves(w):
        return [piece(wview(w, half * 512, 512), 8, 512) for half in range(2)]

    def xc(c):
        return xT[:, c * T:(c + 1) * T]

    def hc(c):
        return hT[:, c * T:(c + 1) * T]

    kx = [k_xh[0]] * 4 + [k_xh[1]] * 4
    w = I["l0_w_in"]
    first = [piece(wview(w, a, 256), 8, 256) for a in (0, 256)]
    k_cc = load(sp, "cc", CC[:, 128:], I["consts"][:, 128:])

    sil = BB[:, 1792:2048]
    sil3 = sil[:, :].rearrange("p (c t) -> p c t", c=8)
    s2 = sil3[:, :, 0:2]
    cview = PC[:, COLS["c"][0]:COLS["c"][0] + 16].rearrange("p (c t) -> p c t", c=8)
    k_c0 = dve(lambda e: e.memset(sil[:, :], 0.0))
    k_c = act(lambda e: e.activation(s2, cview, ACT.Tanh, scale=0.5), k_pc, k_c0)
    k_c = dve(lambda e: e.scalar_tensor_tensor(s2, s2, 1.0, cview, ALU.add, ALU.mult), k_c)
    k_c = dve(lambda e: e.tensor_scalar(s2, s2, 0.5, None, ALU.mult), k_c)
    k_mod = {}
    mtmp = Buf(BB[:, 0:512])

    def mod_piece(g, i):
        b = banks[5]

        def run():
            W, kW, slot = piece(I["w_mod_2"][0].rearrange("(c p) n -> p c n", p=128)[:, 2 * i:2 * i + 2, g * 2048:(g + 1) * 2048], 2, 2048)
            pe.waits([k_c, kW, *b.free])
            for c in range(2):
                for q in range(4):
                    f = lambda e: mm(e, b.ap[32 * q:32 * q + 32, :], sil3[:, 2 * i + c, :], W[:, c, q * 512:(q + 1) * 512],
                                     i == 0 and c == 0, i == 3 and c == 1, True)
                    if c == 1 and q == 3:
                        k = pe(f)
                    else:
                        pe.more(f)
            done_with(slot, k)
            if i == 3:
                k1 = act(lambda e: e.activation(mtmp.ap, b.ap[:, :], ACT.Copy), k, *mtmp.free, *k_spec)
                for j in range(4):
                    k2 = pe(lambda e: e.transpose(b.ap[:, j * 128:(j + 1) * 128], mtmp.ap[:, j * 128:(j + 1) * 128], c_("ident")), k1)
                mtmp.free = (k2,)
                src = b.ap[:, :].rearrange("p (j q r) -> p q j r", j=4, q=4)[:, :, :, 0:2]
                dst = mod[:, 32 * g:32 * g + 32].rearrange("p (q j r) -> p q j r", q=4, j=4)
                bm = PC[:, COLS["b_mod"][0] + 16 * g:COLS["b_mod"][0] + 16 * g + 16].rearrange("p (q j) -> p q j", q=4)
                for r_ in range(2):
                    k3 = dve(lambda e: e.tensor_tensor(dst[:, :, :, r_], src[:, :, :, r_], bm, ALU.add), k2, k_pc)
                b.free = (k3,)
                k_mod[g] = k3
        return run

    for g in range(3):
        for i in range(4):
            fillers.append(mod_piece(g, i))

    def m_(group, c, ctx_=0):
        j = (group * 8 + c) * 2 + ctx_
        return mod[:, j:j + 1]

    def hyena_filters():
        w3 = U[0:64, 0:1024]
        w2 = U[0:64, 1024:1088]
        w1 = U[0:33, 1088:1152]
        zf = U[0:33, 1152:1408]
        kw3 = load(sp, "w3", w3, I["hy_filt_w3_2"][0])
        kw2 = load(sp, "w2", w2, I["hy_filt_w2_2"][0])
        kw1 = load(sp, "w1", w1, I["hy_filt_w1_2"][0])
        kz = load(sp, "zf", zf, I["zfeat"])
        kd = load(sp, "dec", BB[:, 0:1024], I["decay"])
        kfp = load(sp, "fp", fp[:, :], I["filtp"])
        u = BB[0:64, 1024:1280]
        kk = BB[0:64, 1280:1536]
        h = BB[0:64, 1536:1792]

        def sine(b, k, bias):
            k = dve(lambda e: e.tensor_scalar(u, b.ap[0:64, 0:T], fp[:, bias:bias + 1], fp[:, 1:2], ALU.add, ALU.mult), k, kfp)
            b.free = (k,)
            k = dve(lambda e: e.tensor_scalar(kk, u, 1.0 / TWO_PI, MAGIC, ALU.mult, ALU.add), k)
            k = dve(lambda e: e.tensor_scalar(kk, kk, MAGIC, None, ALU.subtract), k)
            c1 = 6.28125
            c2 = float(np.float32(np.round((TWO_PI - c1) * 2 ** 20) / 2 ** 20))
            c3 = TWO_PI - c1 - c2
            for cst in (c1, c2, c3):
                k = dve(lambda e, cst=cst: e.scalar_tensor_tensor(u, kk, -cst, u, ALU.mult, ALU.add), k)
            lim = 3.1415925
            k = dve(lambda e: e.tensor_scalar(u, u, lim, -lim, ALU.min, ALU.max), k)
            return act(lambda e: e.activation(h, u, ACT.Sin), k)
        b = bank()
        k = pe(lambda e: mm(e, b.ap[0:64, 0:T], w1, zf, True), kw1, kz, *b.free)
        yield
        k = sine(b, k, 0)
        yield
        b = bank()
        k = pe(lambda e: mm(e, b.ap[0:64, 0:T], w2, h, True), kw2, k, *b.free)
        yield
        k = sine(b, k, 2)
        yield
        summ = v3(S, 2, 512)
        diff = v3(S, 2, 512, at=1024)
        ks = []
        for t in range(2):
            bf, bb = bank(), bank()
            k1 = pe(lambda e: mm(e, bf.ap[:, :], h[:, t * 128:(t + 1) * 128], w3[:, 0:512], True), k, kw3, *bf.free)
            k2 = pe(lambda e: mm(e, bb.ap[:, :], h[:, t * 128:(t + 1) * 128], w3[:, 512:1024], True), *bb.free)
            dcf = BB[:, t * 512:t * 512 + 256].unsqueeze(1).broadcast_to([128, 2, 256])
            dcb = BB[:, t * 512 + 256:t * 512 + 512].unsqueeze(1).broadcast_to([128, 2, 256])
            o2 = lambda a: a.rearrange("p (o c) -> p o c", o=2)
            tmp = U[:, 1408:1920]
            k3 = dve(lambda e: e.tensor_tensor(o2(summ[:, t, :]), o2(bf.ap[:, :]), dcf, ALU.mult), k1, kd)
            k4 = dve(lambda e: e.tensor_tensor(o2(tmp), o2(bb.ap[:, :]), dcb, ALU.mult), k2, *(ks[-1:]))
            bf.free, bb.free = (k3,), (k4,)
            k5 = dve(lambda e: e.tensor_tensor(diff[:, t, :], summ[:, t, :], tmp, ALU.subtract), k3, k4)
            k6 = dve(lambda e: e.tensor_tensor(summ[:, t, :], summ[:, t, :], tmp, ALU.add), k5)
            ks.append(k6)
            yield
        fw = v3(CC, 2, 512, at=CONST["fwd"][0])
        ny = v3(CC, 2, 128, at=CONST["nyq"][0])
        KA, KB, KC = v3(SPEC, 2, 512), v3(SPEC, 2, 512, at=1024), v3(SPEC, 1, 512, at=2048)
        last = []
        for dst, rhs, lhs in [(KA[:, 0, :], summ, lambda t: fw[:, t, 0:128]), (KA[:, 1, :], summ, lambda t: fw[:, t, 128:256]),
                              (KB[:, 0, :], diff, lambda t: kb0(t)), (KB[:, 1, :], diff, lambda t: fw[:, t, 384:512]),
                              (KC[:, 0, :], summ, lambda t: ny[:, t, :])]:
            b = bank()
            for t in range(2):
                k = pe(lambda e, t=t, rhs=rhs, lhs=lhs, b=b: mm(e, b.ap[:, :], lhs(t), rhs[:, t, :], t == 0, t == 1), ks[t], k_cc,
                       *(b.free if t == 0 else ()))
            k = act(lambda e, dst=dst, b=b: e.activation(dst, b.ap[:, :], ACT.Copy), k)
            b.free = (k,)
            last.append(k)
            yield
        kz0 = pool(lambda e: e.memset(KB[0:1, 0, :], 0.0), last[2])
        k_spec.extend([kz0, *last])

    def kb0(t):
        return v3(CC, 2, 512, at=CONST["fwd"][0])[:, t, 256:384]

    k_spec = []
    kh, _ = rms_T(xc, 8, D, kx, lambda c: p_("l0_norm", c), hc, scr=v3(A, 8))
    hy_steps = hyena_filters()

    mark("l0")
    w = I["l0_w_in"]
    kq = {}
    qk = v3(A, 16)
    for grp, (a, sc) in enumerate(((0, 0.125), (1024, 1.0))):
        for half in range(2):
            ws = first if grp == half == 0 else [piece(wview(w, a + half * 512, 512), 8, 512)]

            def consume(j0, b, k, grp=grp, half=half, sc=sc):
                ch = grp * 8 + half * 4 + j0
                o = A[:, ch * T:(ch + 2) * T]
                k2 = act(lambda e: e.activation(o, b.ap[:, :], ACT.Copy, scale=sc), k)
                kq[ch] = kq[ch + 1] = k2
                return (k2,)
            for j, (W, kW, i) in enumerate(ws):
                k = proj_T(W, kW, hc, kh, [0, 128, 256, 384][:W.shape[2] // 128], 8,
                           consume if j == 0 else lambda j0, b, k: consume(j0 + 2, b, k))
                done_with(i, k)
            next(hy_steps, None)
            next(hy_steps, None)
    kv = {}
    for half in range(2):
        W, kW, i = piece(wview(w, 2048 + half * 512, 512), 8, 512)
        for t in range(2):
            def consume(b, k, t=t, half=half):
                k2 = dve(lambda e: e.tensor_copy(V[:, t * 1024 + half * 512:t * 1024 + half * 512 + 512], b.ap[:, :]), k)
                kv[(t, half)] = k2
                return (k2,)
            k = proj_tok(W, kW, hc, kh, t, 0, 512, 8, consume)
        done_with(i, k)
    kg = []
    for half in range(2):
        W, kW, i = piece(wview(w, 3072 + half * 512, 512), 8, 512)
        k, ks = gate_T(W, kW, hc, kh, [0, 128, 256, 384], 8, G, half * 4)
        kg += ks
        done_with(i, k)

    for _ in hy_steps:
        pass
    act.items.append(("t", "natural_log_exp_and_others"))
    k_hdone = (pe.sem, pe.n)

    def sb_attention():
        e1 = [Buf(R[:, i * 384:(i + 1) * 384]) for i in range(4)]
        Lb = [Buf(hT[:, i * 384:(i + 1) * 384]) for i in range(4)]
        for x_ in Lb:
            x_.free = (k_hdone,)
        abuf = [Buf(S[:, i * 384:(i + 1) * 384]) for i in range(4)]
        st = {}

        def stage_z(h0):
            bs = {}
            for h in (h0, h0 + 1):
                bs[h] = bank()
                pe.waits([kq[h // 2], kq[8 + h // 2], *bs[h].free])
            q = {h: A[64 * (h % 2):64 * (h % 2) + 64, (h // 2) * T:(h // 2 + 1) * T] for h in bs}
            k_ = {h: A[64 * (h % 2):64 * (h % 2) + 64, (8 + h // 2) * T:(9 + h // 2) * T] for h in bs}
            for h in bs:
                pe.more(lambda e: mm(e, bs[h].ap[:, 0:256], k_[h][:, 0:128], q[h], True, True, True))
            for h in bs:
                k = pe(lambda e: mm(e, bs[h].ap[:, 256:384], k_[h][:, 128:256], q[h][:, 128:256], False, True, True))
            for h in bs:
                b = bs[h]
                e_, L = e1[h % 4], Lb[h % 4]
                k0 = dve(lambda e: e.tensor_scalar(L.ap, b.ap[:, 0:384], 0.0, None, ALU.max), k, *L.free)
                k1 = dve(lambda e: e.scalar_tensor_tensor(e_.ap, b.ap[:, 0:384], 0.0, L.ap, ALU.min, ALU.subtract), k0, *e_.free)
                k2 = act(lambda e: e.activation(e_.ap, e_.ap, ACT.Exp), k1)
                k3 = act(lambda e: e.activation(e_.ap, e_.ap, ACT.Ln, bias=1.0), k2)
                k4 = pool(lambda e: e.tensor_tensor(L.ap, L.ap, e_.ap, ALU.add), k3)
                e_.free = (k4,)
                k6 = None
                for a in (0, 256):
                    k6 = pool(lambda e, a=a: e.tensor_tensor(L.ap[:, a:a + 128], L.ap[:, a:a + 128], c_("m01"), ALU.mult), k4, k_cc)
                st[h] = (b, L, k6, k4)

        def stage_c(h):
            b, L, k6, k4 = st[h]
            pe.waits([k6, k4])
            pe.more(lambda e: mm(e, b.ap[:, 0:256], c_("ntri"), L.ap[:, 0:256], False, True, True))
            pe.more(lambda e: mm(e, b.ap[:, 128:256], c_("nones"), L.ap[:, 256:384], False, True, True))
            k = pe(lambda e: mm(e, b.ap[:, 256:384], c_("ntri"), L.ap[:, 256:384], False, True, True))
            L.free = (k,)
            a = abuf[h % 4]
            a.free = a.free or tuple(k_spec)
            k1 = dve(lambda e: e.tensor_tensor(a.ap, b.ap[:, 0:384], c_("cap"), ALU.min), k, *a.free)
            b.free = (k1,)
            k2 = act(lambda e: e.activation(a.ap, a.ap, ACT.Exp), k1)
            st[h] = (a, k2)

        ku = []

        def stage_o(h0):
            b = banks[6 + (h0 // 2) % 2]
            av = {h: st.pop(h) for h in (h0, h0 + 1)}
            for h in av:
                pe.waits([av[h][1], *b.free, kv[(0, h // 8)], kv[(1, h // 8)]])
            for h in av:
                o = b.ap[64 * (h % 2):64 * (h % 2) + 64, 0:256]
                pe.more(lambda e: mm(e, o, V[:, h * 64:h * 64 + 64], av[h][0].ap[:, 0:256], True, True, True))
            for h in av:
                o = b.ap[64 * (h % 2):64 * (h % 2) + 64, 128:256]
                k = pe(lambda e: mm(e, o, V[:, 1024 + h * 64:1088 + h * 64], av[h][0].ap[:, 256:384], False, True, True))
            for h in av:
                av[h][0].free = (k,)
            c = h0 // 2
            k3 = dve(lambda e: e.scalar_tensor_tensor(U[:, c * T:(c + 1) * T], b.ap[:, 0:256], 0.5,
                                                      G[:, c * T:(c + 1) * T], ALU.mult, ALU.mult), k, kg[c // 2], *k_spec)
            b.free = (k3,)
            ku.append(k3)

        for i in range(8 + 2):
            if i < 8:
                stage_z(2 * i)
            if i in (0, 8):
                fill()
            if 0 <= i - 1 < 8:
                stage_c(2 * i - 2)
                stage_c(2 * i - 1)
            if 0 <= i - 2 < 8:
                stage_o(2 * i - 4)
        return ku

    mark("l0attn")
    ku = sb_attention()
    mark("l0out")
    out_proj(halves(I["l0_w_out"]), lambda c: U[:, c * T:(c + 1) * T], ku, None)
    if level == 1:
        return finish(nc, locals())

    mark("l1")
    kh, _ = rms_T(xc, 8, D, kx, lambda c: p_("l1_norm", c), hc, nfill=2)
    k_b16 = act(lambda e: e.activation(causb, c_("caus"), ACT.Copy), act(lambda e: e.activation(identb, c_("ident"), ACT.Copy), k_cc))
    k_rowg = load(sp, "rowg", rowg[:, :], I["rowg"].broadcast_to([128, 128]))
    w = I["l1_w_in"]
    W, kW, i = piece(wview(w, 0, 448), 8, 448)
    lat = [S[:, 0:448], S[:, 448:896]]
    klat = []
    for t in range(2):
        def consume(b, k, t=t):
            k2 = act(lambda e: e.activation(lat[t], b.ap[:, 0:448], ACT.Copy), k, kh[-1])
            klat.append(k2)
            return (k2,)
        k = proj_tok(W, kW, hc, kh, t, 0, 448, 8, consume)
    done_with(i, k)
    sq = S[:, 1024:1472]
    st_ = sm[:, 32:64]
    latT = v3(S, 3, T, at=1472 - 192)
    latT = v3(R, 3, T)
    klt = []
    k_prev = None
    stat_k = []
    for t in range(2):
        k = act(lambda e, t=t: e.activation(sq[:, 0:256], lat[t][:, 0:256], ACT.Square, accum_out=sm[:, 32 + 4 * t:33 + 4 * t]), klat[t])
        k = act(lambda e, t=t: e.activation(sq[:, 256:384], lat[t][:, 256:384], ACT.Square, accum_out=sm[:, 33 + 4 * t:34 + 4 * t]), k)
        k = act(lambda e, t=t: e.activation(sq[:, 384:448], lat[t][:, 384:448], ACT.Square, accum_out=sm[:, 34 + 4 * t:35 + 4 * t]), k)
        ka = dve(lambda e, t=t: e.tensor_scalar(sm[:, 40 + 4 * t:41 + 4 * t], sm[:, 32 + 4 * t:33 + 4 * t], 1.0 / 256, 1e-6, ALU.mult, ALU.add), k)
        kb = dve(lambda e, t=t: e.tensor_scalar(sm[:, 41 + 4 * t:42 + 4 * t], sm[:, 33 + 4 * t:34 + 4 * t], 1.0 / 128, 1e-6, ALU.mult, ALU.add), k)
        k2 = rsq(sm[:, 40 + 4 * t:42 + 4 * t], ka, kb)
        ka = dve(lambda e, t=t: e.tensor_scalar(lat[t][:, 0:256], lat[t][:, 0:256], sm[:, 40 + 4 * t:41 + 4 * t], None, ALU.mult), k2)
        kb = dve(lambda e, t=t: e.tensor_scalar(lat[t][:, 256:384], lat[t][:, 256:384], sm[:, 41 + 4 * t:42 + 4 * t], None, ALU.mult), k2)
        stat_k.append((ka, kb))
    kg = []

    def gate(half):
        W, kW, i = piece(wview(w, 448 + half * 512, 512), 8, 512)
        k, ks = gate_T(W, kW, hc, kh, [0, 128, 256, 384], 8, G, half * 4)
        kg.extend(ks)
        done_with(i, k)
    gate(0)
    bq, bk = bank(), bank()
    for t in range(2):
        for j in range(3):
            b, o = (bq, j * T) if j < 2 else (bk, 0)
            k = pe(lambda e, t=t, j=j, b=b, o=o: e.transpose(b.ap[:, o + t * 128:o + t * 128 + 128], lat[t][:, j * 128:(j + 1) * 128], c_("ident")),
                   *stat_k[t], *(b.free if t == 0 else ()))
    klq = []
    for j in range(3):
        b, o = (bq, j * T) if j < 2 else (bk, 0)
        g = p_("q_a", j) if j < 2 else p_("kv_a")
        klq.append(dve(lambda e, j=j, b=b, o=o, g=g: e.tensor_scalar(latT[:, j, :], b.ap[:, o:o + T], g, None, ALU.mult), k))
    bq.free = bk.free = (klq[-1],)

    mark("l1q")
    Wq, kWq, iq = piece(I["l1_w_uq"].rearrange("(c p) n -> p c n", p=128), 2, 1536)
    qnT, knT = v3(A, 8), v3(A, 8, T, at=8 * T)
    qrT = v3(hT, 4)
    krT = v3(hT, 4, T, at=4 * T)
    qt = [S[:, 0:1536], U[:, 0:1536]]
    kt = [SCK[0], SCK[1]] if False else None
    ssq = sm[:, 64:96]
    kss = {}
    pe_rope = R[:, 3 * T:3 * T + 128]
    t1 = R[:, 4 * T:4 * T + 64]
    cosd = lambda t: c_("cosd", 64 * t, 64 * t + 64)
    sind = lambda t: c_("sind", 64 * t, 64 * t + 64)
    kpe = []
    for t in range(2):
        x_ = lat[t][:, 384:448]
        o = pe_rope[:, 64 * t:64 * t + 64]
        k = dve(lambda e, x_=x_: e.tensor_tensor(x_, x_, rowg[:, 64:128], ALU.mult), klat[t], k_rowg, stat_k[t][0])
        ka = dve(lambda e, t=t, x_=x_, o=o: e.tensor_tensor(o, x_, cosd(t), ALU.mult), k)
        kb = dve(lambda e, t=t, x_=x_: e.tensor_tensor(t1[:, 0:32], x_[:, 32:64], sind(t)[:, 0:32], ALU.mult), k, *kpe[-1:])
        kc = dve(lambda e, t=t, x_=x_: e.tensor_tensor(t1[:, 32:64], x_[:, 0:32], sind(t)[:, 32:64], ALU.mult), k)
        kpe.append(dve(lambda e, o=o: e.tensor_tensor(o, o, t1, ALU.add), ka, kb, kc))

    qn = {}
    sqb = [Buf(R[:, 5 * T:5 * T + 512]), Buf(R[:, 7 * T:7 * T + 512])]
    nsq = [0]
    hq = lambda c: latT[:, c, :]
    k_qt = {}
    for t in range(2):
        for g in range(4):
            def consume(b, k, t=t, g=g):
                o = qt[t][:, g * 384:(g + 1) * 384]
                s = sqb[nsq[0] % 2]
                nsq[0] += 1
                k1 = act(lambda e: e.activation(o, b.ap[:, 0:384], ACT.Copy), k, kpe[0], kpe[1], klq[2])
                k2 = act(lambda e: e.activation(s.ap[:, 0:384], b.ap[:, 0:384], ACT.Square), k, *s.free)
                k3 = dve(lambda e: e.tensor_reduce(ssq[:, t * 8 + 2 * g:t * 8 + 2 * g + 2],
                                                   s.ap[:, 0:384].rearrange("p (h d) -> p h d", h=2), AX.X, ALU.add), k2)
                s.free = (k3,)
                k_qt[(t, g)] = (k1, k3)
                return (k1, k2)
            k = proj_tok(Wq, kWq, hq, klq, t, g * 384, 384, 2, consume)
    done_with(iq, k)
    kqr = []
    tq = R[:, 3 * T + 128:3 * T + 128]
    for t in range(2):
        qv = qt[t].rearrange("p (h d) -> p h d", h=8)[:, :, 128:192]
        tmp = R[:, 5 * T:5 * T + 512].rearrange("p (h d) -> p h d", h=8)
        tm2 = R[:, 7 * T:7 * T + 512].rearrange("p (h d) -> p h d", h=8)
        rg = rowg[:, 0:64].unsqueeze(1).broadcast_to([128, 8, 64])
        cb_ = cosd(t).unsqueeze(1).broadcast_to([128, 8, 64])
        sb_ = lambda a, b, t=t: sind(t)[:, a:b].unsqueeze(1).broadcast_to([128, 8, 32])
        dep = [x for g in range(4) for x in k_qt[(t, g)]] + [x for s in sqb for x in s.free]
        k = dve(lambda e, qv=qv, tmp=tmp, rg=rg: e.tensor_tensor(tmp, qv, rg, ALU.mult), *dep, *kqr[-1:])
        ka = dve(lambda e, tm2=tm2, tmp=tmp, sb_=sb_: e.tensor_tensor(tm2[:, :, 0:32], tmp[:, :, 32:64], sb_(0, 32), ALU.mult), k, *kqr[-1:])
        kb = dve(lambda e, tm2=tm2, tmp=tmp, sb_=sb_: e.tensor_tensor(tm2[:, :, 32:64], tmp[:, :, 0:32], sb_(32, 64), ALU.mult), k)
        kc = dve(lambda e, tmp=tmp, cb_=cb_: e.tensor_tensor(tmp, tmp, cb_, ALU.mult), ka, kb)
        kqr.append(dve(lambda e, qv=qv, tmp=tmp, tm2=tm2: e.tensor_tensor(qv, tmp, tm2, ALU.add), kc, ka, kb))
    for s in sqb:
        s.free = (kqr[-1],)
    scq = sm[:, 96:112]
    k = dve(lambda e: e.tensor_scalar(scq, ssq[:, 0:16], 1.0 / 192, 1e-6, ALU.mult, ALU.add), k_qt[(1, 3)][1], k_qt[(0, 3)][1])
    k = rsq(scq, k)
    k_scq = dve(lambda e: e.tensor_scalar(scq, scq, 192.0 ** -0.5, None, ALU.mult), k)
    gate(1)
    Wk, kWk, ik = piece(I["l1_w_ukv"].unsqueeze(1), 1, 2048)

    k_kh = kh
    k_qnT, k_qrT = {}, {}
    for hp in range(4):
        b = bank()
        for n in range(4):
            h, t = 2 * hp + n // 2, n % 2
            k = pe(lambda e, n=n, h=h, t=t, b=b: e.transpose(b.ap[:, n * 128:(n + 1) * 128], qt[t][:, h * 192:h * 192 + 128], c_("ident")),
                   k_qt[(t, h // 2)][0], *(b.free if n == 0 else ()))
        k = act(lambda e, hp=hp, b=b: e.activation(A[:, 2 * hp * T:(2 * hp + 2) * T], b.ap[:, :], ACT.Copy, scale=p_("gq")), k)
        b.free = (k,)
        k_qnT[hp] = k
    qr2 = R[:, 5 * T:5 * T + 512]
    for t in range(2):
        qv = qt[t].rearrange("p (h d) -> p h d", h=8)[:, :, 128:192]
        kcp = pool(lambda e, qv=qv: e.tensor_copy(qr2.rearrange("p (h d) -> p h d", h=8), qv), kqr[t], *( [k_qrT[(0, 1)]] if t else [kqr[1]]))
        b = bank()
        for n in range(4):
            k = pe(lambda e, n=n, b=b: e.transpose(b.ap[:, n * 128:(n + 1) * 128], qr2[:, n * 128:(n + 1) * 128], c_("ident")), kcp, *(b.free if n == 0 else ()))
        kk = dve(lambda e, b=b, t=t: e.tensor_copy(qrT[:, :, t * 128:(t + 1) * 128], b.ap[:, :].rearrange("p (c t) -> p c t", c=4)), k, (pe.sem, pe.n))
        b.free = (kk,)
        k_qrT[(t, 0)] = kk
        k_qrT[(0, 1)] = k
    k_r2 = k
    ktk = [S[:, 0:1024], U[:, 0:1024]]
    ssk = sm[:, 80:96]
    k_kt = {}
    kvv = {}
    trans_done = (pe.sem, pe.n)
    for t in range(2):
        for g in range(4):
            def consume(b, k, t=t, g=g):
                bb = b.ap[:, :].rearrange("p (h d) -> p h d", h=2)
                o = ktk[t][:, g * 256:(g + 1) * 256].rearrange("p (h d) -> p h d", h=2)
                vv = V[:, t * 1024 + g * 256:t * 1024 + (g + 1) * 256].rearrange("p (h d) -> p h d", h=2)
                s = sqb[nsq[0] % 2]
                nsq[0] += 1
                k1 = act(lambda e: e.activation(o, bb[:, :, 0:128], ACT.Copy), k, trans_done, *kqr)
                k2 = act(lambda e: e.activation(s.ap[:, 0:256].rearrange("p (h d) -> p h d", h=2), bb[:, :, 0:128], ACT.Square), k, *s.free, k_r2)
                k3 = dve(lambda e: e.tensor_reduce(ssk[:, t * 8 + 2 * g:t * 8 + 2 * g + 2],
                                                   s.ap[:, 0:256].rearrange("p (h d) -> p h d", h=2), AX.X, ALU.add), k2)
                k4 = dve(lambda e: e.tensor_copy(vv, bb[:, :, 128:256]), k)
                s.free = (k3,)
                k_kt[(t, g)] = (k1, k3)
                kvv[(t, g)] = k4
                return (k1, k2, k4)
            k = proj_tok(Wk, kWk, lambda c: latT[:, 2, :], [klq[2]], t, g * 512, 512, 1, consume)
    done_with(ik, k)
    fill(2)
    rk = sm[:, 112:128]
    k_knT = {}
    krb = [R[:, 5 * T:5 * T + 512], R[:, 7 * T:7 * T + 512]]
    knorm, krd = [], []
    for t in range(2):
        k = dve(lambda e: e.tensor_scalar(rk[:, 8 * t:8 * t + 8], ssk[:, 8 * t:8 * t + 8], sm[:, 34 + 4 * t:35 + 4 * t], 1.0 / 192, ALU.add, ALU.mult), k_kt[(t, 3)][1])
    k = dve(lambda e: e.tensor_scalar(rk, rk, 1e-6, None, ALU.add), k)
    k_rk = rsq(rk, k)
    for t in range(2):
        kr3 = krb[t].rearrange("p (h d) -> p h d", h=8)
        pr = pe_rope[:, 64 * t:64 * t + 64].unsqueeze(1).broadcast_to([128, 8, 64])
        rb = rk[:, 8 * t:8 * t + 8].unsqueeze(2)
        krd.append(dve(lambda e: e.tensor_tensor(kr3, pr, rb.broadcast_to([128, 8, 64]), ALU.mult), k_rk, k_r2, kpe[t],
                       *[x for s in sqb for x in s.free]))
    for t in range(2):
        kt3 = ktk[t].rearrange("p (h d) -> p h d", h=8)
        rb = rk[:, 8 * t:8 * t + 8].unsqueeze(2)
        knorm.append(dve(lambda e: e.tensor_tensor(kt3, kt3, rb.broadcast_to([128, 8, 128]), ALU.mult), k_rk, *[k_kt[(t, g)][0] for g in range(4)]))
    for t in range(2):
        b = bank()
        for n in range(4):
            k = pe(lambda e: e.transpose(b.ap[:, n * 128:(n + 1) * 128], krb[t][:, n * 128:(n + 1) * 128], c_("ident")), krd[t], *(b.free if n == 0 else ()))
        kk = act(lambda e: e.activation(krT[:, :, t * 128:(t + 1) * 128], b.ap[:, :].rearrange("p (c t) -> p c t", c=4), ACT.Copy), k)
        b.free = (kk,)
        k_knT[("r", t)] = kk
    for hp in range(4):
        b = bank()
        for n in range(4):
            h, t = 2 * hp + n // 2, n % 2
            k = pe(lambda e, n=n, h=h, t=t, b=b: e.transpose(b.ap[:, n * 128:(n + 1) * 128], ktk[t][:, h * 128:h * 128 + 128], c_("ident")),
                   knorm[t], *(b.free if n == 0 else ()))
        k = act(lambda e, hp=hp, b=b: e.activation(A[:, (8 + 2 * hp) * T:(8 + 2 * hp + 2) * T], b.ap[:, :], ACT.Copy, scale=p_("gk")), k)
        b.free = (k,)
        k_knT[hp] = k
    k_alltr = (pe.sem, pe.n)

    def mla_attention():
        pb = [Buf(S[:, i * 384:(i + 1) * 384]) for i in range(3)]
        pt = [Buf(R[:, 5 * T + i * 384:5 * T + (i + 1) * 384]) for i in range(3)]
        for x_ in pb + pt:
            x_.free = (k_alltr,)
        st = {}
        ku = []
        s8 = lambda h, j: sm[:, 128 + (h % 4) * 8 + j:129 + (h % 4) * 8 + j]
        r0 = [k_b16, klq[2], k_qrT[(0, 0)], k_qrT[(1, 0)], k_knT[("r", 0)], k_knT[("r", 1)]]

        def stage_s(h):
            b = bank()
            p0 = 64 * (h % 2)
            q, k_ = qnT[:, h, :], knT[:, h, :]
            qr = hT[p0:p0 + 64, (h // 2) * T:(h // 2 + 1) * T]
            kr = hT[p0:p0 + 64, (4 + h // 2) * T:(5 + h // 2) * T]
            pe.waits([k_qnT[h // 2], k_knT[h // 2], *r0, *b.free])
            add = lambda f: pe.more(f)
            add(lambda e: mm(e, b.ap[:, 0:128], q[:, 0:128], k_[:, 0:128], True, True, True))
            add(lambda e: mm(e, b.ap[:, 128:384], q[:, 128:256], k_[:, 0:256], False, True, True))
            add(lambda e: mm(e, b.ap[:, 0:128], identb, causb, False, True, True))
            add(lambda e: mm(e, b.ap[:, 256:384], identb, causb, False, True, True))
            add(lambda e: mm(e, b.ap[:, 0:128], qr[:, 0:128], kr[:, 0:128], False, True, True))
            k = pe(lambda e: mm(e, b.ap[:, 128:384], qr[:, 128:256], kr[:, 0:256], False, True, True))
            p = pb[h % 3]
            rng = [(0, 128), (128, 384)]
            ke = []
            for t in range(2):
                a, z = rng[t]
                k1 = dve(lambda e, a=a, z=z, t=t: e.tensor_reduce(s8(h, t), b.ap[:, a:z], AX.X, ALU.max), k, *st.get(("s", h - 4), ()))
                k2 = dve(lambda e, t=t: e.tensor_scalar(s8(h, 2 + t), s8(h, t), scq[:, 8 * t + h:8 * t + h + 1], -1.0, ALU.mult, ALU.mult), k1, k_scq)
                k3 = act(lambda e, a=a, z=z, t=t: e.activation(p.ap[:, a:z], b.ap[:, a:z], ACT.Exp, bias=s8(h, 2 + t),
                                                               scale=scq[:, 8 * t + h:8 * t + h + 1], accum_out=s8(h, 4 + t)), k2, *p.free)
                k4 = dve(lambda e, t=t: e.reciprocal(s8(h, 6 + t), s8(h, 4 + t)), k3)
                k5 = dve(lambda e, a=a, z=z, t=t: e.tensor_scalar(p.ap[:, a:z], p.ap[:, a:z], s8(h, 6 + t), None, ALU.mult), k4)
                ke.append(k5)
            b.free = (k3,)
            st[("s", h)] = (k5,)
            st[h] = (p, ke)

        def stage_t(h):
            p, ke = st[h]
            b = bank()
            pe.waits([*ke, *b.free])
            pe.more(lambda e: e.transpose(b.ap[:, 0:128], p.ap[:, 0:128], c_("ident")))
            pe.more(lambda e: e.transpose(b.ap[:, 128:256], p.ap[:, 128:256], c_("ident")))
            k = pe(lambda e: e.transpose(b.ap[:, 256:384], p.ap[:, 256:384], c_("ident")))
            p.free = (k,)
            q = pt[h % 3]
            k2 = act(lambda e: e.activation(q.ap, b.ap[:, 0:384], ACT.Copy), k, *q.free)
            b.free = (k2,)
            st[h] = (q, k2)

        def stage_o(h):
            q, k2 = st.pop(h)
            b = bank()
            pe.waits([k2, *b.free, kvv[(0, h // 2)], kvv[(1, h // 2)]])
            pe.more(lambda e: mm(e, b.ap[:, 0:256], V[:, h * 128:(h + 1) * 128], q.ap[:, 0:256], True, True, True))
            k = pe(lambda e: mm(e, b.ap[:, 128:256], V[:, 1024 + h * 128:1024 + (h + 1) * 128], q.ap[:, 256:384], False, True, True))
            q.free = (k,)
            k3 = dve(lambda e: e.scalar_tensor_tensor(U[:, h * T:(h + 1) * T], b.ap[:, 0:256], 0.5, G[:, h * T:(h + 1) * T], ALU.mult, ALU.mult),
                     k, kg[h // 2], k_alltr)
            b.free = (k3,)
            ku.append(k3)
        for i in range(8 + 3):
            if i < 8:
                stage_s(i)
            if i in (0, 1, 8):
                fill()
            if 0 <= i - 2 < 8:
                stage_t(i - 2)
            if 0 <= i - 3 < 8:
                stage_o(i - 3)
        return ku

    mark("mla")
    ku = mla_attention()
    ws = halves(I["l1_w_out"])
    k_s = (act.sem, act.n), (dve.sem, dve.n), (pe.sem, pe.n)
    k_ctx = load(sp, "ctx", v3(S, 8), I["ctxT"].rearrange("(c p) t -> p c t", p=128), *k_s)
    k_wm = load(sp, "wm", A[:, 15 * T:16 * T], I["wmask"], *k_s)
    k_rw = load(sp, "rw", rw[:, :].rearrange("p (c e) -> p c e", c=8), I["router_w_2"][0].rearrange("(c p) e -> p c e", p=128))
    wmask = A[:, 15 * T:16 * T]
    gs = sm[:, 192:216]
    modv = mod[:, :].rearrange("p (g c t) -> p g c t", g=6, t=2)

    def gain(j, group, col, name):
        return dve(lambda e: e.scalar_tensor_tensor(gs[:, 8 * j:8 * j + 8], modv[:, group, :, col], 1.0, p_(name, 0, 8),
                                                    ALU.add, ALU.mult), k_pc, k_mod[group // 2])

    def sc_(c):
        return S[:, c * T:(c + 1) * T]

    state = {}

    def ctx_norm():
        fill(max(0, len(fillers) - 8))
        kg_ = [gain(0, 1, 0, "norm1"), gain(1, 1, 1, "norm1")]
        state["gain"] = kg_
        state["khc"], _ = rms_T(sc_, 8, D, [k_ctx] * 8, lambda c: gs[:, 8 + c:9 + c], sc_, lambda c: m_(0, c, 1),
                                scr=v3(A, 8), k_scr=k_s)

    mark("l1out")
    out_proj(ws, lambda c: U[:, c * T:(c + 1) * T], ku, None, hook=ctx_norm)
    if level == 2:
        return finish(nc, locals())
    khc = state["khc"]
    k_old = (pe.sem, pe.n)
    kh, _ = rms_T(xc, 8, D, kx, lambda c: gs[:, c:c + 1], hc, lambda c: m_(0, c), scr=v3(A, 8), k_scr=(k_old, *khc), nfill=12)
    k_gain = gain(2, 4, 0, "norm2")
    k_mods = (pe.sem, pe.n)
    w = I["w_in_2"][0]

    mark("l2")
    HU = G[:, 0:6 * 258].rearrange("p (c t) -> p c t", c=6)
    CF = A[:, 12 * T:12 * T + 572].rearrange("p (c t) -> p c t", c=2)
    CT = v3(R, 6)
    cy = v3(R, 2, T, at=6 * T)
    kz1 = pool(lambda e: e.memset(HU[:, :, 0:1], 0.0), k_old)
    kz1 = pool(lambda e: e.memset(HU[:, :, 257:258], 0.0), k_old)
    kz2 = pool(lambda e: e.memset(CF[:, :, 0:15], 0.0), k_old)
    kz2 = pool(lambda e: e.memset(CF[:, :, 271:286], 0.0), k_old)
    k_hu, k_cf = {}, []
    aglu = {}

    def consume_mix(ch, b, k):
        bb = b.ap[:, :].rearrange("p (c t) -> p c t", c=2)
        if ch < 6:
            k2 = act(lambda e: e.activation(HU[:, ch:ch + 2, 1:257], bb, ACT.Copy), k, k_old)
            k_hu[ch] = k_hu[ch + 1] = k2
            return (k2,)
        if ch == 6:
            o = CF[:, :, 15:271]
            k2 = act(lambda e: e.activation(o, bb, ACT.Copy), k, k_old)
            aglu[0] = k2
            return (k2,)
        tg = v3(A, 2, T, at=8 * T)
        k2 = act(lambda e: e.activation(tg, bb, ACT.Tanh, scale=0.5), k, k_old)
        for c in range(2):
            k_cf.append(dve(lambda e, c=c: e.scalar_tensor_tensor(CF[:, c, 15:271], tg[:, c, :], 1.0, CF[:, c, 15:271], ALU.add, ALU.mult), k2, aglu[0]))
        return (k2,)

    ch = 0
    for a, n in ((1536, 512), (2048, 512), (2560, 256)):
        W, kW, i = piece(wview(w, a, n), 8, n)
        k = proj_T(W, kW, hc, kh, list(range(0, n, 128)), 8, lambda j0, b, k, ch=ch: consume_mix(ch + j0, b, k))
        done_with(i, k)
        ch += n // 128

    k_ct = []
    for c in range(6):
        kk = dve(lambda e, c=c: e.tensor_scalar(CT[:, c, :], HU[:, c, 0:256], p_("sw", 3 * c), p_("sb", c), ALU.mult, ALU.add), k_hu[c], kz1, k_old)
        for j in (1, 2):
            kk = dve(lambda e, c=c, j=j: e.scalar_tensor_tensor(CT[:, c, :], HU[:, c, j:j + 256], p_("sw", 3 * c + j), CT[:, c, :], ALU.mult, ALU.add), kk)
        k_ct.append(kk)
    kcy = [None, None]
    for j in range(31):
        for c in range(2):
            if j == 0:
                kcy[c] = dve(lambda e, c=c: e.tensor_scalar(cy[:, c, :], CF[:, c, 0:256], p_("cw", c), None, ALU.mult), *k_cf, kz2, k_old)
            else:
                kcy[c] = dve(lambda e, c=c, j=j: e.scalar_tensor_tensor(cy[:, c, :], CF[:, c, j:j + 256], p_("cw", 2 * j + c), cy[:, c, :], ALU.mult, ALU.add), kcy[c])

    qkT = v3(A, 12)
    k_q = {}
    for src, off, a, sc in ((0, 0, 0, 0.125), (0, 4, 512, 1.0), (1, 8, 512, 1.0)):
        if src == 0:
            W, kW, i = piece(wview(w, a, 512), 8, 512)

        def consume(j0, b, k, off=off, sc=sc):
            k2 = act(lambda e: e.activation(qkT[:, off + j0:off + j0 + 2, :], b.ap[:, :].rearrange("p (c t) -> p c t", c=2), ACT.Copy, scale=sc),
                     k, *k_cf)
            k_q[off + j0] = k_q[off + j0 + 1] = k2
            return (k2,)
        hs, kk = (sc_, khc) if src else (hc, kh)
        k = proj_T(W, kW, hs, kk, [0, 128, 256, 384], 8, consume)
        done_with(i, k)
    W, kW, i = piece(wview(w, 1024, 512), 8, 512)
    k_v = []
    for t in range(4):
        def consume(b, k, t=t):
            k2 = act(lambda e: e.activation(V[:, t * 512:(t + 1) * 512], b.ap[:, :], ACT.Copy), k, k_old)
            k_v.append(k2)
            return (k2,)
        k = proj_tok(W, kW, sc_ if t >= 2 else hc, khc if t >= 2 else kh, t % 2, 0, 512, 8, consume)
    done_with(i, k)
    k_proj = k

    rota[0] = 6

    bias = [Buf(BB[:, i * 512:(i + 1) * 512]) for i in range(4)]
    for b_ in bias:
        b_.free = (k_mods,)
    bsem = [sem(f"s_bias{i}") for i in range(4)]
    buse = [0] * 4
    k_bias = {}
    rpb = I["rpb"]

    def load_bias(h):
        b = bias[h % 4]
        for r in range(4):
            src = bass.AP(rpb.tensor, h * 465 + (7 - r) * 31 + 15 - 63, [[1, 64], [31, 4], [1, 64]])
            dst = b.ap[64 * (r % 2):64 * (r % 2) + 64, (r // 2) * 256:(r // 2) * 256 + 256].rearrange("p (a c) -> p a c", a=4)
            sp.dma(lambda e: e.dma_start(dst, src), bsem[h % 4], *b.free)
        buse[h % 4] += 64
        b3 = b.ap.rearrange("p (t k) -> p t k", t=2)
        k_bias[h] = pool(lambda e: e.tensor_tensor(b3, b3, wmask.unsqueeze(1).broadcast_to([128, 2, 256]), ALU.add),
                         (bsem[h % 4], buse[h % 4]), k_wm)

    for h in range(4):
        load_bias(h)

    fwd = v3(CC, 2, 512, at=CONST["fwd"][0])
    inv = v3(CC, 4, 256, at=CONST["inv"][0])
    KA, KB, KC = v3(SPEC, 2, 512), v3(SPEC, 2, 512, at=1024), SPEC[:, 2048:2560]
    kmix = [None] * 8

    def hyena_run():
        Zt = v3(G, 2)
        Y = v3(G, 4, T, at=2 * T)
        tmp = v3(G, 2, T, at=6 * T)
        zT = CT[:, 4:6, :]
        kzt = [k_ct[4], k_ct[5]]
        for n in range(2):
            b = bank()
            for c in range(2):
                for t in range(2):
                    o = b.ap[:, t * 256 + c * 128:t * 256 + c * 128 + 128]
                    k = pe(lambda e: e.transpose(o, zT[:, c, t * 128:(t + 1) * 128], c_("ident")), kzt[c], *b.free)
            k = act(lambda e: e.activation(Zt, b.ap[:, :].rearrange("p (c t) -> p c t", c=2), ACT.Copy), k, *k_ct)
            b.free = (k,)
            yield
            zb = []
            for part in range(2):
                b = bank()
                for f in range(2):
                    for t in range(2):
                        kk = pe(lambda e: mm(e, b.ap[:, f * 256:(f + 1) * 256], fwd[:, t, part * 256 + f * 128:part * 256 + f * 128 + 128],
                                             Zt[:, t, :], t == 0, t == 1), k, *b.free)
                zb.append((b, kk))
            (br, kr), (bi, ki) = zb
            sl = slice(n * 256, n * 256 + 256)
            c2 = lambda a: a.rearrange("p (c t) -> p c t", c=2)
            k1 = dve(lambda e: e.tensor_tensor(Y[:, 0:2, :], c2(br.ap[:, :]), KA[:, :, sl], ALU.mult), kr, *k_ct)
            k2 = dve(lambda e: e.tensor_tensor(tmp, c2(bi.ap[:, :]), KB[:, :, sl], ALU.mult), ki)
            k3 = pool(lambda e: e.tensor_tensor(Y[:, 0:2, :], Y[:, 0:2, :], tmp, ALU.subtract), k1, k2)
            k4 = dve(lambda e: e.tensor_tensor(Y[:, 2:4, :], c2(br.ap[:, :]), KB[:, :, sl], ALU.mult), kr)
            k5 = dve(lambda e: e.tensor_tensor(tmp[:, 0, :], bi.ap[:, 0:256], KC[:, sl], ALU.mult), k3)
            k6 = dve(lambda e: e.tensor_tensor(tmp[:, 1, :], bi.ap[:, 256:512], KA[:, 1, sl], ALU.mult), k3)
            br.free, bi.free = (k4,), (k6,)
            k7 = pool(lambda e: e.tensor_tensor(Y[:, 2:4, :], Y[:, 2:4, :], tmp, ALU.add), k4, k5, k6)
            yield
            yield
            b = bank()
            for c in range(2):
                for f in range(4):
                    k = pe(lambda e: mm(e, b.ap[:, c * 256:(c + 1) * 256], Y[:, f, c * 128:(c + 1) * 128], inv[:, f, :], f == 0, f == 3), k3, k7, *b.free)
            kn = []
            for c in range(2):
                o = zT[:, c, :] if n == 0 else U[:, (4 + c) * T:(5 + c) * T]
                k8 = dve(lambda e: e.scalar_tensor_tensor(zT[:, c, :], zT[:, c, :], p_("bd", 2 * n + c), b.ap[:, c * 256:(c + 1) * 256], ALU.mult, ALU.add), k)
                k9 = dve(lambda e: e.tensor_tensor(o, zT[:, c, :], CT[:, 2 * n + c, :], ALU.mult), k8, k_ct[2 * n + c], k_old)
                kn.append(k9)
            b.free = (k8,)
            kzt = kn
            yield
        kmix[4], kmix[5] = kn

    def cf_run():
        t8 = v3(R, 2, T, at=8 * T)
        t9 = v3(A, 2, T, at=12 * T)
        ky = []
        for c in range(2):
            ky.append(dve(lambda e: e.tensor_scalar(cy[:, c, :], cy[:, c, :], 0.5, p_("cb", c), ALU.mult, ALU.add), kcy[c]))
        b = bank()
        for c in range(2):
            k = pe(lambda e: mm(e, b.ap[:, 0:T], c_("nones"), cy[:, c, :], c == 0, c == 1), ky[c], *b.free)
        for c in range(2):
            ky[c] = dve(lambda e: e.scalar_tensor_tensor(cy[:, c, :], b.ap[:, 0:T], 1.0 / 256, cy[:, c, :], ALU.mult, ALU.add), k)
        b.free = (ky[1],)
        k = act(lambda e: e.activation(t8, cy, ACT.Square), *ky)
        yield
        b = bank()
        for c in range(2):
            kk = pe(lambda e: mm(e, b.ap[:, 0:T], c_("nones"), t8[:, c, :], c == 0, c == 1), k, *b.free)
        k = dve(lambda e: e.tensor_scalar(sm_r, b.ap[:, 0:T], -1.0 / 256, 1e-6, ALU.mult, ALU.add), kk, *smr_free[0])
        b.free = (k,)
        k = rsq(sm_r, k)
        for c in range(2):
            k1 = dve(lambda e: e.tensor_tensor(cy[:, c, :], cy[:, c, :], sm_r, ALU.mult), k)
            ky[c] = dve(lambda e: e.tensor_scalar(cy[:, c, :], cy[:, c, :], p_("lng", c), p_("lnb", c), ALU.mult, ALU.add), k1)
        smr_free[0] = (k1,)
        k = act(lambda e: e.activation(t9, cy, ACT.Tanh, scale=0.5), *ky)
        yield
        for c in range(2):
            k1 = dve(lambda e: e.scalar_tensor_tensor(cy[:, c, :], t9[:, c, :], 1.0, cy[:, c, :], ALU.add, ALU.mult), k)
            kmix[6 + c] = dve(lambda e: e.tensor_scalar(U[:, (6 + c) * T:(7 + c) * T], cy[:, c, :], 0.5, None, ALU.mult), k1, k_old)

    def na_attention(steps):
        pb = [Buf(hT[:, i * 512:(i + 1) * 512]) for i in range(4)]
        pt = [Buf(S[:, i * 512:(i + 1) * 512]) for i in range(4)]
        for x_ in pb + pt:
            x_.free = (k_proj,)
        st = {}
        s4 = lambda u, j: sm[:, 128 + (u % 4) * 4 + j:129 + (u % 4) * 4 + j]

        def stage_s(u0):
            hp, t = u0 // 4, (u0 // 2) % 2
            us = {u0: 2 * hp, u0 + 1: 2 * hp + 1}
            bs = {}
            for u, h in us.items():
                bs[u] = bank()
                pe.waits([k_q[hp], k_q[4 + hp], k_q[8 + hp], k_bias[h], *bs[u].free])
            for off, j in ((0, 4), (256, 8)):
                for u, h in us.items():
                    p0 = 64 * (h % 2)
                    pe.more(lambda e: mm(e, bs[u].ap[:, off:off + 256], qkT[p0:p0 + 64, hp, t * 128:(t + 1) * 128],
                                         qkT[p0:p0 + 64, j + hp, :], off == 0, True, True))
            for u, h in us.items():
                k = pe(lambda e: mm(e, bs[u].ap[:, 0:256], c_("flip"), bias[h % 4].ap[:, t * 256:(t + 1) * 256], False, True, True))
                if t == 1:
                    bias[h % 4].free = (k,)
            if t == 1:
                for h in (2 * hp + 4, 2 * hp + 5):
                    if h < 8:
                        load_bias(h)
            for u in us:
                b = bs[u]
                p = pb[u % 4]
                k1 = dve(lambda e: e.tensor_reduce(s4(u, 0), b.ap[:, :], AX.X, ALU.max), k, *st.get(("s", u - 4), ()))
                k2 = dve(lambda e: e.tensor_scalar(s4(u, 1), s4(u, 0), -1.0, None, ALU.mult), k1)
                k3 = act(lambda e: e.activation(p.ap, b.ap[:, :], ACT.Exp, bias=s4(u, 1), accum_out=s4(u, 2)), k2, *p.free)
                b.free = (k3,)
                k4 = dve(lambda e: e.reciprocal(s4(u, 3), s4(u, 2)), k3)
                k5 = dve(lambda e: e.tensor_scalar(p.ap, p.ap, s4(u, 3), None, ALU.mult), k4)
                st[("s", u)] = (k5,)
                st[u] = (p, k5)

        def stage_t(u):
            p, kp = st[u]
            b = bank()
            for j in range(4):
                k = pe(lambda e: e.transpose(b.ap[:, j * 128:(j + 1) * 128], p.ap[:, j * 128:(j + 1) * 128], c_("ident")), kp, *b.free)
            p.free = (k,)
            q = pt[u % 4]
            k2 = act(lambda e: e.activation(q.ap, b.ap[:, :], ACT.Copy), k, *q.free)
            b.free = (k2,)
            st[u] = (q, k2)


        def stage_o(u0):
            hp, t = u0 // 4, (u0 // 2) % 2
            b = banks[6 + hp % 2]
            q = {u: st.pop(u) for u in (u0, u0 + 1)}
            pe.waits([*k_v, *b.free, *[x_[1] for x_ in q.values()]])
            for j in range(4):
                for u in q:
                    p0 = 64 * (u % 2)
                    h = 2 * hp + u % 2
                    k = pe(lambda e: mm(e, b.ap[p0:p0 + 64, t * 128:(t + 1) * 128], V[:, j * 512 + h * 64:j * 512 + h * 64 + 64],
                                        q[u][0].ap[:, j * 128:(j + 1) * 128], j == 0, j == 3))
            for u in q:
                q[u][0].free = (k,)
            if t == 1:
                k3 = dve(lambda e: e.tensor_copy(U[:, hp * T:(hp + 1) * T], b.ap[:, 0:256]), k, k_old)
                b.free = (k3,)
                kmix[hp] = k3

        def step():
            if steps:
                try:
                    next(steps[0])
                except StopIteration:
                    steps.pop(0)

        for i in range(8 + 2):
            if i < 8:
                stage_s(2 * i)
            step()
            if 0 <= i - 1 < 8:
                stage_t(2 * i - 2)
                stage_t(2 * i - 1)
            step()
            if 0 <= i - 2 < 8:
                stage_o(2 * i - 4)

    steps = [hyena_run(), cf_run()]
    mark("na")
    na_attention(steps)
    for s_ in steps:
        for _ in s_:
            pass
    if level == 25:
        s5 = sem("s_dbg")
        sp.dma(lambda e: e.dma_start(O["dbg"], U[:, :]), s5, *kmix)
        sp.items.append(("w", s5, 16))
        return finish(nc, locals())
    mark("l2out")
    ws = halves(I["w_out_2"][0])
    done = tuple((q.sem, q.n) for q in (pe, act, dve, pool))
    for i in range(NSLOT, NSLOT + 3):
        order.insert(NSLOT - 2 + i - NSLOT, i)
        slot_free[i] = done
    out_proj(ws, lambda c: U[:, c * T:(c + 1) * T], kmix, lambda c: m_(2, c))
    mark("end")
    if level == 3:
        return finish(nc, locals())

    mark("route")
    k_old = (pe.sem, pe.n)
    kh, _ = rms_T(xc, 8, D, kx, lambda c: gs[:, 16 + c:17 + c], hc, lambda c: m_(3, c))
    b = bank()
    for t in range(2):
        for c in range(8):
            k = pe(lambda e: mm(e, b.ap[:, t * 16:(t + 1) * 16], hc(c)[:, t * 128:(t + 1) * 128], rw[:, c * 16:(c + 1) * 16], c == 0, c == 7),
                   kh[c], k_rw, *b.free)
    aff = sm[:, 128:160]
    a3 = aff.rearrange("p (t e) -> p t e", t=2)
    mx = sm[:, 160:164]
    b3 = b.ap[:, 0:32].rearrange("p (t e) -> p t e", t=2)
    k = dve(lambda e: e.tensor_reduce(mx[:, 0:2], b3, AX.X, ALU.max), k)
    k = dve(lambda e: e.tensor_tensor(a3, b3, mx[:, 0:2].unsqueeze(2).broadcast_to([128, 2, 16]), ALU.subtract), k)
    b.free = (k,)
    k = act(lambda e: e.activation(aff, aff, ACT.Exp), k)
    k = dve(lambda e: e.tensor_reduce(mx[:, 2:4], a3, AX.X, ALU.add), k)
    k = dve(lambda e: e.reciprocal(mx[:, 2:4], mx[:, 2:4]), k)
    k_aff = dve(lambda e: e.tensor_tensor(a3, a3, mx[:, 2:4].unsqueeze(2).broadcast_to([128, 2, 16]), ALU.mult), k)
    b = bank()
    for t in range(2):
        k = pe(lambda e: e.transpose(b.ap[0:16, t * 128:(t + 1) * 128], a3[:, t, :], c_("ident")), k_aff, *b.free)
    w0 = U[0:16, 1024:1280]
    sel = U[0:16, 1280:1536]
    slot = U[0:16, 1536:1792]
    m8 = U[0:16, 1792:1824]
    k = dve(lambda e: e.tensor_copy(w0, b.ap[0:16, 0:256]), k, k_old)
    b.free = (k,)
    k_ht = []
    for t in range(2):
        for c0 in (0, 4):
            b = bank()
            for c in range(c0, c0 + 4):
                kk = pe(lambda e: e.transpose(b.ap[:, (c - c0) * 128:(c - c0 + 1) * 128], hc(c)[:, t * 128:(t + 1) * 128], c_("ident")), kh[c], *b.free)
            kk = act(lambda e: e.activation(V[:, t * 1024 + c0 * 128:t * 1024 + c0 * 128 + 512], b.ap[:, :], ACT.Copy), kk, k_old)
            b.free = (kk,)
            k_ht.append(kk)
    for r in range(4):
        k = dve(lambda e: e.max(m8[:, 8 * r:8 * r + 8], w0), k)
        k = dve(lambda e: e.match_replace(w0, m8[:, 8 * r:8 * r + 8], w0, -1.0), k)
    k = dve(lambda e: e.tensor_scalar(sel, w0, -1.0, None, ALU.is_equal), k)
    k = dve(lambda e: e.tensor_tensor_scan(slot, sel, sel, 0.0, ALU.add, ALU.bypass), k)
    k = dve(lambda e: e.tensor_tensor(slot, slot, sel, ALU.mult), k)
    b = bank()
    for t in range(2):
        k1 = pe(lambda e: e.transpose(b.ap[:, t * 16:(t + 1) * 16], slot[:, t * 128:(t + 1) * 128], c_("ident")[0:16, 0:16]), k, *b.free)
    GM = v3(S, 2, 512)
    gx = [Buf(S[:, 1024 + i * T:1024 + (i + 1) * T]) for i in range(2)]
    k_gm = []
    io = c_("iota").unsqueeze(1).broadcast_to([128, 16, 32])
    ko_ = (act.sem, act.n)
    for t in range(2):
        g3 = GM[:, t, :].rearrange("p (e j) -> p e j", e=16)
        k2 = dve(lambda e: e.tensor_tensor(g3, b.ap[:, t * 16:(t + 1) * 16].unsqueeze(2).broadcast_to([128, 16, 32]), io, ALU.is_equal), k1, k_old, kh[0])
        k_gm.append(k2)
    b.free = (k2,)
    xe = [(hT if c < 4 else G)[:, c % 4 * 512:c % 4 * 512 + 512] for c in range(8)]
    k_tr = (pe.sem, pe.n)
    k_xe = []
    for c in range(8):
        b = bank()
        for t in range(2):
            k = pe(lambda e: mm(e, b.ap[:, :], V[:, t * 1024 + c * 128:t * 1024 + (c + 1) * 128], GM[:, t, :], t == 0, t == 1),
                   k_gm[t], *k_ht, *b.free)
        if c % 2:
            k = act(lambda e: e.activation(xe[c], b.ap[:, :], ACT.Copy), k, k_tr)
        else:
            k = dve(lambda e: e.tensor_copy(xe[c], b.ap[:, :]), k, k_tr)
        b.free = (k,)
        k_xe.append(k)
    mark("moe")
    sg = [Buf(R[:, (8 + i) * T:(9 + i) * T]) for i in range(2)]
    k_old = (pe.sem, pe.n)
    hs = [Buf(V[:, i * 512:(i + 1) * 512]) for i in range(2)]
    ht = [Buf(V[:, (2 + i) * 512:(3 + i) * 512]) for i in range(2)]
    ysb = Buf(U[:, 0:1024])
    for x_ in hs + ht + sg + gx + [ysb]:
        x_.free = (k_old,)
    W1, W3, W2 = I["expert_w1_2"][0], I["expert_w3_2"][0], I["expert_w2_2"][0]
    rowv = lambda w_: w_.rearrange("(c p) n -> p c n", p=128)
    yb, gb = banks[4:6], banks[6:8]
    ksc = []

    def scatter(ex, ky):
        s_ = sg[ex % 2]
        for c0 in range(0, 8, 2):
            b = gb[(c0 // 2) % 2]
            for c in (c0, c0 + 1):
                o = b.ap[:, (c % 2) * T:(c % 2 + 1) * T]
                k = pe(lambda e: mm(e, o, ysb.ap[:, c * 128:(c + 1) * 128], s_.ap, True), *ky, *b.free)
            for c in (c0, c0 + 1):
                o = b.ap[:, (c % 2) * T:(c % 2 + 1) * T]
                kx[c] = dve(lambda e: e.scalar_tensor_tensor(xc(c), o, m_(5, c), xc(c), ALU.mult, ALU.add), k, kx[c])
            b.free = (kx[c],)
        ysb.free = (k,)
        s_.free = (k,)

    prev = None
    for ex in range(16):
        a_, u_ = banks[2 * (ex % 2)], banks[2 * (ex % 2) + 1]
        for w_, b in ((W1, a_), (W3, u_)):
            for i4 in range(4):
                W, kW, i = piece(rowv(w_[ex])[:, 2 * i4:2 * i4 + 2, :], 2, 2048)
                pe.waits([kW, *k_xe, *b.free])
                for c in range(2):
                    for q in range(4):
                        fn = lambda e: mm(e, b.ap[32 * q:32 * q + 32, :], xe[2 * i4 + c][:, ex * 32:ex * 32 + 32],
                                          W[:, c, q * 512:(q + 1) * 512], i4 == 0 and c == 0, i4 == 3 and c == 1, True)
                        if c == 1 and q == 3:
                            k = pe(fn)
                        else:
                            pe.more(fn)
                done_with(i, k)
            if w_ is W1:
                ka = k
        h_ = hs[ex % 2]
        k1 = act(lambda e: e.activation(h_.ap, a_.ap[:, :], ACT.Tanh, scale=0.5), ka, *h_.free)
        k2 = dve(lambda e: e.scalar_tensor_tensor(h_.ap, h_.ap, 1.0, a_.ap[:, :], ALU.add, ALU.mult), k1)
        k3 = dve(lambda e: e.scalar_tensor_tensor(h_.ap, h_.ap, 0.5, u_.ap[:, :], ALU.mult, ALU.mult), k2, k)
        a_.free, u_.free = (k2,), (k3,)
        if prev is not None:
            scatter(*prev)
        b = gb[0]
        for j in range(4):
            k = pe(lambda e: e.transpose(b.ap[:, j * 128:(j + 1) * 128], h_.ap[:, j * 128:(j + 1) * 128], c_("ident")), k3, *b.free)
        h_.free = (k,)
        t_ = ht[ex % 2]
        k4 = act(lambda e: e.activation(t_.ap, b.ap[:, :], ACT.Copy), k, *t_.free)
        b.free = (k4,)
        b = gb[1]
        s_ = sg[ex % 2]
        g_ = gx[ex % 2]
        for t in range(2):
            src = GM[:, t, ex * 32:(ex + 1) * 32].unsqueeze(1).broadcast_to([128, 4, 32])
            k5 = pool(lambda e: e.tensor_scalar(g_.ap[:, t * 128:(t + 1) * 128].rearrange("p (a j) -> p a j", a=4), src,
                                                a3[:, t, ex:ex + 1], None, ALU.mult), k_gm[t], k_aff, *g_.free)
            k = pe(lambda e: e.transpose(b.ap[:, t * 128:(t + 1) * 128], g_.ap[:, t * 128:(t + 1) * 128], c_("ident")), k5, *b.free)
        g_.free = (k,)
        k5 = act(lambda e: e.activation(s_.ap, b.ap[:, 0:256], ACT.Copy), k, *s_.free)
        b.free = (k5,)
        for fq in range(4):
            W, kW, i = piece(rowv(W2[ex])[:, 4 * fq:4 * fq + 4, :], 4, 1024)
            pe.waits([kW, k4, *yb[0].free, *yb[1].free])
            for half in range(2):
                for j in range(4):
                    fn = lambda e: mm(e, yb[half].ap[32 * j:32 * j + 32, :], t_.ap[:, j * 128 + fq * 32:j * 128 + fq * 32 + 32],
                                      W[:, j, half * 512:(half + 1) * 512], fq == 0, fq == 3, True)
                    if half == 1 and j == 3:
                        k = pe(fn)
                    else:
                        pe.more(fn)
            done_with(i, k)
        t_.free = (k,)
        ky = []
        for half in range(2):
            kk = act(lambda e: e.activation(ysb.ap[:, half * 512:(half + 1) * 512], yb[half].ap[:, :], ACT.Copy), k, *ysb.free)
            yb[half].free = (kk,)
            ky.append(kk)
        prev = (ex, (*ky, k5))
    scatter(*prev)
    mark("tail")
    mark("end")
    if level == 4:
        return finish(nc, locals())
    oT = lambda c: hT[:, c * T:(c + 1) * T]
    ko, _ = rms_T(xc, 8, D, kx, lambda c: p_("final", c), oT)
    xout = []
    for half in range(2):
        s = sem(f"s_out{half}")
        sp.dma(lambda e: e.dma_start(O["out"].rearrange("(c p) t -> p c t", p=128)[:, 4 * half:4 * half + 4, :], v3(hT, 4, T, at=4 * half * T)), s,
               *ko[4 * half:4 * half + 4])
        xout.append(s)
    for s in xout:
        sp.items.append(("w", s, 16))
    finish(nc, locals())


def finish(nc, L):
    I, O = L["I"], L["O"]
    sp, sem = L["sp"], L["sem"]
    if "xout" not in L:
        s = sem("s_out")
        xT = L["xT"]
        sp.dma(lambda e: e.dma_start(O["out"].rearrange("(c p) t -> p c t", p=128), xT[:, :].rearrange("p (c t) -> p c t", c=8)), s, *L["kx"])
        sp.items.append(("w", s, 16))
        if L["level"] == 0:
            s2 = sem("s_out2")
            sp.dma(lambda e: e.dma_start(O["dbg"], L["SPEC"][:, :]), s2, *L["k_spec"])
            sp.items.append(("w", s2, 16))
    block = L["ctx"].enter_context(nc.Block())

    def emit(q, eng):
        for it in q.items:
            if it[0] == "w":
                eng.wait_ge(it[1], it[2])
            elif it[0] == "m":
                it[1](eng)
            elif it[0] == "t":
                eng.preload_act_table_set(it[1])
            else:
                it[1](eng).then_inc(it[2], it[3])

    @block.sync
    def _(eng):
        emit(L["sp"], eng)

    @block.gpsimd
    def _(eng):
        emit(L["pool"], eng)

    @block.scalar
    def _(eng):
        emit(L["act"], eng)

    @block.vector
    def _(eng):
        emit(L["dve"], eng)

    @block.tensor
    def _(eng):
        emit(L["pe"], eng)


def _constants():
    f = np.float64
    p = np.arange(128)
    c = {}
    c["ident"] = np.eye(128)
    c["ntri"] = -(p[:, None] >= p[None, :]).astype(f)
    c["nones"] = -np.ones((128, 128))
    c["m01"] = (p[:, None] < p[None, :]).astype(f)
    cap = np.where(p[:, None] < p[None, :], 0.0, NEG)
    c["cap"] = np.concatenate([cap, np.zeros((128, 128)), cap], 1)
    c["caus"] = np.where(p[None, :] <= p[:, None], 0.0, NEG)
    c["iota"] = np.tile(np.arange(1, 33), (128, 1))
    half = 32
    inv = (np.float32(10000.0) ** (-np.arange(half, dtype=np.float32) / np.float32(half))).astype(np.float32)
    ang = (np.arange(T, dtype=np.float32)[:, None] * inv[None, :]).astype(np.float32).astype(f)
    cos = np.concatenate([np.cos(ang), np.cos(ang)], 1)
    sin = np.concatenate([-np.sin(ang), np.sin(ang)], 1)
    c["cosd"] = np.concatenate([cos[:128], cos[128:]], 1)
    c["sind"] = np.concatenate([sin[:128], sin[128:]], 1)
    s = np.arange(T)
    k = np.arange(T)
    th = 2 * math.pi * ((s[:, None] * k[None, :]) % 512) / 512
    Fre, Fim = np.cos(th), -np.sin(th)
    alt = np.where(s % 2 == 0, 1.0, -1.0)
    Fimn = Fim.copy()
    Fimn[:, 0] = alt
    fw = np.concatenate([Fre, Fimn], 1)
    c["fwd"] = np.concatenate([fw[:128], fw[128:]], 1)
    ny = Fre[:, :128].copy()
    ny[:, 0] = alt
    c["nyq"] = np.concatenate([ny[:128], ny[128:]], 1)
    wt = np.where(k == 0, 1.0, 2.0)[:, None] / 512
    Gre = wt * np.cos(th.T)
    Gim = -(2.0 / 512) * np.sin(th.T)
    Gim[0] = alt / 512
    g = np.concatenate([Gre, Gim], 0)
    c["inv"] = np.concatenate([g[i * 128:(i + 1) * 128] for i in range(4)], 1)
    c["flip"] = (p[:, None] // 64 * 64 + 63 - p[:, None] % 64 == p[None, :]).astype(f)
    out = np.zeros((128, NCONST), np.float32)
    for name, (at, n) in CONST.items():
        out[:, at:at + n] = c[name].astype(np.float32)
    t = np.arange(T, dtype=np.float32)[:, None] / np.float32(T - 1)
    fb = np.linspace(1e-4, 15, 16, dtype=np.float32)[None, :]
    angf = (fb * np.float32(TWO_PI) * np.arange(T, dtype=np.float32)[:, None] / np.float32(T)).astype(f)
    z = np.concatenate([t.astype(f), np.cos(angf), -np.sin(angf)], 1).T.astype(np.float32)
    rate = np.abs(np.linspace(math.log(1e-2) / 1.5, math.log(1e-2) / 0.3, 256, dtype=np.float32)).astype(f)
    dec = np.exp(-t.astype(f) * rate[None, :])
    decb = dec.copy()
    decb[0] = 0
    d = np.concatenate([dec[:128], decb[:128], dec[128:], decb[128:]], 1).astype(np.float32)
    col = np.arange(T) % 64
    c0 = np.clip(col - 8, 0, 48)
    ok = (col[None, :] >= c0[:, None]) & (col[None, :] < c0[:, None] + 16)
    wm = np.where(ok, 0.0, NEG).astype(np.float32)[:128]
    wm = np.ascontiguousarray(wm.reshape(2, 64, T)[:, ::-1].reshape(128, T))
    return out, np.ascontiguousarray(z), d, wm


def _cols(inp):
    out = np.zeros((128, NCOL), np.float32)

    def put(name, a):
        at, n = COLS[name]
        out[:, at:at + n] = a

    ch = lambda v: np.asarray(v).reshape(-1, 128).T
    put("l0_norm", ch(inp["l0_norm"]))
    put("l1_norm", ch(inp["l1_norm"]))
    put("q_a", ch(inp["l1_q_a_norm"]))
    put("kv_a", ch(inp["l1_kv_a_norm"]))
    put("gq", np.asarray(inp["l1_q_head_norm"])[:128, None])
    put("gk", np.asarray(inp["l1_k_head_norm"])[:128, None])
    put("b_mod", ch(inp["b_mod_2"][0]))
    put("norm1", ch(inp["norm1_g_2"][0]))
    put("norm2", ch(inp["norm2_g_2"][0]))
    put("final", ch(inp["final_norm_g_2"]))
    put("c", np.stack([ch(inp["c_2"][0]), ch(inp["c_ctx_2"])], 2).reshape(128, 16))
    put("sw", np.asarray(inp["hy_short_w_2"][0]).reshape(3, 6, 128).transpose(2, 1, 0).reshape(128, 18))
    put("sb", ch(inp["hy_short_b_2"][0]))
    put("bd", np.asarray(inp["hy_bias_d_2"][0]).reshape(2, 2, 128).transpose(2, 0, 1).reshape(128, 4))
    put("cw", np.asarray(inp["cf_dw_w_2"][0]).reshape(31, 2, 128).transpose(2, 0, 1).reshape(128, 62))
    put("cb", ch(inp["cf_dw_b_2"][0]))
    put("lng", ch(inp["cf_ln_g_2"][0]))
    put("lnb", ch(inp["cf_ln_b_2"][0]))
    return out


def kernel(**inputs):
    import concourse.bacc as _bacc
    from concourse.bass_utils import run_bass_kernel_spmd as _run

    inp = {k: np.asarray(v) for k, v in inputs.items()}
    consts, zfeat, decay, wmask = _constants()
    arr = {
        "xT": np.ascontiguousarray(inp["x"][0].T),
        "ctxT": np.ascontiguousarray(inp["ctx_2"][0].T),
        "cols": _cols(inp),
        "consts": consts, "zfeat": zfeat, "decay": decay, "wmask": wmask,
        "rowg": np.concatenate([inp["l1_q_head_norm"][128:], inp["l1_k_head_norm"][128:]])[None, :],
        "filtp": np.stack([inp["hy_filt_b1_2"][0], inp["hy_filt_freq_2"][0], inp["hy_filt_b2_2"][0]], 1),
        "rpb": np.ascontiguousarray(inp["na_rpb_2"][0].reshape(8, 15 * 31)),
    }
    for n in ["l0_w_in", "l0_w_out", "l1_w_in", "l1_w_uq", "l1_w_ukv", "l1_w_out", "w_mod_2", "w_in_2",
              "hy_filt_w1_2", "hy_filt_w2_2", "hy_filt_w3_2", "w_out_2", "router_w_2",
              "expert_w1_2", "expert_w3_2", "expert_w2_2"]:
        arr[n] = np.ascontiguousarray(inp[n])
    nc = _bacc.Bacc("TRN2", target_bir_lowering=False, num_devices=1)
    ins = {n: nc.dram_tensor(f"in_{n}", a.shape, F32, kind="ExternalInput").ap() for n, a in arr.items()}
    outs = {"out": nc.dram_tensor("out_0", (D, T), F32, kind="ExternalOutput").ap()}
    if LEVEL == 25:
        outs["dbg"] = nc.dram_tensor("dbg_0", (128, 8 * T), F32, kind="ExternalOutput").ap()
    build_program(nc, ins, outs, LEVEL)
    r = _run(nc, [{f"in_{n}": a for n, a in arr.items()}], core_ids=[0])
    got = np.asarray(r.results[0]["out_0"])
    return np.ascontiguousarray(got.T)[None]


LEVEL = 99
MARKS = []
CNT = [0, 0]
```

```python
import math
from collections import deque
from contextlib import ExitStack

import numpy as np
import concourse.bass as bass
from concourse import mybir

F32 = mybir.dt.float32
F32R = mybir.dt.float32r
ALU = mybir.AluOpType
ACT = mybir.ActivationFunctionType
AX = mybir.AxisListType

T = 256
D = 1024
NEG = -1e30
NSLOT = 6
SLOT = 4096
TWO_PI = 2.0 * math.pi
MAGIC = 1.5 * 2.0 ** 23

COLS = {}


def _cols_layout():
    at = 0
    for name, n in [("l0_norm", 8), ("l1_norm", 8), ("q_a", 2), ("kv_a", 1), ("gq", 1), ("gk", 1),
                    ("b_mod", 48), ("norm1", 8), ("norm2", 8), ("final", 8), ("c", 16),
                    ("sw", 18), ("sb", 6), ("bd", 4), ("cw", 62), ("cb", 2), ("lng", 2), ("lnb", 2)]:
        COLS[name] = (at, n)
        at += n
    return at


NCOL = _cols_layout()

CONST = {}


def _const_layout():
    at = 0
    for name, n in [("nones", 128), ("ident", 128), ("ntri", 128), ("m01", 128),
                    ("cap", 384), ("caus", 128), ("iota", 32), ("cosd", 128), ("sind", 128),
                    ("flip", 128), ("fwd", 1024), ("nyq", 256), ("inv", 1024)]:
        CONST[name] = (at, n)
        at += n
    return at


NCONST = _const_layout()


class Recorder:

    def matmul(self, *a, **k):
        CNT[1] += 1
        return lambda e: e.matmul(*a, **k)

    def transpose(self, *a, **k):
        CNT[0] += 1
        return lambda e: e.transpose(*a, **k)

    def activation(self, *a, **k):
        return lambda e: e.activation(*a, **k)

    def tensor_scalar(self, *a, **k):
        return lambda e: e.tensor_scalar(*a, **k)

    def tensor_tensor(self, *a, **k):
        return lambda e: e.tensor_tensor(*a, **k)

    def scalar_tensor_tensor(self, *a, **k):
        return lambda e: e.scalar_tensor_tensor(*a, **k)

    def tensor_copy(self, *a, **k):
        return lambda e: e.tensor_copy(*a, **k)

    def tensor_reduce(self, *a, **k):
        return lambda e: e.tensor_reduce(*a, **k)

    def reciprocal(self, *a, **k):
        return lambda e: e.reciprocal(*a, **k)

    def memset(self, *a, **k):
        return lambda e: e.memset(*a, **k)

    def dma_start(self, *a, **k):
        return lambda e: e.dma_start(*a, **k)

    def max(self, *a, **k):
        return lambda e: e.max(*a, **k)

    def match_replace(self, *a, **k):
        return lambda e: e.match_replace(*a, **k)

    def tensor_tensor_scan(self, *a, **k):
        return lambda e: e.tensor_tensor_scan(*a, **k)

    def bn_stats(self, *a, **k):
        return lambda e: e.bn_stats(*a, **k)

    def bn_aggr(self, *a, **k):
        return lambda e: e.bn_aggr(*a, **k)


REC = Recorder()


class Queue:

    def __init__(self, name, sem):
        self.name, self.sem, self.n, self.items, self.seen = name, sem, 0, [], {}

    def waits(self, after):
        need = {}
        for tok in after:
            if tok is None:
                continue
            s, v = tok
            if self.seen.get(id(s), 0) < v:
                need[id(s)] = (s, max(v, need.get(id(s), (s, 0))[1]))
        for k, (s, v) in need.items():
            self.seen[k] = v
            self.items.append(("w", s, v))

    def __call__(self, fn, *after):
        self.waits(after)
        self.n += 1
        self.items.append(("i", fn(REC), self.sem, 1))
        return (self.sem, self.n)

    def dma(self, fn, sem, *after):
        self.waits(after)
        self.items.append(("i", fn(REC), sem, 16))

    def more(self, fn):
        self.items.append(("m", fn(REC)))


class Buf:

    def __init__(self, ap):
        self.ap, self.free = ap, ()


def build_program(nc, ins, outs, level=99):
    with ExitStack() as ctx:
        _program(nc, ins, outs, ctx, level)


def _program(nc, I, O, ctx, level):
    twins = {}

    def sb(name, n, p=128, rounded=False):
        at = (nc.sbuf_base + 31) // 32 * 32
        t = ctx.enter_context(nc.sbuf_tensor(name, [p, n], F32))
        if rounded:
            twins[name] = nc.alloc_sbuf_tensor_at(name + "_r", [p, n], F32R, offset=at)
        return t

    def sem(name):
        return ctx.enter_context(nc.semaphore(name))

    pe = Queue("pe", sem("s_pe"))
    act = Queue("act", sem("s_act"))
    dve = Queue("dve", sem("s_dve"))
    pool = Queue("pool", sem("s_pool"))
    sp = Queue("sp", None)
    out_sems = []

    ring = [sb(f"ring{i}", SLOT, rounded=True) for i in range(NSLOT)]
    late = [sb(f"late{i}", n, rounded=True) for i, n in enumerate((16 * T, 18 * T, NCONST + 11 * T))]
    xT = sb("xT", 8 * T)
    hT = sb("hT", 8 * T, rounded=True)
    A = late[0]
    V = sb("V", 8 * T)
    G = sb("G", 8 * T, rounded=True)
    U = sb("U", 8 * T, rounded=True)
    S = sb("S", 8 * T, rounded=True)
    CC = late[2][:, 0:NCONST]
    PC = sb("PC", NCOL)
    SPEC = late[1][:, 0:10 * T]
    BB = late[1][:, 10 * T:18 * T]
    R = late[2][:, NCONST:NCONST + 11 * T]
    at = CONST["fwd"][0]
    ring += [late[1][:, 0:SLOT], late[2][:, at:at + SLOT], late[0][:, 0:SLOT]]
    b16 = ctx.enter_context(nc.sbuf_tensor("b16", [128, 256], mybir.dt.bfloat16))
    identb, causb = b16[:, 0:128], b16[:, 128:256]
    mod = sb("mod", 96)
    sm = sb("sm", 256)
    rowg = sb("rowg", 128)
    rw = sb("rw", 128)
    fp = sb("fp", 3, 64)

    banks = [Buf(ctx.enter_context(nc.psum_tensor(f"ps{i}", [128, 512], F32))) for i in range(8)]
    turn = [0]

    rota = [5]

    def bank():
        b = banks[turn[0] % rota[0]]
        turn[0] += 1
        return b

    def c_(name, a=None, b=None):
        at, n = CONST[name]
        return CC[:, at + (a or 0):at + (n if b is None else b)]

    def p_(name, i=0, n=1):
        at, _ = COLS[name]
        return PC[:, at + i:at + i + n]

    def v3(t, c, w=T, at=0):
        return t[:, at:at + c * w].rearrange("p (c t) -> p c t", c=c)

    s_ld = {}

    def load(q, name, dst, src, *after):
        s = sem("s_ld_" + name)
        q.dma(lambda e: e.dma_start(dst, src), s, *after)
        s_ld[name] = (s, 16)
        return s_ld[name]

    xv = I["xT"].rearrange("(c p) t -> p c t", p=128)
    k_xh = [load(act, f"x{i}", v3(xT, 4, at=1024 * i), xv[:, 4 * i:4 * i + 4, :]) for i in range(2)]
    k_on = load(sp, "ones", CC[:, 0:128], I["consts"][:, 0:128])
    k_pc = load(sp, "pc", PC[:, :], I["cols"])

    def mark(name):
        MARKS.append((name, CNT[0], CNT[1]))

    slot_sem = [sem(f"s_ring{i}") for i in range(NSLOT + 3)]
    slot_uses = [0] * (NSLOT + 3)
    slot_free = [()] * (NSLOT + 3)
    order = deque(range(NSLOT))

    def piece(src, c, n):
        i = order.popleft()
        dst = ring[i][:, 0:c * n].rearrange("p (c n) -> p c n", c=c)
        sp.dma(lambda e: e.dma_start(dst, src), slot_sem[i], *slot_free[i])
        slot_uses[i] += 1
        return dst, (slot_sem[i], 16 * slot_uses[i]), i

    def done_with(i, *toks):
        slot_free[i] = toks
        assert i not in order
        order.append(i)

    todo, opened, emitted, taken = deque(), [], [0], [0]
    AHEAD = 2

    def r_(ap):
        return bass.AP(twins[ap.tensor.name], ap.offset, ap.ap)

    def plan(src, n, lo_q):
        todo.append((src, n, lo_q))

    def open_piece():
        src, n, lo_q = todo.popleft()
        W, kW, i = piece(src, 8, n)
        i2 = order.popleft()
        m = (n + 255) // 256
        base = opened[-1]["base"] + opened[-1]["m"] if opened else 0
        opened.append(dict(W=W, kW=kW, i=(i, i2), q=lo_q, k=[], m=m, n=n, base=base,
                           H=ring[i2][:, 0:8 * n].rearrange("p (c n) -> p c n", c=8), free=slot_free[i2]))

    def emit_chunk():
        if not opened or emitted[0] == opened[-1]["base"] + opened[-1]["m"]:
            open_piece()
        p = [p for p in opened if len(p["k"]) < p["m"]][0]
        a = 256 * len(p["k"])
        z = min(a + 256, p["n"])
        w_, h_ = p["W"][:, :, a:z], p["H"][:, :, a:z]
        k1 = act(lambda e: e.activation(r_(h_), w_, ACT.Copy), p["kW"], *p["free"])
        k2 = p["q"](lambda e: e.tensor_tensor(r_(w_), w_, r_(h_), ALU.subtract), k1, p["kW"])
        p["k"].append((k1, k2))
        emitted[0] += 1

    def take():
        if taken[0] == len(opened):
            open_piece()
        taken[0] += 1
        return opened[taken[0] - 1]

    def need(p, j, ahead=True):
        while emitted[0] < p["base"] + j + 1 or (ahead and emitted[0] < p["base"] + j + 1 + AHEAD and (todo or emitted[0] < opened[-1]["base"] + opened[-1]["m"])):
            emit_chunk()
        return p["k"][j]

    def parts(hi, lo, kh, c):
        return ((0, hi(c), kh[c]), (0, lo(c), kh[c]), (1, hi(c), kh[c]))

    def split_h(src, hi, ks, k_free=(), bias_of=None):
        out = []
        for c, k in enumerate(ks):
            if bias_of is None:
                k1 = act(lambda e: e.activation(r_(hi(c)), src(c), ACT.Copy), k, *k_free)
                k2 = dve(lambda e: e.tensor_tensor(r_(src(c)), src(c), r_(hi(c)), ALU.subtract), k1, k)
            else:
                k1 = act(lambda e: e.activation(r_(hi(c)), src(c), ACT.Identity, bias=bias_of(c)), k, *k_free)
                k2 = dve(lambda e: e.scalar_tensor_tensor(r_(src(c)), src(c), bias_of(c), r_(hi(c)), ALU.add, ALU.subtract), k1, k)
            out.append((k2, k1))
        return out

    pre = {}

    def take_now():
        if taken[0] == len(opened):
            open_piece()
        return opened[taken[0]]

    def out_pre(p, j, cs, hi, lo, kh):
        b = bank()
        pe.waits([*need(p, j, False), *b.free])
        for n in range(2):
            a = j * 256 + n * 128
            o = b.ap[:, n * T:(n + 1) * T]
            for c in cs:
                pe.waits(kh[c])
                H, L = p["H"][:, c, a:a + 128], p["W"][:, c, a:a + 128]
                pe.more(lambda e: mm(e, o, r_(H), r_(hi(c)), n == 0 and c == cs[0], True, True))
                pe.more(lambda e: mm(e, o, r_(H), r_(lo(c)), False, True, True))
                pe.more(lambda e: mm(e, o, r_(L), r_(hi(c)), False, True, True))
        pre[j] = (b, cs)

    def sproj_T(p, hi, lo, kh, consume, last=True, ahead=True):
        for j in range(p["m"]):
            kk = need(p, j, ahead or j + 1 < p["m"])
            b, cs = pre.pop(j) if j in pre else (bank(), ())
            pe.waits([*kk, *(() if cs else b.free)])
            for n in range(2):
                a = j * 256 + n * 128
                for c in [c for c in range(8) if c not in cs]:
                    end = 7 if 7 not in cs else min(cs) - 1
                    pe.waits(kh[c])
                    H, L = p["H"][:, c, a:a + 128], p["W"][:, c, a:a + 128]
                    o = b.ap[:, n * T:(n + 1) * T]
                    pe.more(lambda e: mm(e, o, r_(H), r_(hi(c)), c == 0 and not cs, bool(cs), bool(cs)))
                    pe.more(lambda e: mm(e, o, r_(H), r_(lo(c)), False, bool(cs), bool(cs)))
                    f = lambda e: mm(e, o, r_(L), r_(hi(c)), False, c == 7 or bool(cs), bool(cs))
                    if c < end:
                        pe.more(f)
                    else:
                        k = pe(f)
            b.free = consume(2 * j, b, k)
        if last:
            for i in p["i"]:
                done_with(i, k)
        return k

    def sproj_tok(p, hi, lo, kh, t, consume, last=True):
        n = p["n"]
        for j in range(p["m"]):
            pe.waits(need(p, j))
        b = bank()
        pe.waits(b.free)
        for c in range(8):
            pe.waits(kh[c])
            ts = slice(t * 128, (t + 1) * 128)
            pe.more(lambda e: mm(e, b.ap[:, 0:n], r_(hi(c)[:, ts]), r_(p["H"][:, c, :]), c == 0, False))
            pe.more(lambda e: mm(e, b.ap[:, 0:n], r_(hi(c)[:, ts]), r_(p["W"][:, c, :]), False, False))
            f = lambda e: mm(e, b.ap[:, 0:n], r_(lo(c)[:, ts]), r_(p["H"][:, c, :]), False, c == 7)
            if c < 7:
                pe.more(f)
            else:
                k = pe(f)
        b.free = consume(b, k)
        if last:
            for i in p["i"]:
                done_with(i, k)
        return k

    def wview(w, a, n):
        return w.rearrange("(c p) n -> p c n", p=128)[:, :, a:a + n]

    mm = lambda e, o, l, r, st, sp_=True, sk=False: e.matmul(o, l, r, start=st, stop=sp_, skip_group_check=sk)

    def rsq(ap, *k):
        act.items.append(("t", "sqrt_and_others"))
        k = act(lambda e: e.activation(ap, ap, ACT.Sqrt), *k)
        act.items.append(("t", "exp_and_others"))
        return dve(lambda e: e.reciprocal(ap, ap), k)

    def rms_T(src, nch, dim, k_src, scale_of, out, bias_of=None, scr=None, k_scr=(), nfill=0, mid=None):
        scr = scr if scr is not None else v3(S, 8)
        b = bank()
        ks = []
        for c in range(nch):
            ks.append(act(lambda e, c=c: e.activation(scr[:, c, :], src(c), ACT.Square),
                          k_src[c], *(k_scr if c == 0 else ())))
        for c in range(nch):
            o = b.ap[32 * (c % 4):32 * (c % 4) + 32, 0:T]
            k = pe(lambda e: mm(e, o, c_("nones", 0, 32), scr[:, c, :], c < 4, c >= nch - 4, True),
                   ks[c], *(b.free if c == 0 else ()), k_on)
        k1 = dve(lambda e: e.tensor_copy(sm_r, b.ap[:, 0:T]), k, *smr_free[0])
        k = pe(lambda e: mm(e, b.ap[:, T:2 * T], c_("nones"), sm_r, True), k1)
        act.items.append(("t", "sqrt_and_others"))
        k1 = act(lambda e: e.activation(sm_r, b.ap[:, T:2 * T], ACT.Sqrt, scale=1.0 / (32 * dim), bias=epsc), k, k_eps)
        if mid is not None:
            mid()
        else:
            act.items.append(("t", "exp_and_others"))
        b.free = (k1,)
        k2 = dve(lambda e: e.reciprocal(sm_r, sm_r), k1)
        ko = []
        for c in range(nch):
            k3 = dve(lambda e, c=c: e.scalar_tensor_tensor(out(c), src(c), scale_of(c), sm_r, ALU.mult, ALU.mult),
                     k2, k_pc)
            if bias_of is not None:
                k3 = act(lambda e, c=c: e.activation(out(c), out(c), ACT.Identity, bias=bias_of(c)), k3)
            ko.append(k3)
        smr_free[0] = (k3,) if bias_of is None else (ko[-1], (dve.sem, dve.n))
        fill(nfill)
        return tuple(ko), k

    epsc = sm[:, 255:256]
    k_eps = pool(lambda e: e.memset(epsc, 1e-6))
    sm_r = R[:, 10 * T:11 * T]
    smr_free = [()]

    def proj_T(W, kW, hsrc, kh, cols, nch, consume):
        for j0 in range(0, len(cols), 2):
            b = bank()
            js = cols[j0:j0 + 2]
            for n, j in enumerate(js):
                for c in range(nch):
                    first = n == 0 and c == 0
                    if c < nch - 1:
                        pe.waits([kW, kh[c]] + (list(b.free) if first else []))
                        pe.more(lambda e, n=n, j=j, c=c: mm(
                            e, b.ap[:, n * T:(n + 1) * T], W[:, c, j:j + 128], hsrc(c), c == 0, False))
                    else:
                        k = pe(lambda e, n=n, j=j, c=c: mm(
                            e, b.ap[:, n * T:(n + 1) * T], W[:, c, j:j + 128], hsrc(c), c == 0, True), kW, kh[c],
                            *(b.free if first else ()))
            b.free = consume(j0, b, k)
        return k

    def proj_tok(W, kW, hsrc, kh, t, a, n, nch, consume, order=None):
        b = bank()
        for c in range(nch):
            f = lambda e, c=c: mm(e, b.ap[:, 0:n], hsrc(c)[:, t * 128:(t + 1) * 128], W[:, c, a:a + n], c == 0, c == nch - 1)
            if c < nch - 1:
                pe.waits([kW, kh[c]] + (list(b.free) if c == 0 else []))
                pe.more(f)
            else:
                k = pe(f, kW, kh[c], *(b.free if c == 0 else ()))
        b.free = consume(b, k)
        return k

    fillers = []

    def fill(n=1):
        for _ in range(n):
            if fillers:
                fillers.pop(0)()

    def gate_T(p, hi, lo, kh, dst, ch0, ahead=True):
        ks = []

        def consume(j0, b, k):
            o = v3(dst, 8)[:, ch0 + j0:ch0 + j0 + 2, :]
            bb = b.ap[:, :].rearrange("p (c t) -> p c t", c=2)
            k1 = act(lambda e: e.activation(o, bb, ACT.Tanh, scale=0.5), k)
            k2 = dve(lambda e: e.scalar_tensor_tensor(o, o, 1.0, bb, ALU.add, ALU.mult), k1)
            ks.append(k2)
            return (k2,)
        k = sproj_T(p, hi, lo, kh, consume, True, ahead)
        return k, ks

    def out_proj(hi, lo, ku, scale_of, k_extra=(), hook=None):
        for half in range(2):
            def consume(j0, b, k, half=half):
                kk = None
                for n in range(2):
                    c = half * 4 + j0 + n
                    xc = xT[:, c * T:(c + 1) * T]
                    if scale_of is None:
                        kk = dve(lambda e, n=n, xc=xc: e.tensor_tensor(xc, b.ap[:, n * T:(n + 1) * T], xc, ALU.add), k, *k_extra)
                    else:
                        kk = dve(lambda e, n=n, xc=xc, c=c: e.scalar_tensor_tensor(
                            xc, b.ap[:, n * T:(n + 1) * T], scale_of(c), xc, ALU.mult, ALU.add), k, *k_extra)
                    kx[c] = kk
                return (kk,)
            k = sproj_T(take(), hi, lo, ku, consume)
            if half == 0 and hook is not None:
                hook()

    def xc(c):
        return xT[:, c * T:(c + 1) * T]

    def hc(c):
        return hT[:, c * T:(c + 1) * T]

    kx = [k_xh[0]] * 4 + [k_xh[1]] * 4
    w = I["l0_w_in"]
    for a in (0, 256):
        plan(wview(w, a, 256), 256, dve if a else pool)
    for a in range(512, 4096, 512):
        plan(wview(w, a, 512), 512, dve)
    for a in (0, 512):
        plan(wview(I["l0_w_out"], a, 512), 512, dve)
    plan(wview(I["l1_w_in"], 0, 448), 448, dve)
    for a in (448, 960):
        plan(wview(I["l1_w_in"], a, 512), 512, dve)
    for a in (0, 512):
        plan(wview(I["l1_w_out"], a, 512), 512, dve)
    w = I["w_in_2"][0]
    for a, n in ((1536, 512), (2048, 512), (2560, 256)):
        plan(wview(w, a, n), n, dve)
    for a in (0, 512, 1024):
        plan(wview(w, a, 512), 512, pool)
    for a in (0, 512):
        plan(wview(I["w_out_2"][0], a, 512), 512, dve)
    open_piece()
    open_piece()
    k_cc = load(sp, "cc", CC[:, 128:], I["consts"][:, 128:])

    sil = BB[:, 1792:2048]
    sil3 = sil[:, :].rearrange("p (c t) -> p c t", c=8)
    s2 = sil3[:, :, 0:2]
    cview = PC[:, COLS["c"][0]:COLS["c"][0] + 16].rearrange("p (c t) -> p c t", c=8)
    k_c0 = dve(lambda e: e.memset(sil[:, :], 0.0))
    k_c = act(lambda e: e.activation(s2, cview, ACT.Tanh, scale=0.5), k_pc, k_c0)
    k_c = dve(lambda e: e.scalar_tensor_tensor(s2, s2, 1.0, cview, ALU.add, ALU.mult), k_c)
    k_c = dve(lambda e: e.tensor_scalar(s2, s2, 0.5, None, ALU.mult), k_c)
    k_mod = {}
    mtmp = Buf(BB[:, 0:512])

    def mod_piece(g, i):
        b = banks[5]

        def run():
            W, kW, slot = piece(I["w_mod_2"][0].rearrange("(c p) n -> p c n", p=128)[:, 2 * i:2 * i + 2, g * 2048:(g + 1) * 2048], 2, 2048)
            pe.waits([k_c, kW, *b.free])
            for c in range(2):
                for q in range(4):
                    f = lambda e: mm(e, b.ap[32 * q:32 * q + 32, :], sil3[:, 2 * i + c, :], W[:, c, q * 512:(q + 1) * 512],
                                     i == 0 and c == 0, i == 3 and c == 1, True)
                    if c == 1 and q == 3:
                        k = pe(f)
                    else:
                        pe.more(f)
            done_with(slot, k)
            if i == 3:
                k1 = act(lambda e: e.activation(mtmp.ap, b.ap[:, :], ACT.Copy), k, *mtmp.free, *k_spec)
                for j in range(4):
                    k2 = pe(lambda e: e.transpose(b.ap[:, j * 128:(j + 1) * 128], mtmp.ap[:, j * 128:(j + 1) * 128], c_("ident")), k1)
                mtmp.free = (k2,)
                src = b.ap[:, :].rearrange("p (j q r) -> p q j r", j=4, q=4)[:, :, :, 0:2]
                dst = mod[:, 32 * g:32 * g + 32].rearrange("p (q j r) -> p q j r", q=4, j=4)
                bm = PC[:, COLS["b_mod"][0] + 16 * g:COLS["b_mod"][0] + 16 * g + 16].rearrange("p (q j) -> p q j", q=4)
                for r_ in range(2):
                    k3 = dve(lambda e: e.tensor_tensor(dst[:, :, :, r_], src[:, :, :, r_], bm, ALU.add), k2, k_pc)
                b.free = (k3,)
                k_mod[g] = k3
        return run

    for g in range(3):
        for i in range(4):
            fillers.append(mod_piece(g, i))

    def m_(group, c, ctx_=0):
        j = (group * 8 + c) * 2 + ctx_
        return mod[:, j:j + 1]

    def hyena_filters():
        w3 = U[0:64, 0:1024]
        w2 = U[0:64, 1024:1088]
        w1 = U[0:33, 1088:1152]
        zf = U[0:33, 1152:1408]
        kw3 = load(sp, "w3", w3, I["hy_filt_w3_2"][0])
        kw2 = load(sp, "w2", w2, I["hy_filt_w2_2"][0])
        kw1 = load(sp, "w1", w1, I["hy_filt_w1_2"][0])
        kz = load(sp, "zf", zf, I["zfeat"])
        kd = load(sp, "dec", BB[:, 0:1024], I["decay"])
        kfp = load(sp, "fp", fp[:, :], I["filtp"])
        u = BB[0:64, 1024:1280]
        kk = BB[0:64, 1280:1536]
        h = BB[0:64, 1536:1792]

        def sine(b, k, bias):
            k = dve(lambda e: e.tensor_scalar(u, b.ap[0:64, 0:T], fp[:, bias:bias + 1], fp[:, 1:2], ALU.add, ALU.mult), k, kfp)
            b.free = (k,)
            k = dve(lambda e: e.tensor_scalar(kk, u, 1.0 / TWO_PI, MAGIC, ALU.mult, ALU.add), k)
            k = dve(lambda e: e.tensor_scalar(kk, kk, MAGIC, None, ALU.subtract), k)
            c1 = 6.28125
            c2 = float(np.float32(np.round((TWO_PI - c1) * 2 ** 20) / 2 ** 20))
            c3 = TWO_PI - c1 - c2
            for cst in (c1, c2, c3):
                k = dve(lambda e, cst=cst: e.scalar_tensor_tensor(u, kk, -cst, u, ALU.mult, ALU.add), k)
            lim = 3.1415925
            k = dve(lambda e: e.tensor_scalar(u, u, lim, -lim, ALU.min, ALU.max), k)
            return act(lambda e: e.activation(h, u, ACT.Sin), k)
        b = bank()
        k = pe(lambda e: mm(e, b.ap[0:64, 0:T], w1, zf, True), kw1, kz, *b.free)
        yield
        k = sine(b, k, 0)
        yield
        b = bank()
        k = pe(lambda e: mm(e, b.ap[0:64, 0:T], w2, h, True), kw2, k, *b.free)
        yield
        k = sine(b, k, 2)
        yield
        summ = v3(S, 2, 512)
        diff = v3(S, 2, 512, at=1024)
        ks = []
        for t in range(2):
            bf, bb = bank(), bank()
            k1 = pe(lambda e: mm(e, bf.ap[:, :], h[:, t * 128:(t + 1) * 128], w3[:, 0:512], True), k, kw3, *bf.free)
            k2 = pe(lambda e: mm(e, bb.ap[:, :], h[:, t * 128:(t + 1) * 128], w3[:, 512:1024], True), *bb.free)
            dcf = BB[:, t * 512:t * 512 + 256].unsqueeze(1).broadcast_to([128, 2, 256])
            dcb = BB[:, t * 512 + 256:t * 512 + 512].unsqueeze(1).broadcast_to([128, 2, 256])
            o2 = lambda a: a.rearrange("p (o c) -> p o c", o=2)
            tmp = U[:, 1408:1920]
            k3 = dve(lambda e: e.tensor_tensor(o2(summ[:, t, :]), o2(bf.ap[:, :]), dcf, ALU.mult), k1, kd)
            k4 = dve(lambda e: e.tensor_tensor(o2(tmp), o2(bb.ap[:, :]), dcb, ALU.mult), k2, *(ks[-1:]))
            bf.free, bb.free = (k3,), (k4,)
            k5 = dve(lambda e: e.tensor_tensor(diff[:, t, :], summ[:, t, :], tmp, ALU.subtract), k3, k4)
            k6 = dve(lambda e: e.tensor_tensor(summ[:, t, :], summ[:, t, :], tmp, ALU.add), k5)
            ks.append(k6)
            yield
        fw = v3(CC, 2, 512, at=CONST["fwd"][0])
        ny = v3(CC, 2, 128, at=CONST["nyq"][0])
        KA, KB, KC = v3(SPEC, 2, 512), v3(SPEC, 2, 512, at=1024), v3(SPEC, 1, 512, at=2048)
        last = []
        for dst, rhs, lhs in [(KA[:, 0, :], summ, lambda t: fw[:, t, 0:128]), (KA[:, 1, :], summ, lambda t: fw[:, t, 128:256]),
                              (KB[:, 0, :], diff, lambda t: kb0(t)), (KB[:, 1, :], diff, lambda t: fw[:, t, 384:512]),
                              (KC[:, 0, :], summ, lambda t: ny[:, t, :])]:
            b = bank()
            for t in range(2):
                k = pe(lambda e, t=t, rhs=rhs, lhs=lhs, b=b: mm(e, b.ap[:, :], lhs(t), rhs[:, t, :], t == 0, t == 1), ks[t], k_cc,
                       *(b.free if t == 0 else ()))
            k = act(lambda e, dst=dst, b=b: e.activation(dst, b.ap[:, :], ACT.Copy), k)
            b.free = (k,)
            last.append(k)
            yield
        kz0 = pool(lambda e: e.memset(KB[0:1, 0, :], 0.0), last[2])
        k_spec.extend([kz0, *last])

    def kb0(t):
        return v3(CC, 2, 512, at=CONST["fwd"][0])[:, t, 256:384]

    k_spec = []
    kh, _ = rms_T(xc, 8, D, kx, lambda c: p_("l0_norm", c), hc, scr=v3(A, 8), mid=emit_chunk)
    hi = lambda c: R[:, c * T:(c + 1) * T]
    kh = split_h(hc, hi, kh)
    hy_steps = hyena_filters()

    mark("l0")
    w = I["l0_w_in"]
    kq = {}
    qk = v3(A, 16)
    for grp, (a, sc) in enumerate(((0, 0.125), (1024, 1.0))):
        for half in range(2):

            def consume(j0, b, k, grp=grp, half=half, sc=sc):
                ch = grp * 8 + half * 4 + j0
                o = A[:, ch * T:(ch + 2) * T]
                k2 = act(lambda e: e.activation(o, b.ap[:, :], ACT.Copy, scale=sc), k)
                kq[ch] = kq[ch + 1] = k2
                return (k2,)
            k = sproj_T(take(), hi, hc, kh, consume)
            if grp == half == 0:
                k = sproj_T(take(), hi, hc, kh, lambda j0, b, k: consume(j0 + 2, b, k))
            next(hy_steps, None)
            next(hy_steps, None)
    kv = {}
    for half in range(2):
        p = take()
        for t in range(2):
            def consume(b, k, t=t, half=half):
                k2 = dve(lambda e: e.tensor_copy(V[:, t * 1024 + half * 512:t * 1024 + half * 512 + 512], b.ap[:, :]), k)
                kv[(t, half)] = k2
                return (k2,)
            k = sproj_tok(p, hi, hc, kh, t, consume, t == 1)
    kg = []
    for half in range(2):
        k, ks = gate_T(take(), hi, hc, kh, G, half * 4)
        kg += ks

    for _ in hy_steps:
        pass
    act.items.append(("t", "natural_log_exp_and_others"))
    k_hdone = (pe.sem, pe.n)

    def sb_attention():
        e1 = [Buf(R[:, i * 384:(i + 1) * 384]) for i in range(4)]
        for x_ in e1:
            x_.free = (k_hdone,)
        Lb = [Buf(hT[:, i * 384:(i + 1) * 384]) for i in range(4)]
        for x_ in Lb:
            x_.free = (k_hdone,)
        abuf = [Buf(S[:, i * 384:(i + 1) * 384]) for i in range(4)]
        st = {}

        def stage_z(h0):
            bs = {}
            for h in (h0, h0 + 1):
                bs[h] = bank()
                pe.waits([kq[h // 2], kq[8 + h // 2], *bs[h].free])
            q = {h: A[64 * (h % 2):64 * (h % 2) + 64, (h // 2) * T:(h // 2 + 1) * T] for h in bs}
            k_ = {h: A[64 * (h % 2):64 * (h % 2) + 64, (8 + h // 2) * T:(9 + h // 2) * T] for h in bs}
            for h in bs:
                pe.more(lambda e: mm(e, bs[h].ap[:, 0:256], k_[h][:, 0:128], q[h], True, True, True))
            for h in bs:
                k = pe(lambda e: mm(e, bs[h].ap[:, 256:384], k_[h][:, 128:256], q[h][:, 128:256], False, True, True))
            for h in bs:
                b = bs[h]
                e_, L = e1[h % 4], Lb[h % 4]
                k0 = dve(lambda e: e.tensor_scalar(L.ap, b.ap[:, 0:384], 0.0, None, ALU.max), k, *L.free)
                k1 = dve(lambda e: e.scalar_tensor_tensor(e_.ap, b.ap[:, 0:384], 0.0, L.ap, ALU.min, ALU.subtract), k0, *e_.free)
                k2 = act(lambda e: e.activation(e_.ap, e_.ap, ACT.Exp), k1)
                k3 = act(lambda e: e.activation(e_.ap, e_.ap, ACT.Ln, bias=1.0), k2)
                k4 = pool(lambda e: e.tensor_tensor(L.ap, L.ap, e_.ap, ALU.add), k3)
                e_.free = (k4,)
                k6 = None
                for a in (0, 256):
                    k6 = pool(lambda e, a=a: e.tensor_tensor(L.ap[:, a:a + 128], L.ap[:, a:a + 128], c_("m01"), ALU.mult), k4, k_cc)
                st[h] = (b, L, k6, k4)

        def stage_c(h):
            b, L, k6, k4 = st[h]
            pe.waits([k6, k4])
            pe.more(lambda e: mm(e, b.ap[:, 0:256], c_("ntri"), L.ap[:, 0:256], False, True, True))
            pe.more(lambda e: mm(e, b.ap[:, 128:256], c_("nones"), L.ap[:, 256:384], False, True, True))
            k = pe(lambda e: mm(e, b.ap[:, 256:384], c_("ntri"), L.ap[:, 256:384], False, True, True))
            L.free = (k,)
            a = abuf[h % 4]
            a.free = a.free or tuple(k_spec)
            k1 = dve(lambda e: e.tensor_tensor(a.ap, b.ap[:, 0:384], c_("cap"), ALU.min), k, *a.free)
            b.free = (k1,)
            k2 = act(lambda e: e.activation(a.ap, a.ap, ACT.Exp), k1)
            st[h] = (a, k2)

        ku = []

        def stage_o(h0):
            b = banks[6 + (h0 // 2) % 2]
            av = {h: st.pop(h) for h in (h0, h0 + 1)}
            for h in av:
                pe.waits([av[h][1], *b.free, kv[(0, h // 8)], kv[(1, h // 8)]])
            for h in av:
                o = b.ap[64 * (h % 2):64 * (h % 2) + 64, 0:256]
                pe.more(lambda e: mm(e, o, V[:, h * 64:h * 64 + 64], av[h][0].ap[:, 0:256], True, True, True))
            for h in av:
                o = b.ap[64 * (h % 2):64 * (h % 2) + 64, 128:256]
                k = pe(lambda e: mm(e, o, V[:, 1024 + h * 64:1088 + h * 64], av[h][0].ap[:, 256:384], False, True, True))
            for h in av:
                av[h][0].free = (k,)
            c = h0 // 2
            k3 = dve(lambda e: e.scalar_tensor_tensor(U[:, c * T:(c + 1) * T], b.ap[:, 0:256], 0.5,
                                                      G[:, c * T:(c + 1) * T], ALU.mult, ALU.mult), k, kg[c // 2], *k_spec)
            b.free = (k3,)
            ku.append(k3)

        for i in range(8 + 2):
            if i < 8:
                stage_z(2 * i)
            if i in (0, 8):
                fill()
            if 0 <= i - 2 < 8:
                stage_o(2 * i - 4)
            if 0 <= i - 1 < 8:
                stage_c(2 * i - 2)
                stage_c(2 * i - 1)
        return ku

    mark("l0attn")
    ku = sb_attention()
    mark("l0out")
    uc = lambda c: U[:, c * T:(c + 1) * T]
    hi = lambda c: A[:, c * T:(c + 1) * T]
    out_proj(hi, uc, split_h(uc, hi, ku), None)
    if level == 1:
        return finish(nc, locals())

    mark("l1")
    kh, _ = rms_T(xc, 8, D, kx, lambda c: p_("l1_norm", c), hc, nfill=2)
    k_o = (pe.sem, pe.n)
    kh = split_h(hc, hi, kh)
    k_b16 = act(lambda e: e.activation(causb, c_("caus"), ACT.Copy), act(lambda e: e.activation(identb, c_("ident"), ACT.Copy), k_cc))
    k_rowg = load(sp, "rowg", rowg[:, :], I["rowg"].broadcast_to([128, 128]))
    w = I["l1_w_in"]
    p = take()
    lat = [S[:, 0:448], S[:, 448:896]]
    klat = []
    for t in range(2):
        def consume(b, k, t=t):
            k2 = act(lambda e: e.activation(lat[t], b.ap[:, 0:448], ACT.Copy), k)
            klat.append(k2)
            return (k2,)
        k = sproj_tok(p, hi, hc, kh, t, consume, t == 1)
    sq = S[:, 1024:1472]
    st_ = sm[:, 32:64]
    latT = v3(S, 3, T, at=1472 - 192)
    latT = v3(R, 3, T)
    klt = []
    k_prev = None
    stat_k = []
    for t in range(2):
        k = act(lambda e, t=t: e.activation(sq[:, 0:256], lat[t][:, 0:256], ACT.Square, accum_out=sm[:, 32 + 4 * t:33 + 4 * t]), klat[t])
        k = act(lambda e, t=t: e.activation(sq[:, 256:384], lat[t][:, 256:384], ACT.Square, accum_out=sm[:, 33 + 4 * t:34 + 4 * t]), k)
        k = act(lambda e, t=t: e.activation(sq[:, 384:448], lat[t][:, 384:448], ACT.Square, accum_out=sm[:, 34 + 4 * t:35 + 4 * t]), k)
        ka = dve(lambda e, t=t: e.tensor_scalar(sm[:, 40 + 4 * t:41 + 4 * t], sm[:, 32 + 4 * t:33 + 4 * t], 1.0 / 256, 1e-6, ALU.mult, ALU.add), k)
        kb = dve(lambda e, t=t: e.tensor_scalar(sm[:, 41 + 4 * t:42 + 4 * t], sm[:, 33 + 4 * t:34 + 4 * t], 1.0 / 128, 1e-6, ALU.mult, ALU.add), k)
        k2 = rsq(sm[:, 40 + 4 * t:42 + 4 * t], ka, kb)
        ka = dve(lambda e, t=t: e.tensor_scalar(lat[t][:, 0:256], lat[t][:, 0:256], sm[:, 40 + 4 * t:41 + 4 * t], None, ALU.mult), k2)
        kb = dve(lambda e, t=t: e.tensor_scalar(lat[t][:, 256:384], lat[t][:, 256:384], sm[:, 41 + 4 * t:42 + 4 * t], None, ALU.mult), k2)
        stat_k.append((ka, kb))
    kg = []

    def gate(half):
        k, ks = gate_T(take(), hi, hc, kh, G, half * 4, half == 0)
        kg.extend(ks)
    gate(0)
    bq, bk = bank(), bank()
    for t in range(2):
        for j in range(3):
            b, o = (bq, j * T) if j < 2 else (bk, 0)
            k = pe(lambda e, t=t, j=j, b=b, o=o: e.transpose(b.ap[:, o + t * 128:o + t * 128 + 128], lat[t][:, j * 128:(j + 1) * 128], c_("ident")),
                   *stat_k[t], *(b.free if t == 0 else ()))
    klq = []
    for j in range(3):
        b, o = (bq, j * T) if j < 2 else (bk, 0)
        g = p_("q_a", j) if j < 2 else p_("kv_a")
        klq.append(act(lambda e, j=j, b=b, o=o, g=g: e.activation(latT[:, j, :], b.ap[:, o:o + T], ACT.Copy, scale=g), k))
    bq.free = bk.free = (klq[-1],)
    fill()

    mark("l1q")
    Wq, kWq, iq = piece(I["l1_w_uq"].rearrange("(c p) n -> p c n", p=128), 2, 1536)
    qnT, knT = v3(A, 8), v3(A, 8, T, at=8 * T)
    qrT = v3(hT, 4)
    krT = v3(hT, 4, T, at=4 * T)
    qt = [S[:, 0:1536], U[:, 0:1536]]
    kt = [SCK[0], SCK[1]] if False else None
    ssq = sm[:, 64:96]
    kss = {}
    pe_rope = R[:, 3 * T:3 * T + 128]
    t1 = R[:, 4 * T:4 * T + 64]
    cosd = lambda t: c_("cosd", 64 * t, 64 * t + 64)
    sind = lambda t: c_("sind", 64 * t, 64 * t + 64)
    kpe = []
    for t in range(2):
        x_ = lat[t][:, 384:448]
        o = pe_rope[:, 64 * t:64 * t + 64]
        k = dve(lambda e, x_=x_: e.tensor_tensor(x_, x_, rowg[:, 64:128], ALU.mult), klat[t], k_rowg, stat_k[t][0])
        ka = dve(lambda e, t=t, x_=x_, o=o: e.tensor_tensor(o, x_, cosd(t), ALU.mult), k)
        kb = dve(lambda e, t=t, x_=x_: e.tensor_tensor(t1[:, 0:32], x_[:, 32:64], sind(t)[:, 0:32], ALU.mult), k, *kpe[-1:])
        kc = dve(lambda e, t=t, x_=x_: e.tensor_tensor(t1[:, 32:64], x_[:, 0:32], sind(t)[:, 32:64], ALU.mult), k)
        kpe.append(dve(lambda e, o=o: e.tensor_tensor(o, o, t1, ALU.add), ka, kb, kc))

    qn = {}
    sqb = [Buf(R[:, 5 * T:5 * T + 512]), Buf(R[:, 7 * T:7 * T + 512])]
    nsq = [0]
    hq = lambda c: latT[:, c, :]
    k_qt = {}
    for t in range(2):
        for g in range(4):
            def consume(b, k, t=t, g=g):
                o = qt[t][:, g * 384:(g + 1) * 384]
                s = sqb[nsq[0] % 2]
                nsq[0] += 1
                k1 = act(lambda e: e.activation(o, b.ap[:, 0:384], ACT.Copy), k, kpe[0], kpe[1], klq[2])
                k2 = act(lambda e: e.activation(s.ap[:, 0:384], b.ap[:, 0:384], ACT.Square), k, *s.free)
                k3 = dve(lambda e: e.tensor_reduce(ssq[:, t * 8 + 2 * g:t * 8 + 2 * g + 2],
                                                   s.ap[:, 0:384].rearrange("p (h d) -> p h d", h=2), AX.X, ALU.add), k2)
                s.free = (k3,)
                k_qt[(t, g)] = (k1, k3)
                return (k1, k2)
            k = proj_tok(Wq, kWq, hq, klq, t, g * 384, 384, 2, consume)
    done_with(iq, k)
    kqr = []
    qrp = [S[:, 1536:2048], U[:, 1536:2048]]
    for t in range(2):
        qv = qt[t].rearrange("p (h d) -> p h d", h=8)[:, :, 128:192]
        tmp = qrp[t].rearrange("p (h d) -> p h d", h=8)
        tm2 = R[:, 7 * T:7 * T + 512].rearrange("p (h d) -> p h d", h=8)
        rg = rowg[:, 0:64].unsqueeze(1).broadcast_to([128, 8, 64])
        cb_ = cosd(t).unsqueeze(1).broadcast_to([128, 8, 64])
        sb_ = lambda a, b, t=t: sind(t)[:, a:b].unsqueeze(1).broadcast_to([128, 8, 32])
        dep = [x for g in range(4) for x in k_qt[(t, g)]] + [x for s in sqb for x in s.free]
        k = dve(lambda e, qv=qv, tmp=tmp, rg=rg: e.tensor_tensor(tmp, qv, rg, ALU.mult), *dep, *kqr[-1:])
        ka = dve(lambda e, tm2=tm2, tmp=tmp, sb_=sb_: e.tensor_tensor(tm2[:, :, 0:32], tmp[:, :, 32:64], sb_(0, 32), ALU.mult), k, *kqr[-1:])
        kb = dve(lambda e, tm2=tm2, tmp=tmp, sb_=sb_: e.tensor_tensor(tm2[:, :, 32:64], tmp[:, :, 0:32], sb_(32, 64), ALU.mult), k)
        kc = dve(lambda e, tmp=tmp, cb_=cb_: e.tensor_tensor(tmp, tmp, cb_, ALU.mult), ka, kb)
        kqr.append(dve(lambda e: e.tensor_tensor(tmp, tmp, tm2, ALU.add), kc, ka, kb))
    for s in sqb:
        s.free = (kqr[-1],)
    scq = sm[:, 96:112]
    k = dve(lambda e: e.tensor_scalar(scq, ssq[:, 0:16], 1.0 / 192, 1e-6, ALU.mult, ALU.add), k_qt[(1, 3)][1], k_qt[(0, 3)][1])
    k = rsq(scq, k)
    k_scq = dve(lambda e: e.tensor_scalar(scq, scq, 192.0 ** -0.5, None, ALU.mult), k)
    gate(1)
    Wk, kWk, ik = piece(I["l1_w_ukv"].unsqueeze(1), 1, 2048)

    k_kh = kh
    k_qnT, k_qrT = {}, {}
    for hp in range(4):
        b = bank()
        for n in range(4):
            h, t = 2 * hp + n // 2, n % 2
            k = pe(lambda e, n=n, h=h, t=t, b=b: e.transpose(b.ap[:, n * 128:(n + 1) * 128], qt[t][:, h * 192:h * 192 + 128], c_("ident")),
                   k_qt[(t, h // 2)][0], *(b.free if n == 0 else ()))
        k = act(lambda e, hp=hp, b=b: e.activation(A[:, 2 * hp * T:(2 * hp + 2) * T], b.ap[:, :], ACT.Copy, scale=p_("gq")), k)
        b.free = (k,)
        k_qnT[hp] = k
    for t in range(2):
        b = bank()
        for n in range(4):
            k = pe(lambda e: e.transpose(b.ap[:, n * 128:(n + 1) * 128], qrp[t][:, n * 128:(n + 1) * 128], c_("ident")), kqr[t], *(b.free if n == 0 else ()))
        kk = dve(lambda e: e.tensor_copy(qrT[:, :, t * 128:(t + 1) * 128], b.ap[:, :].rearrange("p (c t) -> p c t", c=4)), k, (pe.sem, pe.n))
        b.free = (kk,)
        k_qrT[(t, 0)] = kk
    k_r2 = k
    ktk = [S[:, 0:1024], U[:, 0:1024]]
    ssk = sm[:, 80:96]
    k_kt = {}
    kvv = {}
    trans_done = (pe.sem, pe.n)
    for t in range(2):
        for g in range(4):
            def consume(b, k, t=t, g=g):
                bb = b.ap[:, :].rearrange("p (h d) -> p h d", h=2)
                o = ktk[t][:, g * 256:(g + 1) * 256].rearrange("p (h d) -> p h d", h=2)
                vv = V[:, t * 1024 + g * 256:t * 1024 + (g + 1) * 256].rearrange("p (h d) -> p h d", h=2)
                s = sqb[nsq[0] % 2]
                nsq[0] += 1
                k1 = act(lambda e: e.activation(o, bb[:, :, 0:128], ACT.Copy), k, trans_done, *kqr)
                k2 = act(lambda e: e.activation(s.ap[:, 0:256].rearrange("p (h d) -> p h d", h=2), bb[:, :, 0:128], ACT.Square), k, *s.free, k_r2)
                k3 = dve(lambda e: e.tensor_reduce(ssk[:, t * 8 + 2 * g:t * 8 + 2 * g + 2],
                                                   s.ap[:, 0:256].rearrange("p (h d) -> p h d", h=2), AX.X, ALU.add), k2)
                k4 = dve(lambda e: e.tensor_copy(vv, bb[:, :, 128:256]), k)
                s.free = (k3,)
                k_kt[(t, g)] = (k1, k3)
                kvv[(t, g)] = k4
                return (k1, k2, k4)
            k = proj_tok(Wk, kWk, lambda c: latT[:, 2, :], [klq[2]], t, g * 512, 512, 1, consume)
    done_with(ik, k)
    fill(2)
    rk = sm[:, 112:128]
    k_knT = {}
    krb = [R[:, 5 * T:5 * T + 512], R[:, 7 * T:7 * T + 512]]
    knorm, krd = [], []
    for t in range(2):
        k = dve(lambda e: e.tensor_scalar(rk[:, 8 * t:8 * t + 8], ssk[:, 8 * t:8 * t + 8], sm[:, 34 + 4 * t:35 + 4 * t], 1.0 / 192, ALU.add, ALU.mult), k_kt[(t, 3)][1])
    k = dve(lambda e: e.tensor_scalar(rk, rk, 1e-6, None, ALU.add), k)
    k_rk = rsq(rk, k)
    for t in range(2):
        kr3 = krb[t].rearrange("p (h d) -> p h d", h=8)
        pr = pe_rope[:, 64 * t:64 * t + 64].unsqueeze(1).broadcast_to([128, 8, 64])
        rb = rk[:, 8 * t:8 * t + 8].unsqueeze(2)
        krd.append(dve(lambda e: e.tensor_tensor(kr3, pr, rb.broadcast_to([128, 8, 64]), ALU.mult), k_rk, k_r2, kpe[t],
                       *[x for s in sqb for x in s.free]))
    for t in range(2):
        kt3 = ktk[t].rearrange("p (h d) -> p h d", h=8)
        rb = rk[:, 8 * t:8 * t + 8].unsqueeze(2)
        knorm.append(dve(lambda e: e.tensor_tensor(kt3, kt3, rb.broadcast_to([128, 8, 128]), ALU.mult), k_rk, *[k_kt[(t, g)][0] for g in range(4)]))
    for t in range(2):
        b = bank()
        for n in range(4):
            k = pe(lambda e: e.transpose(b.ap[:, n * 128:(n + 1) * 128], krb[t][:, n * 128:(n + 1) * 128], c_("ident")), krd[t], *(b.free if n == 0 else ()))
        kk = act(lambda e: e.activation(krT[:, :, t * 128:(t + 1) * 128], b.ap[:, :].rearrange("p (c t) -> p c t", c=4), ACT.Copy), k)
        b.free = (kk,)
        k_knT[("r", t)] = kk
    for hp in range(4):
        b = bank()
        for n in range(4):
            h, t = 2 * hp + n // 2, n % 2
            k = pe(lambda e, n=n, h=h, t=t, b=b: e.transpose(b.ap[:, n * 128:(n + 1) * 128], ktk[t][:, h * 128:h * 128 + 128], c_("ident")),
                   knorm[t], *(b.free if n == 0 else ()))
        k = act(lambda e, hp=hp, b=b: e.activation(A[:, (8 + 2 * hp) * T:(8 + 2 * hp + 2) * T], b.ap[:, :], ACT.Copy, scale=p_("gk")), k)
        b.free = (k,)
        k_knT[hp] = k
    k_alltr = (pe.sem, pe.n)

    def mla_attention():
        pb = [Buf(S[:, i * 384:(i + 1) * 384]) for i in range(3)]
        pt = [Buf(R[:, 5 * T + i * 384:5 * T + (i + 1) * 384]) for i in range(3)]
        for x_ in pb + pt:
            x_.free = (k_alltr,)
        st = {}
        ku = []
        s8 = lambda h, j: sm[:, 128 + (h % 4) * 8 + j:129 + (h % 4) * 8 + j]
        r0 = [k_b16, klq[2], k_qrT[(0, 0)], k_qrT[(1, 0)], k_knT[("r", 0)], k_knT[("r", 1)]]

        def stage_s(h):
            b = bank()
            p0 = 64 * (h % 2)
            q, k_ = qnT[:, h, :], knT[:, h, :]
            qr = hT[p0:p0 + 64, (h // 2) * T:(h // 2 + 1) * T]
            kr = hT[p0:p0 + 64, (4 + h // 2) * T:(5 + h // 2) * T]
            pe.waits([k_qnT[h // 2], k_knT[h // 2], *r0, *b.free])
            add = lambda f: pe.more(f)
            add(lambda e: mm(e, b.ap[:, 0:128], q[:, 0:128], k_[:, 0:128], True, True, True))
            add(lambda e: mm(e, b.ap[:, 128:384], q[:, 128:256], k_[:, 0:256], False, True, True))
            add(lambda e: mm(e, b.ap[:, 0:128], identb, causb, False, True, True))
            add(lambda e: mm(e, b.ap[:, 256:384], identb, causb, False, True, True))
            add(lambda e: mm(e, b.ap[:, 0:128], qr[:, 0:128], kr[:, 0:128], False, True, True))
            k = pe(lambda e: mm(e, b.ap[:, 128:384], qr[:, 128:256], kr[:, 0:256], False, True, True))
            p = pb[h % 3]
            rng = [(0, 128), (128, 384)]
            ke, k2 = [], []
            for t in range(2):
                a, z = rng[t]
                k1 = dve(lambda e: e.tensor_reduce(s8(h, t), b.ap[:, a:z], AX.X, ALU.max), k, *st.get(("s", h - 4), ()))
                k2.append(dve(lambda e: e.tensor_scalar(s8(h, 2 + t), s8(h, t), scq[:, 8 * t + h:8 * t + h + 1], -1.0, ALU.mult, ALU.mult), k1, k_scq))
            for t in range(2):
                a, z = rng[t]
                k3 = act(lambda e: e.activation(p.ap[:, a:z], b.ap[:, a:z], ACT.Exp, bias=s8(h, 2 + t),
                                                scale=scq[:, 8 * t + h:8 * t + h + 1], accum_out=s8(h, 4 + t)), *k2, *p.free)
            k4 = dve(lambda e: e.reciprocal(s8(h, 6), s8(h, 4)), k3)
            k4 = dve(lambda e: e.reciprocal(s8(h, 7), s8(h, 5)), k3)
            for t in range(2):
                a, z = rng[t]
                k5 = dve(lambda e: e.tensor_scalar(p.ap[:, a:z], p.ap[:, a:z], s8(h, 6 + t), None, ALU.mult), k4)
                ke.append(k5)
            b.free = (k3,)
            st[("s", h)] = (k5,)
            st[h] = (p, ke)

        def stage_t(h):
            p, ke = st[h]
            b = bank()
            pe.waits([*ke, *b.free])
            pe.more(lambda e: e.transpose(b.ap[:, 0:128], p.ap[:, 0:128], c_("ident")))
            pe.more(lambda e: e.transpose(b.ap[:, 128:256], p.ap[:, 128:256], c_("ident")))
            k = pe(lambda e: e.transpose(b.ap[:, 256:384], p.ap[:, 256:384], c_("ident")))
            p.free = (k,)
            q = pt[h % 3]
            k2 = act(lambda e: e.activation(q.ap, b.ap[:, 0:384], ACT.Copy), k, *q.free)
            b.free = (k2,)
            st[h] = (q, k2)

        def stage_o(h):
            q, k2 = st.pop(h)
            b = bank()
            pe.waits([k2, *b.free, kvv[(0, h // 2)], kvv[(1, h // 2)]])
            pe.more(lambda e: mm(e, b.ap[:, 0:256], V[:, h * 128:(h + 1) * 128], q.ap[:, 0:256], True, True, True))
            k = pe(lambda e: mm(e, b.ap[:, 128:256], V[:, 1024 + h * 128:1024 + (h + 1) * 128], q.ap[:, 256:384], False, True, True))
            q.free = (k,)
            k3 = dve(lambda e: e.scalar_tensor_tensor(U[:, h * T:(h + 1) * T], b.ap[:, 0:256], 0.5, G[:, h * T:(h + 1) * T], ALU.mult, ALU.mult),
                     k, kg[h // 2], k_alltr)
            b.free = (k3,)
            ku.append(k3)
        for i in range(8 + 3):
            if i < 8:
                stage_s(i)
            if i in (0, 1, 8):
                fill()
            if i in (3, 5):
                emit_chunk()
            if 0 <= i - 2 < 8:
                stage_t(i - 2)
            if 0 <= i - 3 < 8:
                stage_o(i - 3)
        return ku

    mark("mla")
    ku = mla_attention()
    open_piece()
    k_s = (act.sem, act.n), (dve.sem, dve.n), (pe.sem, pe.n)
    k_ctx = load(sp, "ctx", v3(S, 8), I["ctxT"].rearrange("(c p) t -> p c t", p=128), *k_s)
    k_wm = load(sp, "wm", A[:, 15 * T:16 * T], I["wmask"], *k_s)
    k_rw = load(sp, "rw", rw[:, :].rearrange("p (c e) -> p c e", c=8), I["router_w_2"][0].rearrange("(c p) e -> p c e", p=128))
    wmask = A[:, 15 * T:16 * T]
    gs = sm[:, 192:216]
    modv = mod[:, :].rearrange("p (g c t) -> p g c t", g=6, t=2)

    def gain(j, group, col, name):
        return dve(lambda e: e.scalar_tensor_tensor(gs[:, 8 * j:8 * j + 8], modv[:, group, :, col], 1.0, p_(name, 0, 8),
                                                    ALU.add, ALU.mult), k_pc, k_mod[group // 2])

    def sc_(c):
        return S[:, c * T:(c + 1) * T]

    state = {}

    def ctx_norm():
        fill(max(0, len(fillers) - 8))
        kg_ = [gain(0, 1, 0, "norm1"), gain(1, 1, 1, "norm1")]
        state["gain"] = kg_
        state["khc"], _ = rms_T(sc_, 8, D, [k_ctx] * 8, lambda c: gs[:, 8 + c:9 + c], sc_,
                                scr=v3(V, 8), k_scr=k_s)

    mark("l1out")
    out_proj(hi, uc, split_h(uc, hi, ku), None, hook=ctx_norm)
    if level == 2:
        return finish(nc, locals())
    khc = state["khc"]
    k_old = (pe.sem, pe.n)
    kh, _ = rms_T(xc, 8, D, kx, lambda c: gs[:, c:c + 1], hc, scr=v3(V, 8), k_scr=(k_old, *khc), nfill=12)
    hi = uc
    kh = split_h(hc, hi, kh, (k_old,), lambda c: m_(0, c))
    k_gain = gain(2, 4, 0, "norm2")
    k_mods = (pe.sem, pe.n)
    hi_c = lambda c: BB[:, c * T:(c + 1) * T]
    khc = split_h(sc_, hi_c, khc, (k_mods,), lambda c: m_(0, c, 1))
    w = I["w_in_2"][0]

    mark("l2")
    HU = G[:, 0:6 * 258].rearrange("p (c t) -> p c t", c=6)
    CF = A[:, 12 * T:12 * T + 572].rearrange("p (c t) -> p c t", c=2)
    CT = v3(R, 6)
    cy = v3(R, 2, T, at=6 * T)
    kz1 = pool(lambda e: e.memset(HU[:, :, 0:1], 0.0), k_old)
    kz1 = pool(lambda e: e.memset(HU[:, :, 257:258], 0.0), k_old)
    kz2 = pool(lambda e: e.memset(CF[:, :, 0:15], 0.0), k_old)
    kz2 = pool(lambda e: e.memset(CF[:, :, 271:286], 0.0), k_old)
    k_hu, k_cf = {}, []
    aglu = {}

    def consume_mix(ch, b, k):
        bb = b.ap[:, :].rearrange("p (c t) -> p c t", c=2)
        if ch < 6:
            k2 = act(lambda e: e.activation(HU[:, ch:ch + 2, 1:257], bb, ACT.Copy), k, k_old)
            k_hu[ch] = k_hu[ch + 1] = k2
            return (k2,)
        if ch == 6:
            o = CF[:, :, 15:271]
            k2 = act(lambda e: e.activation(o, bb, ACT.Copy), k, k_old)
            aglu[0] = k2
            return (k2,)
        tg = v3(A, 2, T, at=8 * T)
        k2 = act(lambda e: e.activation(tg, bb, ACT.Tanh, scale=0.5), k, k_old)
        for c in range(2):
            k_cf.append(dve(lambda e, c=c: e.scalar_tensor_tensor(CF[:, c, 15:271], tg[:, c, :], 1.0, CF[:, c, 15:271], ALU.add, ALU.mult), k2, aglu[0]))
        return (k2,)

    ch = 0
    for a, n in ((1536, 512), (2048, 512), (2560, 256)):
        k = sproj_T(take(), hi, hc, kh, lambda j0, b, k, ch=ch: consume_mix(ch + j0, b, k))
        ch += n // 128

    k_ct = []
    for c in range(6):
        kk = dve(lambda e, c=c: e.tensor_scalar(CT[:, c, :], HU[:, c, 0:256], p_("sw", 3 * c), p_("sb", c), ALU.mult, ALU.add), k_hu[c], kz1, k_old)
        for j in (1, 2):
            kk = dve(lambda e, c=c, j=j: e.scalar_tensor_tensor(CT[:, c, :], HU[:, c, j:j + 256], p_("sw", 3 * c + j), CT[:, c, :], ALU.mult, ALU.add), kk)
        k_ct.append(kk)
    kcy = [None, None]
    for j in range(31):
        for c in range(2):
            if j == 0:
                kcy[c] = dve(lambda e, c=c: e.tensor_scalar(cy[:, c, :], CF[:, c, 0:256], p_("cw", c), None, ALU.mult), *k_cf, kz2, k_old)
            else:
                kcy[c] = dve(lambda e, c=c, j=j: e.scalar_tensor_tensor(cy[:, c, :], CF[:, c, j:j + 256], p_("cw", 2 * j + c), cy[:, c, :], ALU.mult, ALU.add), kcy[c])

    for c in range(2):
        kcy[c] = dve(lambda e: e.tensor_scalar(cy[:, c, :], cy[:, c, :], 0.5, p_("cb", c), ALU.mult, ALU.add), kcy[c])

    qkT = v3(A, 12)
    k_q = {}
    for src, off, a, sc in ((0, 0, 0, 0.125), (0, 4, 512, 1.0), (1, 8, 512, 1.0)):
        if src == 0:
            p = take()

        def consume(j0, b, k, off=off, sc=sc):
            k2 = act(lambda e: e.activation(qkT[:, off + j0:off + j0 + 2, :], b.ap[:, :].rearrange("p (c t) -> p c t", c=2), ACT.Copy, scale=sc),
                     k, *k_cf)
            k_q[off + j0] = k_q[off + j0 + 1] = k2
            return (k2,)
        k = sproj_T(p, *((hi_c, sc_, khc) if src else (hi, hc, kh)), consume, off != 4)
    p = take()
    k_v = []
    for t in (2, 3, 0, 1):
        def consume(b, k, t=t):
            k2 = act(lambda e: e.activation(V[:, t * 512:(t + 1) * 512], b.ap[:, :], ACT.Copy), k, k_old)
            k_v.append(k2)
            return (k2,)
        k = sproj_tok(p, *((hi_c, sc_, khc) if t >= 2 else (hi, hc, kh)), t % 2, consume, t == 1)
        if t == 3:
            k_cx = k
    k_proj = k

    rota[0] = 6

    bias = [Buf(BB[:, i * 512:(i + 1) * 512]) for i in range(4)]
    for b_ in bias:
        b_.free = (k_cx,)
    bsem = [sem(f"s_bias{i}") for i in range(4)]
    buse = [0] * 4
    k_bias = {}
    rpb = I["rpb"]

    def load_bias(h):
        b = bias[h % 4]
        for r in range(4):
            src = bass.AP(rpb.tensor, h * 465 + (7 - r) * 31 + 15 - 63, [[1, 64], [31, 4], [1, 64]])
            dst = b.ap[64 * (r % 2):64 * (r % 2) + 64, (r // 2) * 256:(r // 2) * 256 + 256].rearrange("p (a c) -> p a c", a=4)
            sp.dma(lambda e: e.dma_start(dst, src), bsem[h % 4], *b.free)
        buse[h % 4] += 64
        b3 = b.ap.rearrange("p (t k) -> p t k", t=2)
        k_bias[h] = pool(lambda e: e.tensor_tensor(b3, b3, wmask.unsqueeze(1).broadcast_to([128, 2, 256]), ALU.add),
                         (bsem[h % 4], buse[h % 4]), k_wm)

    for h in range(4):
        load_bias(h)

    fwd = v3(CC, 2, 512, at=CONST["fwd"][0])
    inv = v3(CC, 4, 256, at=CONST["inv"][0])
    KA, KB, KC = v3(SPEC, 2, 512), v3(SPEC, 2, 512, at=1024), SPEC[:, 2048:2560]
    kmix = [None] * 8

    def hyena_run():
        Zt = v3(G, 2)
        Y = v3(G, 4, T, at=2 * T)
        tmp = v3(G, 2, T, at=6 * T)
        zT = CT[:, 4:6, :]
        kzt = [k_ct[4], k_ct[5]]
        for n in range(2):
            b = bank()
            for c in range(2):
                for t in range(2):
                    o = b.ap[:, t * 256 + c * 128:t * 256 + c * 128 + 128]
                    k = pe(lambda e: e.transpose(o, zT[:, c, t * 128:(t + 1) * 128], c_("ident")), kzt[c], *b.free)
            k = act(lambda e: e.activation(Zt, b.ap[:, :].rearrange("p (c t) -> p c t", c=2), ACT.Copy), k, *k_ct)
            b.free = (k,)
            yield
            zb = []
            for part in range(2):
                b = bank()
                for f in range(2):
                    for t in range(2):
                        kk = pe(lambda e: mm(e, b.ap[:, f * 256:(f + 1) * 256], fwd[:, t, part * 256 + f * 128:part * 256 + f * 128 + 128],
                                             Zt[:, t, :], t == 0, t == 1), k, *b.free)
                zb.append((b, kk))
            (br, kr), (bi, ki) = zb
            sl = slice(n * 256, n * 256 + 256)
            c2 = lambda a: a.rearrange("p (c t) -> p c t", c=2)
            k1 = dve(lambda e: e.tensor_tensor(Y[:, 0:2, :], c2(br.ap[:, :]), KA[:, :, sl], ALU.mult), kr, *k_ct)
            k2 = dve(lambda e: e.tensor_tensor(tmp, c2(bi.ap[:, :]), KB[:, :, sl], ALU.mult), ki)
            k3 = pool(lambda e: e.tensor_tensor(Y[:, 0:2, :], Y[:, 0:2, :], tmp, ALU.subtract), k1, k2)
            k4 = dve(lambda e: e.tensor_tensor(Y[:, 2:4, :], c2(br.ap[:, :]), KB[:, :, sl], ALU.mult), kr)
            k5 = dve(lambda e: e.tensor_tensor(tmp[:, 0, :], bi.ap[:, 0:256], KC[:, sl], ALU.mult), k3)
            k6 = dve(lambda e: e.tensor_tensor(tmp[:, 1, :], bi.ap[:, 256:512], KA[:, 1, sl], ALU.mult), k3)
            br.free, bi.free = (k4,), (k6,)
            k7 = pool(lambda e: e.tensor_tensor(Y[:, 2:4, :], Y[:, 2:4, :], tmp, ALU.add), k4, k5, k6)
            yield
            yield
            b = bank()
            for c in range(2):
                for f in range(4):
                    k = pe(lambda e: mm(e, b.ap[:, c * 256:(c + 1) * 256], Y[:, f, c * 128:(c + 1) * 128], inv[:, f, :], f == 0, f == 3), k3, k7, *b.free)
            kn = []
            for c in range(2):
                o = zT[:, c, :] if n == 0 else U[:, (4 + c) * T:(5 + c) * T]
                k8 = dve(lambda e: e.scalar_tensor_tensor(zT[:, c, :], zT[:, c, :], p_("bd", 2 * n + c), b.ap[:, c * 256:(c + 1) * 256], ALU.mult, ALU.add), k)
                k9 = dve(lambda e: e.tensor_tensor(o, zT[:, c, :], CT[:, 2 * n + c, :], ALU.mult), k8, k_ct[2 * n + c], k_old)
                kn.append(k9)
            b.free = (k8,)
            kzt = kn
            yield
        kmix[4], kmix[5] = kn

    def cf_run():
        t8 = v3(R, 2, T, at=8 * T)
        t9 = v3(A, 2, T, at=12 * T)
        ky = list(kcy)
        b = bank()
        for c in range(2):
            k = pe(lambda e: mm(e, b.ap[:, 0:T], c_("nones"), cy[:, c, :], c == 0, c == 1), ky[c], *b.free)
        for c in range(2):
            ky[c] = dve(lambda e: e.scalar_tensor_tensor(cy[:, c, :], b.ap[:, 0:T], 1.0 / 256, cy[:, c, :], ALU.mult, ALU.add), k)
        b.free = (ky[1],)
        yield
        k = act(lambda e: e.activation(t8, cy, ACT.Square), *ky)
        yield
        b = bank()
        for c in range(2):
            kk = pe(lambda e: mm(e, b.ap[:, 0:T], c_("nones"), t8[:, c, :], c == 0, c == 1), k, *b.free)
        k = dve(lambda e: e.tensor_scalar(sm_r, b.ap[:, 0:T], -1.0 / 256, 1e-6, ALU.mult, ALU.add), kk, *smr_free[0])
        b.free = (k,)
        k = rsq(sm_r, k)
        for c in range(2):
            k1 = dve(lambda e: e.tensor_tensor(cy[:, c, :], cy[:, c, :], sm_r, ALU.mult), k)
            ky[c] = dve(lambda e: e.tensor_scalar(cy[:, c, :], cy[:, c, :], p_("lng", c), p_("lnb", c), ALU.mult, ALU.add), k1)
        smr_free[0] = (k1,)
        yield
        k = act(lambda e: e.activation(t9, cy, ACT.Tanh, scale=0.5), *ky)
        yield
        for c in range(2):
            k1 = dve(lambda e: e.scalar_tensor_tensor(cy[:, c, :], t9[:, c, :], 1.0, cy[:, c, :], ALU.add, ALU.mult), k)
            kmix[6 + c] = dve(lambda e: e.tensor_scalar(U[:, (6 + c) * T:(7 + c) * T], cy[:, c, :], 0.5, None, ALU.mult), k1, k_old)

    def na_attention(steps):
        pb = [Buf(hT[:, i * 512:(i + 1) * 512]) for i in range(4)]
        pt = [Buf(S[:, i * 512:(i + 1) * 512]) for i in range(4)]
        for x_ in pb + pt:
            x_.free = (k_proj,)
        st = {}
        s4 = lambda u, j: sm[:, 128 + (u % 4) * 4 + j:129 + (u % 4) * 4 + j]

        def stage_s(u0):
            hp, t = u0 // 4, (u0 // 2) % 2
            us = {u0: 2 * hp, u0 + 1: 2 * hp + 1}
            bs = {}
            for u, h in us.items():
                bs[u] = bank()
                pe.waits([k_q[hp], k_q[4 + hp], k_q[8 + hp], k_bias[h], *bs[u].free])
            for off, j in ((0, 4), (256, 8)):
                for u, h in us.items():
                    p0 = 64 * (h % 2)
                    pe.more(lambda e: mm(e, bs[u].ap[:, off:off + 256], qkT[p0:p0 + 64, hp, t * 128:(t + 1) * 128],
                                         qkT[p0:p0 + 64, j + hp, :], off == 0, True, True))
            for u, h in us.items():
                k = pe(lambda e: mm(e, bs[u].ap[:, 0:256], c_("flip"), bias[h % 4].ap[:, t * 256:(t + 1) * 256], False, True, True))
                if t == 1:
                    bias[h % 4].free = (k,)
            if t == 1:
                for h in (2 * hp + 4, 2 * hp + 5):
                    if h < 8:
                        load_bias(h)
            k1, k3 = {}, {}
            for u in us:
                k = dve(lambda e: e.tensor_reduce(s4(u, 0), bs[u].ap[:, :], AX.X, ALU.max), k, *st.get(("s", u - 4), ()))
                k1[u] = dve(lambda e: e.tensor_scalar(s4(u, 1), s4(u, 0), -1.0, None, ALU.mult), k)
            for u in us:
                p = pb[u % 4]
                k3[u] = act(lambda e: e.activation(p.ap, bs[u].ap[:, :], ACT.Exp, bias=s4(u, 1), accum_out=s4(u, 2)), k1[u], *p.free)
                bs[u].free = (k3[u],)
            for u in us:
                p = pb[u % 4]
                k4 = dve(lambda e: e.reciprocal(s4(u, 3), s4(u, 2)), k3[u])
                k5 = dve(lambda e: e.tensor_scalar(p.ap, p.ap, s4(u, 3), None, ALU.mult), k4)
                st[("s", u)] = (k5,)
                st[u] = (p, k5)

        def stage_t(u):
            p, kp = st[u]
            b = bank()
            for j in range(4):
                k = pe(lambda e: e.transpose(b.ap[:, j * 128:(j + 1) * 128], p.ap[:, j * 128:(j + 1) * 128], c_("ident")), kp, *b.free)
            p.free = (k,)
            q = pt[u % 4]
            k2 = act(lambda e: e.activation(q.ap, b.ap[:, :], ACT.Copy), k, *q.free)
            b.free = (k2,)
            st[u] = (q, k2)


        def stage_o(u0):
            hp, t = u0 // 4, (u0 // 2) % 2
            b = banks[6 + hp % 2]
            q = {u: st.pop(u) for u in (u0, u0 + 1)}
            pe.waits([*k_v, *b.free, *[x_[1] for x_ in q.values()]])
            for j in range(4):
                for u in q:
                    p0 = 64 * (u % 2)
                    h = 2 * hp + u % 2
                    k = pe(lambda e: mm(e, b.ap[p0:p0 + 64, t * 128:(t + 1) * 128], V[:, j * 512 + h * 64:j * 512 + h * 64 + 64],
                                        q[u][0].ap[:, j * 128:(j + 1) * 128], j == 0, j == 3))
            for u in q:
                q[u][0].free = (k,)
            if t == 1:
                k3 = dve(lambda e: e.tensor_copy(U[:, hp * T:(hp + 1) * T], b.ap[:, 0:256]), k, k_old)
                b.free = (k3,)
                kmix[hp] = k3

        def step():
            if steps:
                g = steps.pop(0)
                try:
                    next(g)
                    steps.append(g)
                except StopIteration:
                    pass

        for i in range(8 + 2):
            if i == 7:
                while steps:
                    step()
                g_free.extend((q.sem, q.n) for q in (dve, pool, pe))
                ku.update(zip(range(4, 8), split_h(lambda c: uc(c + 4), lambda c: hi_u(c + 4), kmix[4:], g_free)))
            step()
            if i < 8:
                stage_s(2 * i)
            if i == 9:
                out_pre(take_now(), 1, (4, 5, 6, 7), hi_u, uc, ku)
            if 0 <= i - 2 < 8:
                stage_o(2 * i - 4)
            if i == 8:
                out_pre(take_now(), 0, (4, 5, 6, 7), hi_u, uc, ku)
            step()
            if 0 <= i - 1 < 8:
                stage_t(2 * i - 2)
                stage_t(2 * i - 1)

    hi_u = lambda c: G[:, c * T:(c + 1) * T]
    ku, g_free = {}, []
    steps = [hyena_run(), cf_run()]
    mark("na")
    na_attention(steps)
    if level == 25:
        s5 = sem("s_dbg")
        sp.dma(lambda e: e.dma_start(O["dbg"], U[:, :]), s5, *kmix)
        sp.items.append(("w", s5, 16))
        return finish(nc, locals())
    mark("l2out")
    done = tuple((q.sem, q.n) for q in (pe, act, dve, pool))
    ku.update(zip(range(4), split_h(uc, hi_u, kmix[:4], g_free)))
    while todo:
        open_piece()
    for i in range(NSLOT, NSLOT + 3):
        done_with(i, *done)
    out_proj(hi_u, uc, ku, lambda c: m_(2, c))
    mark("end")
    if level == 3:
        return finish(nc, locals())

    mark("route")
    k_old = (pe.sem, pe.n)
    kh, _ = rms_T(xc, 8, D, kx, lambda c: gs[:, 16 + c:17 + c], hc, lambda c: m_(3, c))
    b = bank()
    for c in range(8):
        for t in range(2):
            k = pe(lambda e: mm(e, b.ap[:, t * 16:(t + 1) * 16], hc(c)[:, t * 128:(t + 1) * 128], rw[:, c * 16:(c + 1) * 16],
                                c == 0 and t == 0, c == 7, True), kh[c], k_rw, *b.free)
    aff = sm[:, 128:160]
    a3 = aff.rearrange("p (t e) -> p t e", t=2)
    mx = sm[:, 160:164]
    b3 = b.ap[:, 0:32].rearrange("p (t e) -> p t e", t=2)
    k = dve(lambda e: e.tensor_reduce(mx[:, 0:2], b3, AX.X, ALU.max), k)
    k = dve(lambda e: e.tensor_tensor(a3, b3, mx[:, 0:2].unsqueeze(2).broadcast_to([128, 2, 16]), ALU.subtract), k)
    b.free = (k,)
    k = act(lambda e: e.activation(aff, aff, ACT.Exp), k)
    k = dve(lambda e: e.tensor_reduce(mx[:, 2:4], a3, AX.X, ALU.add), k)
    k = dve(lambda e: e.reciprocal(mx[:, 2:4], mx[:, 2:4]), k)
    k_aff = dve(lambda e: e.tensor_tensor(a3, a3, mx[:, 2:4].unsqueeze(2).broadcast_to([128, 2, 16]), ALU.mult), k)
    b = bank()
    for t in range(2):
        k = pe(lambda e: e.transpose(b.ap[0:16, t * 128:(t + 1) * 128], a3[:, t, :], c_("ident")), k_aff, *b.free)
    w0 = U[0:16, 1024:1280]
    sel = U[0:16, 1280:1536]
    slot = U[0:16, 1536:1792]
    m8 = U[0:16, 1792:1824]
    k = dve(lambda e: e.tensor_copy(w0, b.ap[0:16, 0:256]), k, k_old)
    b.free = (k,)
    k_ht = []
    for t in range(2):
        for c0 in (0, 4):
            b = bank()
            for c in range(c0, c0 + 4):
                kk = pe(lambda e: e.transpose(b.ap[:, (c - c0) * 128:(c - c0 + 1) * 128], hc(c)[:, t * 128:(t + 1) * 128], c_("ident")), kh[c], *b.free)
            kk = act(lambda e: e.activation(V[:, t * 1024 + c0 * 128:t * 1024 + c0 * 128 + 512], b.ap[:, :], ACT.Copy), kk, k_old)
            b.free = (kk,)
            k_ht.append(kk)
    for r in range(4):
        k = dve(lambda e: e.max(m8[:, 8 * r:8 * r + 8], w0), k)
        k = dve(lambda e: e.match_replace(w0, m8[:, 8 * r:8 * r + 8], w0, -1.0), k)
    k = dve(lambda e: e.tensor_scalar(sel, w0, -1.0, None, ALU.is_equal), k)
    k = dve(lambda e: e.tensor_tensor_scan(slot, sel, sel, 0.0, ALU.add, ALU.bypass), k)
    k = dve(lambda e: e.tensor_tensor(slot, slot, sel, ALU.mult), k)
    b = bank()
    for t in range(2):
        k1 = pe(lambda e: e.transpose(b.ap[:, t * 16:(t + 1) * 16], slot[:, t * 128:(t + 1) * 128], c_("ident")[0:16, 0:16]), k, *b.free)
    GM = v3(S, 2, 512)
    gx = [Buf(S[:, 1024 + i * T:1024 + (i + 1) * T]) for i in range(2)]
    k_gm = []
    io = c_("iota").unsqueeze(1).broadcast_to([128, 16, 32])
    ko_ = (act.sem, act.n)
    for e0, e1_ in ((0, 4), (4, 16)):
        for t in range(2):
            g3 = GM[:, t, 32 * e0:32 * e1_].rearrange("p (e j) -> p e j", j=32)
            k2 = dve(lambda e: e.tensor_tensor(g3, b.ap[:, t * 16 + e0:t * 16 + e1_].unsqueeze(2).broadcast_to([128, e1_ - e0, 32]),
                                               io[:, e0:e1_, :], ALU.is_equal), k1, k_old, kh[0])
            k_gm.append(k2)
    b.free = (k2,)
    xe = [(hT if c < 4 else G)[:, c % 4 * 512:c % 4 * 512 + 512] for c in range(8)]
    k_tr = (pe.sem, pe.n)
    k_xe = {}

    def gather(g, bs):
        ks = []
        for c in range(8):
            b = bs[c // 4]
            for t in range(2):
                k = pe(lambda e: mm(e, b.ap[:, c % 4 * 128:c % 4 * 128 + 128], V[:, t * 1024 + c * 128:t * 1024 + (c + 1) * 128],
                                    GM[:, t, g * 128:(g + 1) * 128], t == 0, t == 1), k_gm[t + 2 * (g > 0)], *k_ht, *b.free)
            if c % 4 == 3:
                o = (hT, G)[c // 4][:, 0:2048].rearrange("p (c n) -> p c n", c=4)[:, :, g * 128:(g + 1) * 128]
                i_ = b.ap[:, :].rearrange("p (c n) -> p c n", c=4)
                if c == 3:
                    k = act(lambda e: e.activation(o, i_, ACT.Copy), k, k_tr)
                else:
                    k = dve(lambda e: e.tensor_copy(o, i_), k, k_tr)
                b.free = (k,)
                ks.append(k)
        k_xe[g] = tuple(ks)
        return (pe.sem, pe.n)

    gather(0, banks[6:8])
    mark("moe")
    sg = [Buf(R[:, (8 + i) * T:(9 + i) * T]) for i in range(2)]
    k_old = (pe.sem, pe.n)
    hs = [Buf(S[:, 1536:2048]), Buf(V[:, 0:512])]
    ht = [Buf(U[:, 1024:1536]), Buf(V[:, 512:1024])]
    ysb = Buf(U[:, 0:1024])
    for x_ in hs + ht + sg + gx + [ysb]:
        x_.free = (k_old,)
    W1, W3, W2 = I["expert_w1_2"][0], I["expert_w3_2"][0], I["expert_w2_2"][0]
    rowv = lambda w_: w_.rearrange("(c p) n -> p c n", p=128)
    yb, gb = banks[4:6], banks[6:8]
    ksc = []

    def scatter(ex, ky):
        s_ = sg[ex % 2]
        for c0 in range(0, 8, 2):
            b = gb[(c0 // 2) % 2]
            for c in (c0, c0 + 1):
                o = b.ap[:, (c % 2) * T:(c % 2 + 1) * T]
                k = pe(lambda e: mm(e, o, ysb.ap[:, c * 128:(c + 1) * 128], s_.ap, True), *ky, *b.free)
            for c in (c0, c0 + 1):
                o = b.ap[:, (c % 2) * T:(c % 2 + 1) * T]
                kx[c] = dve(lambda e: e.scalar_tensor_tensor(xc(c), o, m_(5, c), xc(c), ALU.mult, ALU.add), k, kx[c])
            b.free = (kx[c],)
        ysb.free = (k,)
        s_.free = (k,)

    prev = None
    for ex in range(16):
        a_, u_ = banks[2 * (ex % 2)], banks[2 * (ex % 2) + 1]
        for w_, b in ((W1, a_), (W3, u_)):
            for i4 in range(4):
                W, kW, i = piece(rowv(w_[ex])[:, 2 * i4:2 * i4 + 2, :], 2, 2048)
                pe.waits([kW, k_xe[ex // 4][i4 // 2], *b.free])
                for c in range(2):
                    for q in range(4):
                        fn = lambda e: mm(e, b.ap[32 * q:32 * q + 32, :], xe[2 * i4 + c][:, ex * 32:ex * 32 + 32],
                                          W[:, c, q * 512:(q + 1) * 512], i4 == 0 and c == 0, i4 == 3 and c == 1, True)
                        if c == 1 and q == 3:
                            k = pe(fn)
                        else:
                            pe.more(fn)
                done_with(i, k)
            if w_ is W1:
                ka = k
        h_ = hs[ex % 2]
        k1 = act(lambda e: e.activation(h_.ap, a_.ap[:, :], ACT.Tanh, scale=0.5), ka, *h_.free)
        k2 = dve(lambda e: e.scalar_tensor_tensor(h_.ap, h_.ap, 1.0, a_.ap[:, :], ALU.add, ALU.mult), k1)
        k3 = dve(lambda e: e.scalar_tensor_tensor(h_.ap, h_.ap, 0.5, u_.ap[:, :], ALU.mult, ALU.mult), k2, k)
        a_.free, u_.free = (k2,), (k3,)
        if prev is not None:
            scatter(*prev)
        if ex == 0:
            for g in (1, 2, 3):
                k_g = gather(g, gb)
            for x_ in (hs[1], ht[1]):
                x_.free = (k_g,)
        b = gb[0]
        for j in range(4):
            k = pe(lambda e: e.transpose(b.ap[:, j * 128:(j + 1) * 128], h_.ap[:, j * 128:(j + 1) * 128], c_("ident")), k3, *b.free)
        h_.free = (k,)
        t_ = ht[ex % 2]
        k4 = act(lambda e: e.activation(t_.ap, b.ap[:, :], ACT.Copy), k, *t_.free)
        b.free = (k4,)
        b = gb[1]
        s_ = sg[ex % 2]
        g_ = gx[ex % 2]
        for t in range(2):
            src = GM[:, t, ex * 32:(ex + 1) * 32].unsqueeze(1).broadcast_to([128, 4, 32])
            k5 = pool(lambda e: e.tensor_scalar(g_.ap[:, t * 128:(t + 1) * 128].rearrange("p (a j) -> p a j", a=4), src,
                                                a3[:, t, ex:ex + 1], None, ALU.mult), k_gm[t + 2 * (ex > 3)], k_aff, *g_.free)
            k = pe(lambda e: e.transpose(b.ap[:, t * 128:(t + 1) * 128], g_.ap[:, t * 128:(t + 1) * 128], c_("ident")), k5, *b.free)
        g_.free = (k,)
        k5 = act(lambda e: e.activation(s_.ap, b.ap[:, 0:256], ACT.Copy), k, *s_.free)
        b.free = (k5,)
        for fq in range(4):
            W, kW, i = piece(rowv(W2[ex])[:, 4 * fq:4 * fq + 4, :], 4, 1024)
            pe.waits([kW, k4, *yb[0].free, *yb[1].free])
            for half in range(2):
                for j in range(4):
                    fn = lambda e: mm(e, yb[half].ap[32 * j:32 * j + 32, :], t_.ap[:, j * 128 + fq * 32:j * 128 + fq * 32 + 32],
                                      W[:, j, half * 512:(half + 1) * 512], fq == 0, fq == 3, True)
                    if half == 1 and j == 3:
                        k = pe(fn)
                    else:
                        pe.more(fn)
            done_with(i, k)
        t_.free = (k,)
        ky = []
        for half in range(2):
            o, i_ = ysb.ap[:, half * 512:(half + 1) * 512], yb[half].ap[:, :]
            if half:
                kk = dve(lambda e: e.tensor_copy(o, i_), k, *ysb.free)
            else:
                kk = act(lambda e: e.activation(o, i_, ACT.Copy), k, *ysb.free)
            yb[half].free = (kk,)
            ky.append(kk)
        prev = (ex, (*ky, k5))
    scatter(*prev)
    mark("tail")
    mark("end")
    if level == 4:
        return finish(nc, locals())
    oT = lambda c: hT[:, c * T:(c + 1) * T]
    ko, _ = rms_T(xc, 8, D, kx, lambda c: p_("final", c), oT)
    xout = []
    for half in range(2):
        s = sem(f"s_out{half}")
        sp.dma(lambda e: e.dma_start(O["out"].rearrange("(c p) t -> p c t", p=128)[:, 4 * half:4 * half + 4, :], v3(hT, 4, T, at=4 * half * T)), s,
               *ko[4 * half:4 * half + 4])
        xout.append(s)
    for s in xout:
        sp.items.append(("w", s, 16))
    finish(nc, locals())


def finish(nc, L):
    I, O = L["I"], L["O"]
    sp, sem = L["sp"], L["sem"]
    if "xout" not in L:
        s = sem("s_out")
        xT = L["xT"]
        sp.dma(lambda e: e.dma_start(O["out"].rearrange("(c p) t -> p c t", p=128), xT[:, :].rearrange("p (c t) -> p c t", c=8)), s, *L["kx"])
        sp.items.append(("w", s, 16))
        if L["level"] == 0:
            s2 = sem("s_out2")
            sp.dma(lambda e: e.dma_start(O["dbg"], L["SPEC"][:, :]), s2, *L["k_spec"])
            sp.items.append(("w", s2, 16))
    block = L["ctx"].enter_context(nc.Block())

    def emit(q, eng):
        for it in q.items:
            if it[0] == "w":
                eng.wait_ge(it[1], it[2])
            elif it[0] == "m":
                it[1](eng)
            elif it[0] == "t":
                eng.preload_act_table_set(it[1])
            else:
                it[1](eng).then_inc(it[2], it[3])

    @block.sync
    def _(eng):
        emit(L["sp"], eng)

    @block.gpsimd
    def _(eng):
        emit(L["pool"], eng)

    @block.scalar
    def _(eng):
        emit(L["act"], eng)

    @block.vector
    def _(eng):
        emit(L["dve"], eng)

    @block.tensor
    def _(eng):
        emit(L["pe"], eng)


def _constants():
    f = np.float64
    p = np.arange(128)
    c = {}
    c["ident"] = np.eye(128)
    c["ntri"] = -(p[:, None] >= p[None, :]).astype(f)
    c["nones"] = -np.ones((128, 128))
    c["m01"] = (p[:, None] < p[None, :]).astype(f)
    cap = np.where(p[:, None] < p[None, :], 0.0, NEG)
    c["cap"] = np.concatenate([cap, np.zeros((128, 128)), cap], 1)
    c["caus"] = np.where(p[None, :] <= p[:, None], 0.0, NEG)
    c["iota"] = np.tile(np.arange(1, 33), (128, 1))
    half = 32
    inv = (np.float32(10000.0) ** (-np.arange(half, dtype=np.float32) / np.float32(half))).astype(np.float32)
    ang = (np.arange(T, dtype=np.float32)[:, None] * inv[None, :]).astype(np.float32).astype(f)
    cos = np.concatenate([np.cos(ang), np.cos(ang)], 1)
    sin = np.concatenate([-np.sin(ang), np.sin(ang)], 1)
    c["cosd"] = np.concatenate([cos[:128], cos[128:]], 1)
    c["sind"] = np.concatenate([sin[:128], sin[128:]], 1)
    s = np.arange(T)
    k = np.arange(T)
    th = 2 * math.pi * ((s[:, None] * k[None, :]) % 512) / 512
    Fre, Fim = np.cos(th), -np.sin(th)
    alt = np.where(s % 2 == 0, 1.0, -1.0)
    Fimn = Fim.copy()
    Fimn[:, 0] = alt
    fw = np.concatenate([Fre, Fimn], 1)
    c["fwd"] = np.concatenate([fw[:128], fw[128:]], 1)
    ny = Fre[:, :128].copy()
    ny[:, 0] = alt
    c["nyq"] = np.concatenate([ny[:128], ny[128:]], 1)
    wt = np.where(k == 0, 1.0, 2.0)[:, None] / 512
    Gre = wt * np.cos(th.T)
    Gim = -(2.0 / 512) * np.sin(th.T)
    Gim[0] = alt / 512
    g = np.concatenate([Gre, Gim], 0)
    c["inv"] = np.concatenate([g[i * 128:(i + 1) * 128] for i in range(4)], 1)
    c["flip"] = (p[:, None] // 64 * 64 + 63 - p[:, None] % 64 == p[None, :]).astype(f)
    out = np.zeros((128, NCONST), np.float32)
    for name, (at, n) in CONST.items():
        out[:, at:at + n] = c[name].astype(np.float32)
    t = np.arange(T, dtype=np.float32)[:, None] / np.float32(T - 1)
    fb = np.linspace(1e-4, 15, 16, dtype=np.float32)[None, :]
    angf = (fb * np.float32(TWO_PI) * np.arange(T, dtype=np.float32)[:, None] / np.float32(T)).astype(f)
    z = np.concatenate([t.astype(f), np.cos(angf), -np.sin(angf)], 1).T.astype(np.float32)
    rate = np.abs(np.linspace(math.log(1e-2) / 1.5, math.log(1e-2) / 0.3, 256, dtype=np.float32)).astype(f)
    dec = np.exp(-t.astype(f) * rate[None, :])
    decb = dec.copy()
    decb[0] = 0
    d = np.concatenate([dec[:128], decb[:128], dec[128:], decb[128:]], 1).astype(np.float32)
    col = np.arange(T) % 64
    c0 = np.clip(col - 8, 0, 48)
    ok = (col[None, :] >= c0[:, None]) & (col[None, :] < c0[:, None] + 16)
    wm = np.where(ok, 0.0, NEG).astype(np.float32)[:128]
    wm = np.ascontiguousarray(wm.reshape(2, 64, T)[:, ::-1].reshape(128, T))
    return out, np.ascontiguousarray(z), d, wm


def _cols(inp):
    out = np.zeros((128, NCOL), np.float32)

    def put(name, a):
        at, n = COLS[name]
        out[:, at:at + n] = a

    ch = lambda v: np.asarray(v).reshape(-1, 128).T
    put("l0_norm", ch(inp["l0_norm"]))
    put("l1_norm", ch(inp["l1_norm"]))
    put("q_a", ch(inp["l1_q_a_norm"]))
    put("kv_a", ch(inp["l1_kv_a_norm"]))
    put("gq", np.asarray(inp["l1_q_head_norm"])[:128, None])
    put("gk", np.asarray(inp["l1_k_head_norm"])[:128, None])
    put("b_mod", ch(inp["b_mod_2"][0]))
    put("norm1", ch(inp["norm1_g_2"][0]))
    put("norm2", ch(inp["norm2_g_2"][0]))
    put("final", ch(inp["final_norm_g_2"]))
    put("c", np.stack([ch(inp["c_2"][0]), ch(inp["c_ctx_2"])], 2).reshape(128, 16))
    put("sw", np.asarray(inp["hy_short_w_2"][0]).reshape(3, 6, 128).transpose(2, 1, 0).reshape(128, 18))
    put("sb", ch(inp["hy_short_b_2"][0]))
    put("bd", np.asarray(inp["hy_bias_d_2"][0]).reshape(2, 2, 128).transpose(2, 0, 1).reshape(128, 4))
    put("cw", np.asarray(inp["cf_dw_w_2"][0]).reshape(31, 2, 128).transpose(2, 0, 1).reshape(128, 62))
    put("cb", ch(inp["cf_dw_b_2"][0]))
    put("lng", ch(inp["cf_ln_g_2"][0]))
    put("lnb", ch(inp["cf_ln_b_2"][0]))
    return out


def kernel(**inputs):
    import concourse.bacc as _bacc
    from concourse.bass_utils import run_bass_kernel_spmd as _run

    inp = {k: np.asarray(v) for k, v in inputs.items()}
    consts, zfeat, decay, wmask = _constants()
    arr = {
        "xT": np.ascontiguousarray(inp["x"][0].T),
        "ctxT": np.ascontiguousarray(inp["ctx_2"][0].T),
        "cols": _cols(inp),
        "consts": consts, "zfeat": zfeat, "decay": decay, "wmask": wmask,
        "rowg": np.concatenate([inp["l1_q_head_norm"][128:], inp["l1_k_head_norm"][128:]])[None, :],
        "filtp": np.stack([inp["hy_filt_b1_2"][0], inp["hy_filt_freq_2"][0], inp["hy_filt_b2_2"][0]], 1),
        "rpb": np.ascontiguousarray(inp["na_rpb_2"][0].reshape(8, 15 * 31)),
    }
    for n in ["l0_w_in", "l0_w_out", "l1_w_in", "l1_w_uq", "l1_w_ukv", "l1_w_out", "w_mod_2", "w_in_2",
              "hy_filt_w1_2", "hy_filt_w2_2", "hy_filt_w3_2", "w_out_2", "router_w_2",
              "expert_w1_2", "expert_w3_2", "expert_w2_2"]:
        arr[n] = np.ascontiguousarray(inp[n])
    nc = _bacc.Bacc("TRN2", target_bir_lowering=False, num_devices=1)
    ins = {n: nc.dram_tensor(f"in_{n}", a.shape, F32, kind="ExternalInput").ap() for n, a in arr.items()}
    outs = {"out": nc.dram_tensor("out_0", (D, T), F32, kind="ExternalOutput").ap()}
    if LEVEL == 25:
        outs["dbg"] = nc.dram_tensor("dbg_0", (128, 8 * T), F32, kind="ExternalOutput").ap()
    build_program(nc, ins, outs, LEVEL)
    r = _run(nc, [{f"in_{n}": a for n, a in arr.items()}], core_ids=[0])
    got = np.asarray(r.results[0]["out_0"])
    return np.ascontiguousarray(got.T)[None]


LEVEL = 99
MARKS = []
CNT = [0, 0]
```
